# Optimizing a Trainium2 kernel written in Bass

```python
import math
import jax
import jax.numpy as jnp
from jax import lax
import numpy as np
import jax, jax.numpy as jnp

D_MODEL = 2048
BATCH = 1
SEQ = 256
DEPTH = 1

MLA_HEADS = 8
QK_NOPE = 128
QK_ROPE = 64
V_HEAD = 128
Q_LORA = 512
KV_LORA = 512
ROPE_THETA = 10000.0
Q_BLOCK = 128
GDN_HEADS = 8
GDN_DK = 128
GDN_DV = 128
CONV_WIDTH = 4
CHUNK = 64
GDN_QK = GDN_HEADS * GDN_DK
GDN_V = GDN_HEADS * GDN_DV
CONV_CH = 2 * GDN_QK + GDN_V
D_FF = ((8 * D_MODEL // 3 + 255) // 256) * 256
EPS = 1e-6
IN_SIZES = (Q_LORA, KV_LORA, QK_ROPE, GDN_QK, GDN_QK, GDN_V, GDN_V, GDN_HEADS, GDN_HEADS, 2 * D_MODEL)
IN_WIDTH = Q_LORA + KV_LORA + QK_ROPE + 2 * GDN_QK + 2 * GDN_V + 2 * GDN_HEADS + 2 * D_MODEL


def _rmsnorm(x, w):
    xf = x.astype(jnp.float32)
    y = xf * lax.rsqrt(jnp.mean(xf * xf, axis=-1, keepdims=True) + EPS)
    return (y * w.astype(jnp.float32)).astype(x.dtype)

def _split_cols(p):
    outs, off = [], 0
    for n in IN_SIZES:
        outs.append(p[..., off:off + n])
        off += n
    return outs

def _rope_tables(positions):
    inv_freq = 1.0 / (ROPE_THETA ** (jnp.arange(0, QK_ROPE, 2, dtype=jnp.float32) / QK_ROPE))
    ang = positions.astype(jnp.float32)[..., None] * inv_freq
    return jnp.cos(ang), jnp.sin(ang)

def _rope(x, cos, sin):
    xf = x.astype(jnp.float32)
    x1, x2 = jnp.split(xf, 2, axis=-1)
    return jnp.concatenate([x1 * cos - x2 * sin, x2 * cos + x1 * sin], axis=-1).astype(x.dtype)

def _mla_branch(c_q, c_kv, k_pe, q_norm, kv_norm, w_uq, w_ukv, cos, sin):
    B, T, _ = c_q.shape
    q = (_rmsnorm(c_q, q_norm) @ w_uq).reshape(B, T, MLA_HEADS, QK_NOPE + QK_ROPE)
    q_nope, q_pe = q[..., :QK_NOPE], q[..., QK_NOPE:]
    q_pe = _rope(q_pe, cos[:, :, None, :], sin[:, :, None, :])
    kv = (_rmsnorm(c_kv, kv_norm) @ w_ukv).reshape(B, T, MLA_HEADS, QK_NOPE + V_HEAD)
    k_nope, v = kv[..., :QK_NOPE], kv[..., QK_NOPE:]
    k_pe = _rope(k_pe, cos, sin)
    scale = (QK_NOPE + QK_ROPE) ** -0.5
    outs = []
    for i in range(T // Q_BLOCK):
        q0, k_end = i * Q_BLOCK, (i + 1) * Q_BLOCK
        s = (jnp.einsum('bqhd,bkhd->bhqk', q_nope[:, q0:k_end], k_nope[:, :k_end])
             + jnp.einsum('bqhr,bkr->bhqk', q_pe[:, q0:k_end], k_pe[:, :k_end]))
        s = s.astype(jnp.float32) * scale
        mask = jnp.arange(k_end)[None, :] <= (q0 + jnp.arange(Q_BLOCK))[:, None]
        p = jax.nn.softmax(jnp.where(mask, s, -jnp.inf), axis=-1).astype(v.dtype)
        outs.append(jnp.einsum('bhqk,bkhd->bqhd', p, v[:, :k_end]))
    return jnp.concatenate(outs, axis=1).reshape(B, T, MLA_HEADS * V_HEAD)

def _causal_conv_silu(u, w):
    kern = w[:, None, :].astype(u.dtype)
    y = lax.conv_general_dilated(u, kern, window_strides=(1,), padding=[(CONV_WIDTH - 1, 0)],
                                 dimension_numbers=('NWC', 'WIO', 'NWC'),
                                 feature_group_count=u.shape[-1])
    return jax.nn.silu(y)

def _l2norm(x):
    xf = x.astype(jnp.float32)
    return xf * lax.rsqrt(jnp.sum(xf * xf, axis=-1, keepdims=True) + EPS)

def _gated_delta_chunked(q, k, v, beta, g):
    B, T, H, DK = q.shape
    DV = v.shape[-1]
    N = T // CHUNK
    to_chunks = lambda a: a.reshape(B, N, CHUNK, H, -1).transpose(0, 3, 1, 2, 4)
    q, k, v = to_chunks(q), to_chunks(k), to_chunks(v)
    beta = beta.reshape(B, N, CHUNK, H).transpose(0, 3, 1, 2)
    g = g.reshape(B, N, CHUNK, H).transpose(0, 3, 1, 2)
    G = jnp.cumsum(g, axis=-1)
    idx = jnp.arange(CHUNK)
    lower = idx[:, None] >= idx[None, :]
    strict = idx[:, None] > idx[None, :]
    diff = G[..., :, None] - G[..., None, :]
    decay = jnp.where(lower, jnp.exp(jnp.where(lower, diff, 0.0)), 0.0)
    kb = k * beta[..., None]
    Lmat = jnp.where(strict, jnp.einsum('bhncd,bhnsd->bhncs', kb, k) * decay, 0.0)
    A = Lmat + jnp.eye(CHUNK, dtype=jnp.float32)
    rhs = jnp.concatenate([v * beta[..., None], kb * jnp.exp(G)[..., None]], axis=-1)
    sol = lax.linalg.triangular_solve(A, rhs, left_side=True, lower=True, unit_diagonal=True)
    u, w = sol[..., :DV], sol[..., DV:]
    attn = jnp.where(lower, jnp.einsum('bhncd,bhnsd->bhncs', q, k) * decay, 0.0)

    def step(S, inp):
        q_c, k_c, u_c, w_c, G_c, a_c = inp
        v_new = u_c - jnp.einsum('bhcd,bhde->bhce', w_c, S)
        o = (jnp.einsum('bhcd,bhde->bhce', q_c * jnp.exp(G_c)[..., None], S)
             + jnp.einsum('bhcs,bhse->bhce', a_c, v_new))
        G_last = G_c[..., -1]
        k_dec = k_c * jnp.exp(G_last[..., None] - G_c)[..., None]
        S = S * jnp.exp(G_last)[..., None, None] + jnp.einsum('bhcd,bhce->bhde', k_dec, v_new)
        return S, o

    xs = tuple(jnp.moveaxis(a, 2, 0) for a in (q, k, u, w, G, attn))
    S0 = jnp.zeros((B, H, DK, DV), jnp.float32)
    _, o = lax.scan(step, S0, xs)
    return o.transpose(1, 0, 3, 2, 4).reshape(B, T, H, DV)

def _gdn_branch(qkv, z, b_logit, a_logit, conv_w, A_log, dt_bias, gdn_norm):
    B, T, _ = qkv.shape
    dtype = qkv.dtype
    qkv = _causal_conv_silu(qkv, conv_w)
    q = _l2norm(qkv[..., :GDN_QK].reshape(B, T, GDN_HEADS, GDN_DK)) * (GDN_DK ** -0.5)
    k = _l2norm(qkv[..., GDN_QK:2 * GDN_QK].reshape(B, T, GDN_HEADS, GDN_DK))
    v = qkv[..., 2 * GDN_QK:].reshape(B, T, GDN_HEADS, GDN_DV).astype(jnp.float32)
    beta = jax.nn.sigmoid(b_logit.astype(jnp.float32))
    g = -jnp.exp(A_log.astype(jnp.float32)) * jax.nn.softplus(a_logit.astype(jnp.float32) + dt_bias.astype(jnp.float32))
    o = _gated_delta_chunked(q, k, v, beta, g)
    o = o * lax.rsqrt(jnp.mean(o * o, axis=-1, keepdims=True) + EPS) * gdn_norm.astype(jnp.float32)
    o = o * jax.nn.silu(z.reshape(B, T, GDN_HEADS, GDN_DV).astype(jnp.float32))
    return o.reshape(B, T, GDN_V).astype(dtype)

def first_inputs(seed: int = 0) -> dict:
    key = jax.random.key(seed)
    ks = jax.random.split(key, 24)
    L, D = DEPTH, D_MODEL
    f32 = jnp.float32

    def nrm(k, shape, fan_in, gain=1.0):
        return gain * fan_in ** -0.5 * jax.random.normal(k, shape, f32)

    def gain(k, shape):
        return 1.0 + 0.02 * jax.random.normal(k, shape, f32)

    x = jax.random.normal(ks[0], (BATCH, SEQ, D), f32)
    c = jax.random.normal(ks[1], (BATCH, D), f32)
    positions = (jnp.arange(SEQ, dtype=jnp.int32)[None, :]
                 + jax.random.randint(ks[2], (BATCH, 1), 0, 1024, dtype=jnp.int32))
    dt = jnp.exp(jax.random.uniform(ks[15], (L, GDN_HEADS), f32, math.log(1e-3), math.log(1e-1)))
    return {
        'x': x,
        'c': c,
        'positions': positions,
        'w_ada': nrm(ks[3], (L, D, 6 * D), D, 0.5),
        'b_ada': 0.01 * jax.random.normal(ks[4], (L, 6 * D), f32),
        'norm_mix': gain(ks[5], (L, D)),
        'norm_ffn': gain(ks[6], (L, D)),
        'w_in': nrm(ks[7], (L, D, IN_WIDTH), D),
        'q_a_norm': gain(ks[8], (L, Q_LORA)),
        'kv_a_norm': gain(ks[9], (L, KV_LORA)),
        'w_uq': nrm(ks[10], (L, Q_LORA, MLA_HEADS * (QK_NOPE + QK_ROPE)), Q_LORA),
        'w_ukv': nrm(ks[11], (L, KV_LORA, MLA_HEADS * (QK_NOPE + V_HEAD)), KV_LORA),
        'w_o_mla': nrm(ks[12], (L, MLA_HEADS * V_HEAD, D), MLA_HEADS * V_HEAD),
        'conv_w': nrm(ks[13], (L, CONV_WIDTH, CONV_CH), CONV_WIDTH),
        'A_log': jnp.log(jax.random.uniform(ks[14], (L, GDN_HEADS), f32, 1.0, 16.0)),
        'dt_bias': dt + jnp.log(-jnp.expm1(-dt)),
        'gdn_norm': gain(ks[16], (L, GDN_DV)),
        'w_o_gdn': nrm(ks[17], (L, GDN_V, D), GDN_V),
        'w_o': nrm(ks[18], (L, D, D), D),
        'w_gate_up': nrm(ks[19], (L, D, 2 * D_FF), D),
        'w_down': nrm(ks[20], (L, D_FF, D), D_FF),
        'final_norm': gain(ks[21], (D,)),
    }

def first_block(x, c, positions, w_ada, b_ada, norm_mix, norm_ffn, w_in, q_a_norm, kv_a_norm,
              w_uq, w_ukv, w_o_mla, conv_w, A_log, dt_bias, gdn_norm, w_o_gdn, w_o,
              w_gate_up, w_down, final_norm):
    cos, sin = _rope_tables(positions)
    c_act = jax.nn.silu(c)
    for l in range(DEPTH):
        mod = c_act @ w_ada[l] + b_ada[l]
        sh_a, sc_a, gt_a, sh_f, sc_f, gt_f = [m[:, None, :] for m in jnp.split(mod, 6, axis=-1)]
        h = _rmsnorm(x, norm_mix[l]) * (1.0 + sc_a) + sh_a
        p = h @ w_in[l]
        c_q, c_kv, k_pe, q_g, k_g, v_g, z, b_logit, a_logit, gate_logits = _split_cols(p)
        y_a = _mla_branch(c_q, c_kv, k_pe, q_a_norm[l], kv_a_norm[l], w_uq[l], w_ukv[l], cos, sin) @ w_o_mla[l]
        qkv = jnp.concatenate([q_g, k_g, v_g], axis=-1)
        y_b = _gdn_branch(qkv, z, b_logit, a_logit, conv_w[l], A_log[l], dt_bias[l], gdn_norm[l]) @ w_o_gdn[l]
        g_a, g_b = jnp.split(jax.nn.sigmoid(gate_logits), 2, axis=-1)
        mix = (g_a * y_a + g_b * y_b) @ w_o[l]
        x = x + gt_a * mix
        h = _rmsnorm(x, norm_ffn[l]) * (1.0 + sc_f) + sh_f
        gate, up = jnp.split(h @ w_gate_up[l], 2, axis=-1)
        x = x + gt_f * ((jax.nn.silu(gate) * up) @ w_down[l])
    return _rmsnorm(x, final_norm)


GRID_W = 64
MIX_WIDTH = D_MODEL
CONV_WIDTH_2 = MIX_WIDTH // 2
NA_HEADS = 16
NA_HEAD_DIM = (MIX_WIDTH - CONV_WIDTH_2) // NA_HEADS
NA_WIDTH = NA_HEADS * NA_HEAD_DIM
CONV_KERNEL = 31
WIN_ROWS_MAX = 8
WIN_COLS = 16
D_FF_2 = 4 * D_MODEL
IN_COLS = 2 * CONV_WIDTH_2 + 3 * NA_WIDTH
RMS_EPS = 1e-6
LN_EPS = 1e-5
NEG_INF = -1e30


def rms_norm(x, g):
    xf = x.astype(jnp.float32)
    y = xf * lax.rsqrt(jnp.mean(xf * xf, axis=-1, keepdims=True) + RMS_EPS)
    return (y * g.astype(jnp.float32)).astype(x.dtype)

def layer_norm(x, g, b):
    xf = x.astype(jnp.float32)
    mu = jnp.mean(xf, axis=-1, keepdims=True)
    xc = xf - mu
    var = jnp.mean(xc * xc, axis=-1, keepdims=True)
    y = xc * lax.rsqrt(var + LN_EPS) * g.astype(jnp.float32) + b.astype(jnp.float32)
    return y.astype(x.dtype)

def conformer_conv_group(a, gate, w_dw, b_dw, ln_g, ln_b):
    u = a * jax.nn.sigmoid(gate)
    u = lax.conv_general_dilated(
        u, w_dw[:, None, :].astype(u.dtype),
        window_strides=(1,),
        padding=[(CONV_KERNEL // 2, CONV_KERNEL // 2)],
        dimension_numbers=("NWC", "WIO", "NWC"),
        feature_group_count=CONV_WIDTH_2,
    ) + b_dw.astype(u.dtype)
    return jax.nn.silu(layer_norm(u, ln_g, ln_b))

def neighbourhood_attention_group(q, k, v, rpb):
    B, T, _ = q.shape
    rows = T // GRID_W
    kr = min(WIN_ROWS_MAX, rows)
    r = np.arange(rows)
    c = np.arange(GRID_W)
    row_start = np.clip(r - kr // 2, 0, rows - kr)
    row_idx = row_start[:, None] + np.arange(kr)[None, :]
    col_start = np.clip(c - WIN_COLS // 2, 0, GRID_W - WIN_COLS)
    col_mask = (c[None, :] >= col_start[:, None]) & (c[None, :] < col_start[:, None] + WIN_COLS)
    dr = row_idx - r[:, None] + (WIN_ROWS_MAX - 1)
    dc = np.clip(c[None, :] - c[:, None], -(WIN_COLS - 1), WIN_COLS - 1) + (WIN_COLS - 1)
    bias = rpb[:, dr[:, None, :, None], dc[None, :, None, :]].astype(jnp.float32)

    def to_grid(t):
        return t.reshape(B, rows, GRID_W, NA_HEADS, NA_HEAD_DIM)

    qg, kg, vg = to_grid(q), to_grid(k), to_grid(v)
    k_rows = kg[:, row_idx]
    v_rows = vg[:, row_idx]
    s = jnp.einsum("brwhd,brkvhd->bhrwkv", qg, k_rows,
                   preferred_element_type=jnp.float32) * (NA_HEAD_DIM ** -0.5)
    s = jnp.where(col_mask[:, None, :], s + bias, NEG_INF)
    p = jax.nn.softmax(s.reshape(B, NA_HEADS, rows, GRID_W, kr * GRID_W), axis=-1)
    p = p.reshape(s.shape).astype(v.dtype)
    o = jnp.einsum("bhrwkv,brkvhd->brwhd", p, v_rows)
    return o.reshape(B, T, NA_WIDTH)

def second_inputs(seed: int = 0) -> dict:
    key = jax.random.key(seed)
    ks = jax.random.split(key, 16)
    f32 = jnp.float32
    x = jax.random.normal(ks[0], (BATCH, SEQ, D_MODEL), f32)
    w_in = jax.random.normal(ks[1], (DEPTH, D_MODEL, IN_COLS), f32) * D_MODEL ** -0.5
    w_dw = jax.random.normal(ks[2], (DEPTH, CONV_KERNEL, CONV_WIDTH_2), f32) * CONV_KERNEL ** -0.5
    b_dw = jax.random.normal(ks[3], (DEPTH, CONV_WIDTH_2), f32) * 0.01
    conv_ln_g = 1.0 + 0.05 * jax.random.normal(ks[4], (DEPTH, CONV_WIDTH_2), f32)
    conv_ln_b = 0.01 * jax.random.normal(ks[5], (DEPTH, CONV_WIDTH_2), f32)
    rpb = 0.02 * jax.random.normal(ks[6], (DEPTH, NA_HEADS, 2 * WIN_ROWS_MAX - 1, 2 * WIN_COLS - 1), f32)
    w_out = jax.random.normal(ks[7], (DEPTH, MIX_WIDTH, D_MODEL), f32) * MIX_WIDTH ** -0.5
    w_up = jax.random.normal(ks[8], (DEPTH, D_MODEL, D_FF_2), f32) * D_MODEL ** -0.5
    w_down = jax.random.normal(ks[9], (DEPTH, D_FF_2, D_MODEL), f32) * D_FF_2 ** -0.5
    pre_mix_g = 1.0 + 0.05 * jax.random.normal(ks[10], (DEPTH, D_MODEL), f32)
    post_mix_g = 1.0 + 0.05 * jax.random.normal(ks[11], (DEPTH, D_MODEL), f32)
    pre_mlp_g = 1.0 + 0.05 * jax.random.normal(ks[12], (DEPTH, D_MODEL), f32)
    post_mlp_g = 1.0 + 0.05 * jax.random.normal(ks[13], (DEPTH, D_MODEL), f32)
    return {"x": x, "w_in": w_in, "w_dw": w_dw, "b_dw": b_dw, "conv_ln_g": conv_ln_g,
            "conv_ln_b": conv_ln_b, "rpb": rpb, "w_out": w_out, "w_up": w_up, "w_down": w_down,
            "pre_mix_g": pre_mix_g, "post_mix_g": post_mix_g, "pre_mlp_g": pre_mlp_g,
            "post_mlp_g": post_mlp_g}

def second_block(x, w_in, w_dw, b_dw, conv_ln_g, conv_ln_b, rpb, w_out, w_up, w_down,
              pre_mix_g, post_mix_g, pre_mlp_g, post_mlp_g):
    splits = [CONV_WIDTH_2, 2 * CONV_WIDTH_2, 2 * CONV_WIDTH_2 + NA_WIDTH, 2 * CONV_WIDTH_2 + 2 * NA_WIDTH]
    for l in range(DEPTH):
        h = rms_norm(x, pre_mix_g[l])
        proj = h @ w_in[l]
        a, gate, q, k, v = jnp.split(proj, splits, axis=-1)
        yc = conformer_conv_group(a, gate, w_dw[l], b_dw[l], conv_ln_g[l], conv_ln_b[l])
        ya = neighbourhood_attention_group(q, k, v, rpb[l])
        mix = jnp.concatenate([yc, ya], axis=-1) @ w_out[l]
        x = x + rms_norm(mix, post_mix_g[l])
        h = rms_norm(x, pre_mlp_g[l])
        f = jnp.square(jax.nn.relu(h @ w_up[l])) @ w_down[l]
        x = x + rms_norm(f, post_mlp_g[l])
    return x


def setup_inputs(seed=0):
    out = dict(first_inputs(seed))
    for name, value in second_inputs(seed + 1).items():
        if name != "x":
            out[name + "_2"] = value
    return out


def reference(
    x, c, positions, w_ada, b_ada, norm_mix, norm_ffn, w_in, q_a_norm, kv_a_norm, w_uq, w_ukv,
    w_o_mla, conv_w, A_log, dt_bias, gdn_norm, w_o_gdn, w_o, w_gate_up, w_down, final_norm,
    w_in_2, w_dw_2, b_dw_2, conv_ln_g_2, conv_ln_b_2, rpb_2, w_out_2, w_up_2, w_down_2,
    pre_mix_g_2, post_mix_g_2, pre_mlp_g_2, post_mlp_g_2,
):
    x = first_block(
        x, c, positions, w_ada, b_ada, norm_mix, norm_ffn, w_in, q_a_norm, kv_a_norm, w_uq,
        w_ukv, w_o_mla, conv_w, A_log, dt_bias, gdn_norm, w_o_gdn, w_o, w_gate_up, w_down,
        final_norm,
    )
    return second_block(
        x, w_in_2, w_dw_2, b_dw_2, conv_ln_g_2, conv_ln_b_2, rpb_2, w_out_2, w_up_2, w_down_2,
        pre_mix_g_2, post_mix_g_2, pre_mlp_g_2, post_mlp_g_2,
    )


_drawn_inputs = setup_inputs


def setup_inputs(seed=0):
    import zlib

    import numpy as np

    out = dict(_drawn_inputs(seed))
    spreads = {}
    factors = {'b_ada': 4.874,
     'norm_mix': 8.0,
     'norm_ffn': 8.0,
     'q_a_norm': 8.0,
     'kv_a_norm': 8.0,
     'gdn_norm': 8.0,
     'b_dw_2': 4.215,
     'conv_ln_b_2': 7.949,
     'rpb_2': 8.0}
    for name, (base, spread) in spreads.items():
        noise = np.random.default_rng([zlib.crc32(name.encode()), seed]).standard_normal(out[name].shape)
        drawn = base * np.exp(spread * noise) if base else spread * noise
        out[name] = jnp.asarray(drawn.astype(out[name].dtype))
    for name, factor in factors.items():
        out[name] = (out[name] * factor).astype(out[name].dtype)
    return out
```

```python
import numpy as np
import concourse.bass as bass
from concourse import mybir
from contextlib import ExitStack

T = 256
NRAW, NHL = 5, 3
N_TILES = 6864
N_ADA = 192
ADA_FIRST = 64
ADA_EVERY = 2

COLS = {}
_n = 0
for _name, _w in (("c", 16), ("b_ada", 96), ("norm_mix", 16), ("norm_ffn", 16), ("q_a_norm", 4), ("kv_a_norm", 4),
                  ("conv_w", 96), ("gdn_norm", 1), ("final_norm", 16), ("pre_mix", 16), ("post_mix", 16),
                  ("pre_mlp", 16), ("post_mlp", 16), ("w_dw", 248), ("b_dw", 8), ("ln_g", 8), ("ln_b", 8),
                  ("A_log", 8), ("dt_bias", 8)):
    COLS[_name] = (_n, _w)
    _n += _w
NCOLS = _n

CONSTS = {}
_n = 0
for _name, _w in (("ident", 128), ("ones", 128), ("tri", 128), ("ch", 128), ("lm", 768), ("mm", 256), ("nm", 256),
                  ("rot", 128), ("invf", 1), ("pad", 1)):
    CONSTS[_name] = (_n, _w)
    _n += _w
NCONST = _n


def const_array():
    a = np.zeros((128, NCONST), np.float32)

    def put(name, v):
        o, w = CONSTS[name]
        a[:, o:o + w] = v
    s = np.arange(128)[:, None]
    c = np.arange(128)[None, :]
    put("ident", s == c)
    put("ones", 1.0)
    same = (s // 64) == (c // 64)
    put("tri", (s <= c) & same)
    put("ch", same)
    put("lm", np.concatenate([((c // k) % 2 == 1) & ((s // k) == (c // k) - 1) for k in (1, 2, 4, 8, 16, 32)], axis=1))
    k = np.arange(256)[None, :]
    put("mm", np.where(k <= 128 + s, 0.0, -1e30))
    start = np.clip(s % 64 - 8, 0, 48)
    put("nm", np.where((k % 64 >= start) & (k % 64 < start + 16), 0.0, -1e30))
    rot = np.zeros((128, 128), np.float32)
    for b in (0, 64):
        for j in range(32):
            rot[b + 32 + j, b + j] = -1.0
            rot[b + j, b + 32 + j] = 1.0
    put("rot", rot)
    inv = (np.float32(1.0) / (np.float32(10000.0) ** (np.arange(0, 64, 2, dtype=np.float32) / np.float32(64)))).astype(np.float32)
    put("invf", inv[np.arange(128) % 32][:, None])
    return a


def program(nc, xT, pos, cols_d, consts_d, wada, wst, bias_d, out, log):
    f32 = mybir.dt.float32
    f32r = mybir.dt.float32r
    i32 = mybir.dt.int32
    ALU = mybir.AluOpType
    ACT = mybir.ActivationFunctionType
    AX = mybir.AxisListType.X
    add, sub, mult = ALU.add, ALU.subtract, ALU.mult
    ctx = ExitStack()
    with ctx:
        def sb(name, shape, dt=f32):
            return ctx.enter_context(nc.sbuf_tensor(name, shape, dt))

        RAW = sb("RAW", [128, NRAW, 1024])
        HI = sb("HI", [128, NHL, 1024], f32r)
        LO = sb("LO", [128, NHL, 1024], f32r)
        H1 = sb("H1", [128, 16, 512], f32r)
        H2 = sb("H2", [128, 16, 512], f32r)
        CO = sb("CO", [128, NCOLS])
        CN = sb("CN", [128, NCONST])
        MOD = sb("MOD", [128, 96])
        SC = sb("SC", [128, 256])
        TV = sb("TV", [128, 4, 256])
        TE = sb("TE", [128, 3, 256])
        RS = sb("RS", [128, 3, 256])
        SQ = sb("SQ", [128, 2, 256])
        ADA = sb("ADA", [128, 1024])
        X = sb("X", [128, 16, 256])
        B1 = sb("B1", [128, 24, 256])
        B2 = sb("B2", [128, 24, 256])
        B3 = sb("B3", [128, 8, 256])
        BANK = [ctx.enter_context(nc.psum_tensor(f"BK{i}", [128, 512], f32)) for i in range(8)]

        def sem(name):
            return ctx.enter_context(nc.semaphore(name))

        ENG = ("pe", "act", "dve", "pool", "sp")
        sems = {e: sem("s_" + e) for e in ENG}
        for i in range(NRAW):
            sems[f"r{i}"] = sem(f"s_raw{i}")
        for i in range(4):
            sems[f"b{i}"] = sem(f"s_bias{i}")
        for n in ("cols", "consts", "x", "pos", "x2", "out"):
            sems[n] = sem("s_" + n)
        queue = {e: [] for e in ENG}
        count = {e: 0 for e in ENG}

        def put(e, fn, waits):
            flat = []
            for w in waits:
                flat += w if isinstance(w, list) else [w] if w is not None else []
            queue[e].append((fn, flat, None))
            count[e] += 1
            return (e, count[e])

        def V(fn, *waits):
            return put("dve", fn, waits)

        def A(fn, *waits):
            return put("act", fn, waits)

        def G(fn, *waits):
            return put("pool", fn, waits)

        def P(fn, *waits):
            return put("pe", fn, waits)

        def D(name, value, fn, *waits):
            flat = []
            for w in waits:
                flat += w if isinstance(w, list) else [w] if w is not None else []
            queue["sp"].append((fn, flat, name))
            return (name, value)

        def now():
            return [(e, count[e]) for e in ("pe", "act", "dve", "pool")]

        def col(name, j=0, w=1):
            return CO[:, COLS[name][0] + j:COLS[name][0] + j + w]

        def cn(name, a=0, b=None):
            o, w = CONSTS[name]
            return CN[:, o + a:o + (w if b is None else b)]

        class Ring:
            def __init__(self, items):
                self.items = items
                self.free = [[] for _ in items]
                self.idle = list(range(len(items)))

            def get(self):
                i = self.idle.pop(0)
                return i, self.items[i], self.free[i]

            def release(self, i, *toks):
                self.free[i] = list(toks)
                assert i not in self.idle
                self.idle.append(i)

        tv = Ring([TV[:, i, :] for i in range(4)])
        te = Ring([TE[:, i, :] for i in range(3)])
        lbank = Ring(BANK[0:3])
        mbank = Ring(BANK[3:8])

        tk_cols = D("cols", 16, lambda e: e.dma_start(CO[:, :], cols_d))
        raw_free = [[] for _ in range(NRAW)]
        kinds = ["A"] * ADA_FIRST
        a = ADA_FIRST
        for i in range(N_TILES // 8):
            kinds.append("L")
            if i % ADA_EVERY == ADA_EVERY - 1 and a < N_ADA:
                kinds.append("A")
                a += 1
        lin_at = [i for i, k in enumerate(kinds) if k == "L"]
        st = {"load": 0, "proc": 0, "na": 0, "nl": 0, "la": 0, "ll": 0, "tile": 0}
        split_tok = {}
        unit_pe = {}
        mod_tok = [None] * 12
        ada_last = [None]
        ada_free = [[]]

        def load_next():
            s = st["load"]
            if s >= len(kinds):
                return
            slot = s % NRAW
            if kinds[s] == "A":
                src = wada[st["la"]]
                st["la"] += 1
            else:
                src = wst[st["ll"]]
                st["ll"] += 1
            D(f"r{slot}", 16 * (s // NRAW + 1), lambda e: e.dma_start(RAW[:, slot, :], src), *raw_free[slot])
            st["load"] += 1

        def proc_next():
            s = st["proc"]
            slot = s % NRAW
            got = (f"r{slot}", 16 * (s // NRAW + 1))
            if kinds[s] == "A":
                i = st["na"]
                st["na"] += 1
                j, t = divmod(i, 16)
                if t == 0:
                    k = V(lambda e: e.tensor_scalar(ADA[:, :], RAW[:, slot, :], SC[:, 0:1], None, mult), got, c_tok, ada_free[0])
                else:
                    k = V(lambda e: e.scalar_tensor_tensor(ADA[:, :], RAW[:, slot, :], SC[:, t:t + 1], ADA[:, :], mult, add),
                          got, ada_last[0])
                ada_last[0] = k
                raw_free[slot] = [k]
                if t == 15:
                    bi, bk, fr = mbank.get()

                    def mm(e):
                        for q in range(8):
                            r = e.matmul(bk[:, q:q + 1], ADA[:, q * 128:q * 128 + 128], cn("ones", 0, 1), start=True, stop=True)
                        return r
                    m = P(mm, k, fr, tk_consts)
                    ada_free[0] = [m]
                    ev = V(lambda e: e.tensor_tensor(MOD[:, 8 * j:8 * j + 8], bk[:, 0:8], col("b_ada", 8 * j, 8), add), m, tk_cols)
                    mbank.release(bi, ev)
                    mod_tok[j] = ev
            else:
                u = st["nl"]
                st["nl"] += 1
                h = u % NHL
                old = unit_pe.get(u - NHL)
                k1 = A(lambda e: e.activation(HI[:, h, :], RAW[:, slot, :], ACT.Copy), got, old)
                k2 = V(lambda e: e.tensor_tensor(LO[:, h, :], RAW[:, slot, :], HI[:, h, :].bitcast(f32), sub), k1, old)
                split_tok[u] = k2
                raw_free[slot] = [k2]
            st["proc"] += 1
            load_next()

        def feed(u):
            goal = lin_at[min(u, len(lin_at) - 1)]
            while st["proc"] <= goal:
                proc_next()

        pending = []

        def flush(force=False):
            while pending and (force or pending[0][0] <= st["tile"]):
                pending.pop(0)[1]()

        def block(H, toks, k0, wname, kbase, n, evac):
            while not lbank.idle:
                pending.pop(0)[1]()
            bi, bk, fr = lbank.get()
            K = len(toks)
            for k in range(K):
                t = st["tile"]
                st["tile"] += 1
                log.append((wname, kbase + k, n))
                u, q = divmod(t, 8)
                if q == 0:
                    feed(u)

                def mm(e, k=k, u=u, q=q):
                    hh = HI[:, u % NHL, q * 128:q * 128 + 128]
                    ll = LO[:, u % NHL, q * 128:q * 128 + 128]
                    e.matmul(bk[:, :], hh, H[:, k0 + k, :], start=(k == 0), stop=False, skip_group_check=True)
                    return e.matmul(bk[:, 256:512], ll, H[:, k0 + k, 0:256], start=False, stop=(k == K - 1), skip_group_check=True)
                tok = P(mm, split_tok[u], toks[k], fr if k == 0 else None)
                if q == 7:
                    unit_pe[u] = tok
                    feed(u + 2)
                    flush()
                    yield
            pending.append((st["tile"] + 8, lambda: evac(bk, tok, bi)))
            if q != 7:
                yield

        def raw_sum(dst, bk, tok, bi, *waits):
            i, t, fr = te.get()
            a = A(lambda e: e.activation(t, bk[:, 256:512], ACT.Copy), tok, fr)
            v = V(lambda e: e.tensor_tensor(dst, bk[:, 0:256], t, add), a, *waits)
            te.release(i, v)
            lbank.release(bi, v)
            return v

        def split(dst, j, src, tok, *waits, bias=None):
            if bias is None:
                a = A(lambda e: e.activation(dst[:, j, 0:256], src, ACT.Copy), tok, *waits)
                return V(lambda e: e.tensor_tensor(dst[:, j, 256:512], src, dst[:, j, 0:256].bitcast(f32), sub), a)
            a = A(lambda e: e.activation(dst[:, j, 0:256], src, ACT.Identity, bias=bias), tok, *waits)
            return V(lambda e: e.scalar_tensor_tensor(dst[:, j, 256:512], src, bias, dst[:, j, 0:256].bitcast(f32), add, sub), a)

        def run(gen):
            for _ in gen:
                pass

        def rsqrt(y, t, src, scale, eps, *waits):
            k = V(lambda e: e.tensor_scalar(t, src, scale, eps, mult, add), *waits)
            a = A(lambda e: e.activation(y, t, ACT.Ln), k)
            a = A(lambda e: e.activation(y, y, ACT.Exp, scale=-0.5), a)
            k = V(lambda e: e.tensor_tensor(t, t, y, mult), a)
            k = V(lambda e: e.tensor_tensor(t, t, y, mult), k)
            k = V(lambda e: e.tensor_scalar(t, t, -0.5, 1.5, mult, add), k)
            return V(lambda e: e.tensor_tensor(y, y, t, mult), k)

        class Stats:
            def __init__(self, *waits):
                self.last = list(waits)
                self.first = True

            def square(self, src, tok):
                if self.first:
                    k = G(lambda e: e.tensor_tensor(SQ[:, 0, :], src, src, mult), tok, self.last)
                    self.first = False
                else:
                    k = G(lambda e: e.tensor_tensor(SQ[:, 1, :], src, src, mult), tok, self.last)
                    k = G(lambda e: e.tensor_tensor(SQ[:, 0, :], SQ[:, 0, :], SQ[:, 1, :], add), k)
                self.last = [k]
                return k

            def finish(self, n, eps, *waits):
                bi, bk, fr = mbank.get()
                m = P(lambda e: e.matmul(bk[:, 0:256], cn("ones"), SQ[:, 0, :], start=True, stop=True), self.last, fr)
                self.done = m
                v = rsqrt(RS[:, 0, :], RS[:, 1, :], bk[:, 0:256], 1.0 / n, eps, m, *waits)
                mbank.release(bi, v)
                return v

        def now_x():
            return now()

        tk_consts = D("consts", 16, lambda e: e.dma_start(CN[:, :], consts_d))
        for _ in range(NRAW):
            load_next()
        for i in range(4):
            tk_x = D("x", 16 * i + 16, lambda e, i=i: e.dma_start(X[:, 4 * i:4 * i + 4, :], xT[:, 4 * i:4 * i + 4, :]))
        PI = B3[:, 1, :].bitcast(i32)
        tk_pos = D("pos", 16, lambda e: e.dma_start(PI, pos.rearrange("(a n) -> a n", a=1).broadcast_to([128, 256])))

        k = A(lambda e: e.activation(SC[:, 16:32], col("c", 0, 16), ACT.Sigmoid), tk_cols)
        c_tok = V(lambda e: e.tensor_tensor(SC[:, 0:16], SC[:, 16:32], col("c", 0, 16), mult), k)

        COS, SIN = B3[:, 2, :], B3[:, 3, :]
        F = B3[:, 4, :]
        Q = B3[:, 5, :]
        k = V(lambda e: e.tensor_copy(F, PI), tk_pos, tk_consts)
        k = V(lambda e: e.tensor_scalar(F, F, cn("invf"), None, mult), k)
        k = V(lambda e: e.tensor_scalar(Q, F, float(1.0 / (2 * np.pi)), 12582912.0, mult, add), k)
        k = V(lambda e: e.tensor_scalar(Q, Q, 12582912.0, None, sub), k)
        rest = 2 * np.pi
        parts = []
        for bits in (8, 8, 8, 24):
            step = 2.0 ** (np.floor(np.log2(rest)) - bits + 1)
            p = float(np.floor(rest / step) * step)
            parts.append(p)
            rest = rest - p
        for p in parts:
            k = V(lambda e, p=p: e.scalar_tensor_tensor(F, Q, -p, F, mult, add), k)
        PIF = 3.1415925
        k = V(lambda e: e.tensor_scalar(F, F, PIF, -PIF, ALU.min, ALU.max), k)
        a1 = A(lambda e: e.activation(SIN, F, ACT.Sin), k)
        k = V(lambda e: e.scalar_tensor_tensor(Q, F, -1.0, F, mult, ALU.max), k)
        k = V(lambda e: e.tensor_scalar(Q, Q, -1.0, float(np.pi / 2), mult, add), k)
        tk_cos = A(lambda e: e.activation(COS, Q, ACT.Sin), k, a1)
        B3_free = tk_cos

        S1 = Stats(tk_x)
        for j in range(16):
            S1.square(X[:, j, :], None)
        for s in range(ADA_FIRST):
            proc_next()
        rs_tok = S1.finish(2048, 1e-6)

        def adaln(shift, scale, normname, S_tok, xtoks, *waits):
            m = [mod_tok[2 * shift], mod_tok[2 * shift + 1], mod_tok[2 * scale], mod_tok[2 * scale + 1]]
            g = V(lambda e: e.scalar_tensor_tensor(SC[:, 32:48], MOD[:, 16 * scale:16 * scale + 16], 1.0, col(normname, 0, 16), add, mult),
                  m, tk_cols, now())
            out = []
            for j in range(16):
                i, t, fr = tv.get()
                k = V(lambda e, j=j, t=t: e.scalar_tensor_tensor(t, X[:, j, :], SC[:, 32 + j:33 + j], RS[:, 0, :], mult, mult),
                      g, S_tok, xtoks[j], fr)
                k = split(H1, j, t, k, *waits, bias=MOD[:, 16 * shift + j:16 * shift + j + 1])
                tv.release(i, k)
                out.append(k)
            return out

        h_tok = adaln(0, 1, "norm_mix", rs_tok, [tk_x] * 16)

        CQ = [B2[:, i, :] for i in range(8)]
        KPE = B3[:, 0, :]
        RN = {}

        def rope(dst, src, tok, *waits):
            bi, bk, fr = mbank.get()
            m = P(lambda e: e.matmul(bk[:, 0:256], cn("rot"), src, start=True, stop=True), tok, fr)
            i, t, fr2 = tv.get()
            v1 = V(lambda e: e.tensor_tensor(t, bk[:, 0:256], SIN, mult), m, tk_cos, fr2)
            v2 = V(lambda e: e.tensor_tensor(dst, src, COS, mult), m, *waits)
            v = V(lambda e: e.tensor_tensor(dst, dst, t, add), v1, v2)
            mbank.release(bi, v1)
            tv.release(i, v)
            return v

        cq_tok = [None] * 8

        def ev_c(j):
            def f(bk, tok, bi):
                cq_tok[j] = raw_sum(CQ[j], bk, tok, bi)
            return f

        def ev_kpe(bk, tok, bi):
            k = raw_sum(KPE, bk, tok, bi)
            RN["kpe"] = rope(KPE, KPE, k)

        H2_tok = [None] * 16
        for j in range(8):
            run(block(H1, h_tok, 0, "w_in", 0, j, ev_c(j)))
        kpe_gen = block(H1, h_tok, 0, "w_in", 0, 8, ev_kpe)
        run(kpe_gen)
        flush(True)

        qkv_tok = [None] * 24
        lin_tok = {}

        def ev_qkv(j):
            def f(bk, tok, bi):
                dst = B1[:, j, :]
                i, t, fr = tv.get()
                k = raw_sum(t, bk, tok, bi, fr)
                o = COLS["conv_w"][0] + 4 * j
                v = V(lambda e: e.tensor_scalar(dst, t, CO[:, o + 3:o + 4], None, mult), k)
                for s in (1, 2, 3):
                    v = V(lambda e, s=s: e.scalar_tensor_tensor(dst[:, s:256], t[:, 0:256 - s], CO[:, o + 3 - s:o + 4 - s], dst[:, s:256], mult, add), v)
                s1 = A(lambda e: e.activation(t, dst, ACT.Sigmoid), v)
                v = V(lambda e: e.tensor_tensor(dst, dst, t, mult), s1)
                tv.release(i, v)
                qkv_tok[j] = v
            return f

        def filler1():
            for j in range(24):
                yield from block(H1, h_tok, 0, "w_in", 0, 9 + j, ev_qkv(j))

        fill = filler1()
        for half in range(2):
            S = Stats(*([S1.done] if half == 0 else [Sp.done]))
            for j in range(4):
                S.square(CQ[4 * half + j], cq_tok[4 * half + j])
            Sp = S
            next(fill, None)
            k = S.finish(512, 1e-6, *([h_tok[-1]] if half == 0 else [c_last]))
            name = "q_a_norm" if half == 0 else "kv_a_norm"
            for j in range(4):
                i, t, fr = tv.get()
                c_last = V(lambda e, j=j, t=t, half=half, name=name: e.scalar_tensor_tensor(t, CQ[4 * half + j], col(name, j), RS[:, 0, :], mult, mult), k, fr)
                H2_tok[4 * half + j] = split(H2, 4 * half + j, t, c_last)
                tv.release(i, H2_tok[4 * half + j])
        cq_done = now()
        QN = [X[:, i, :] for i in range(8)]
        QP = [B2[:, 8 + i, :] for i in range(4)]
        KN = [X[:, 8 + i, :] for i in range(8)]
        VT = B2[:, 12:20, :].rearrange("p a t -> p (a t)").rearrange("p (m n) -> p m n", m=2)
        qn_tok, qp_tok, kn_tok, v_tok = [None] * 8, [None] * 4, [None] * 8, [None] * 8

        def ev_plain(lst, toks, j):
            def f(bk, tok, bi):
                toks[j] = raw_sum(lst[j], bk, tok, bi, cq_done)
            return f

        def ev_qp(j):
            def f(bk, tok, bi):
                k = raw_sum(QP[j], bk, tok, bi, cq_done)
                qp_tok[j] = rope(QP[j], QP[j], k)
            return f

        def ev_v(j):
            def f(bk, tok, bi):
                i, t, fr = tv.get()
                k = raw_sum(t, bk, tok, bi, fr)
                mi, mk, mf = mbank.get()

                def tr(e):
                    for m in range(2):
                        r = e.transpose(mk[:, 128 * m:128 * m + 128], t[:, 128 * m:128 * m + 128], cn("ident"))
                    return r
                m = P(tr, k, mf)
                tv.release(i, m)
                v_tok[j] = A(lambda e: e.activation(VT[:, :, 128 * j:128 * j + 128], mk[:, 0:256].rearrange("p (m n) -> p m n", m=2), ACT.Copy), m, cq_done)
                mbank.release(mi, v_tok[j])
            return f

        for j in range(8):
            run(block(H2, H2_tok[0:4], 0, "w_uq", 0, j, ev_plain(QN, qn_tok, j)))
        for j in range(4):
            run(block(H2, H2_tok[0:4], 0, "w_uq", 0, 8 + j, ev_qp(j)))
        for j in range(8):
            run(block(H2, H2_tok[4:8], 4, "w_ukv", 0, j, ev_plain(KN, kn_tok, j)))
        for j in range(8):
            run(block(H2, H2_tok[4:8], 4, "w_ukv", 0, 8 + j, ev_v(j)))
        next(fill, None)
        next(fill, None)
        flush(True)

        def pipeline(n, stages, between):
            d = len(stages)
            for step in range(n + d - 1):
                for s in range(d - 1, -1, -1):
                    i = step - s
                    if 0 <= i < n:
                        stages[s](i)
                between(step)

        pr = Ring([B3[:, 4 + i, :] for i in range(4)])
        ptr = Ring([B2[:, 20, :], B2[:, 21, :]])
        mst = {}
        SM = SC[:, 64:256]

        def softmax_stages(n, scores, biasmask, scale, keys, pv):
            def s0(i):
                bi, bk, fr = mbank.get()
                m = scores(i, bk, fr)
                pi, p, pf = pr.get()
                v = biasmask(i, p[:, 0:keys(i)], bk[:, 0:keys(i)], m, pf)
                mbank.release(bi, v)
                mst[i] = [pi, p[:, 0:keys(i)], v]

            def s1(i):
                pi, p, v = mst[i]
                c = 3 * (i % 32)
                v = V(lambda e: e.tensor_reduce(SM[:, c:c + 1], p, AX, ALU.max, negate=True), v)
                a = A(lambda e: e.activation(p, p, ACT.Exp, bias=SM[:, c:c + 1], accum_out=SM[:, c + 1:c + 2]), v)
                mst[i].append(a)

            def s2(i):
                pi, p, _, a = mst[i]
                c = 3 * (i % 32)
                v = V(lambda e: e.reciprocal(SM[:, c + 2:c + 3], SM[:, c + 1:c + 2]), a)
                v = V(lambda e: e.tensor_scalar(p, p, SM[:, c + 2:c + 3], None, mult), v)
                bi, bk, fr = mbank.get()
                nk = keys(i) // 128

                def tr(e):
                    for q in range(nk):
                        r = e.transpose(bk[:, 128 * q:128 * q + 128], p[:, 128 * q:128 * q + 128], cn("ident"))
                    return r
                m = P(tr, v, fr)
                pr.release(pi, m)
                ti, t, tf = ptr.get()
                a = A(lambda e: e.activation(t[:, 0:keys(i)], bk[:, 0:keys(i)], ACT.Copy), m, tf)
                mbank.release(bi, a)
                mst[i] = [ti, t, a]

            def s3(i):
                ti, t, a = mst[i]
                ptr.release(ti, pv(i, t, a))
            return [s0, s1, s2, s3]

        SCALE = 192.0 ** -0.5
        av = {}
        mo_tok = [None] * 8

        def mla_scores(i, bk, fr):
            h, qb = divmod(i, 2)
            nk = 128 * (qb + 1)
            o = 64 * (h % 2)

            def mm(e):
                e.matmul(bk[:, 0:nk], QN[h][:, 128 * qb:128 * qb + 128], KN[h][:, 0:nk], start=True, stop=False)
                return e.matmul(bk[:, 0:nk], QP[h // 2][o:o + 64, 128 * qb:128 * qb + 128], KPE[o:o + 64, 0:nk], start=False, stop=True)
            return P(mm, qn_tok[h], kn_tok[h], qp_tok[h // 2], RN["kpe"], fr)

        def mla_mask(i, p, ps, m, pf):
            qb = i % 2
            return V(lambda e: e.scalar_tensor_tensor(p, ps, SCALE, cn("mm", 128 - 128 * qb, 256), mult, add), m, pf)

        def mla_pv(i, t, a):
            h, qb = divmod(i, 2)
            if qb == 0:
                av["b"] = mbank.get()
            bi, bk, fr = av["b"]

            def mm(e):
                for q in range(qb + 1):
                    r = e.matmul(bk[:, 128 * qb:128 * qb + 128], VT[:, q, 128 * h:128 * h + 128], t[:, 128 * q:128 * q + 128],
                                 start=(q == 0), stop=(q == qb))
                return r
            m = P(mm, a, v_tok[h], fr if qb == 0 else None)
            if qb == 1:
                x = A(lambda e: e.activation(H2[:, 8 + h, 0:256], bk[:, 0:256], ACT.Copy), m)
                mo_tok[h] = V(lambda e: e.tensor_tensor(H2[:, 8 + h, 256:512], bk[:, 0:256], H2[:, 8 + h, 0:256].bitcast(f32), sub), x)
                mbank.release(bi, mo_tok[h])
            return m

        pipeline(16, softmax_stages(16, mla_scores, mla_mask, SCALE, lambda i: 128 * (i % 2 + 1), mla_pv),
                 lambda s: [next(fill, None), next(fill, None) if s % 2 == 0 else None])
        run(fill)

        BA = B3[:, 4, :]

        def ev_ba(bk, tok, bi):
            lin_tok["ba"] = raw_sum(BA, bk, tok, bi, now())
        run(block(H1, h_tok, 0, "w_in", 0, 41, ev_ba))
        flush(True)
        mla_done = now()

        Z = [B1[:, 16 + i, :] for i in range(8)]
        YA = [B2[:, i, :] for i in range(16)]
        z_tok, ya_tok = [None] * 8, [None] * 16

        def silu_to(dst, src, tok, *waits):
            i, t, fr = te.get()
            a = A(lambda e: e.activation(t, src, ACT.Sigmoid), tok, fr)
            v = V(lambda e: e.tensor_tensor(dst, src, t, mult), a, *waits)
            te.release(i, v)
            return v

        def ev_z(j):
            def f(bk, tok, bi):
                k = raw_sum(Z[j], bk, tok, bi, rounds_done)
                z_tok[j] = silu_to(Z[j], Z[j], k)
            return f

        def ev_ga(j):
            def f(bk, tok, bi):
                k = raw_sum(YA[j], bk, tok, bi, mla_done)
                lin_tok[("g", j)] = A(lambda e: e.activation(YA[j], YA[j], ACT.Sigmoid), k)
            return f

        def ev_ya(j):
            def f(bk, tok, bi):
                i, t, fr = tv.get()
                k = raw_sum(t, bk, tok, bi, fr)
                ya_tok[j] = V(lambda e: e.tensor_tensor(YA[j], YA[j], t, mult), k, lin_tok[("g", j)])
                tv.release(i, ya_tok[j])
            return f

        def filler_z():
            for j in range(8):
                yield from block(H1, h_tok, 0, "w_in", 0, 33 + j, ev_z(j))

        def filler2():
            for j in range(16):
                yield from block(H1, h_tok, 0, "w_in", 0, 42 + j, ev_ga(j))
                yield from block(H2, mo_tok, 8, "w_o_mla", 0, j, ev_ya(j))

        fill = filler2()

        def pump(n=1):
            for _ in range(n):
                next(fill, None)

        GS = B3[:, 5, :]
        def gs(o, w=16):
            return GS[:, o:o + w]
        BA_T, BETA, SPX, SPE, GG, GC, GL, BG, DK = (gs(32 * 0, 32), gs(32), gs(48), gs(64), gs(80), gs(96), gs(112), gs(128), gs(144))
        EA = GS[:, 160:168]

        def m28(x):
            return x.rearrange("p (m h) -> p m h", m=2)

        bi, bk, fr = mbank.get()

        def trba(e):
            for m in range(2):
                r = e.transpose(bk[:, 16 * m:16 * m + 16], BA[0:16, 128 * m:128 * m + 128], CN[0:16, 0:16])
            return r
        m = P(trba, lin_tok["ba"], fr)
        k = V(lambda e: e.tensor_copy(BA_T, bk[:, 0:32]), m, mla_done)
        mbank.release(bi, k)
        bat = BA_T.rearrange("p (m h) -> p m h", m=2)
        a1 = A(lambda e: e.activation(m28(BETA), bat[:, :, 0:8], ACT.Sigmoid), k)
        beta_tok = a1
        k = V(lambda e: e.tensor_tensor(m28(SPX), bat[:, :, 8:16], col("dt_bias", 0, 8).unsqueeze(1).broadcast_to([128, 2, 8]), add), k)
        k2 = V(lambda e: e.scalar_tensor_tensor(SPE, SPX, -1.0, SPX, mult, ALU.max), k)
        a = A(lambda e: e.activation(SPE, SPE, ACT.Exp, scale=-1.0), k2)
        a = A(lambda e: e.activation(SPE, SPE, ACT.Ln, bias=1.0), a)
        a2 = A(lambda e: e.activation(EA, col("A_log", 0, 8), ACT.Exp), a)
        k = V(lambda e: e.scalar_tensor_tensor(SPX, SPX, 0.0, SPE, ALU.max, add), a)
        g_tok = V(lambda e: e.scalar_tensor_tensor(m28(GG), m28(SPX), -1.0, EA.unsqueeze(1).broadcast_to([128, 2, 8]), mult, mult), k, a2)
        bi, bk, fr = mbank.get()

        def cums(e):
            e.matmul(bk[:, 0:16], cn("tri"), GG, start=True, stop=True)
            return e.matmul(bk[:, 16:32], cn("ch"), GG, start=True, stop=True)
        m = P(cums, g_tok, fr)
        k = V(lambda e: e.tensor_copy(GC, bk[:, 0:16]), m)
        k = V(lambda e: e.tensor_copy(GL, bk[:, 16:32]), k)
        mbank.release(bi, k)
        v = V(lambda e: e.tensor_tensor(DK, GL, GC, sub), k)
        a = A(lambda e: e.activation(DK, DK, ACT.Exp), v)
        a = A(lambda e: e.activation(BG, GC, ACT.Exp), a)
        sc_tok = V(lambda e: e.tensor_tensor(BG, BG, BETA, mult), a, beta_tok)
        pump(2)

        for half in range(2):
            for h in range(8):
                src = B1[:, 8 * half + h, :]
                i, t, fr = tv.get()
                g = G(lambda e, src=src, t=t: e.tensor_tensor(t, src, src, mult), qkv_tok[8 * half + h], fr)
                bi, bk, fb = mbank.get()
                m = P(lambda e, bk=bk, t=t: e.matmul(bk[:, 0:256], cn("ones"), t, start=True, stop=True), g, fb)
                j, y, fy = te.get()
                r = rsqrt(y, t, bk[:, 0:256], 1.0, 1e-6, m, fy)
                mbank.release(bi, r)
                if half == 0:
                    v = V(lambda e, src=src, y=y: e.scalar_tensor_tensor(src, src, 128.0 ** -0.5, y, mult, mult), r)
                else:
                    v = V(lambda e, src=src, y=y: e.tensor_tensor(src, src, y, mult), r)
                tv.release(i, r)
                te.release(j, v)
                qkv_tok[8 * half + h] = v
                pump(1)

        TMP = [X[:, 2 * i:2 * i + 2, :].rearrange("p a t -> p (a t)") for i in range(8)] + \
              [B3[:, 6:8, :].rearrange("p a t -> p (a t)"), B3[:, 0:2, :].rearrange("p a t -> p (a t)"),
               B3[:, 2:4, :].rearrange("p a t -> p (a t)")]
        KBG, KDEC, VB, AT, LT, CT, MM_, MT, EG, QG, UU = TMP
        SS = B2[:, 16:18, :].rearrange("p a t -> p (a t)")
        DD = B2[:, 18:20, :].rearrange("p a t -> p (a t)")
        x_free = now()

        def h4(x):
            return x.rearrange("p (h n) -> p h n", h=4)

        def mask4(name, a=0, b=128):
            return cn(name, a, b).unsqueeze(1).broadcast_to([128, 4, 128])

        def colb(x, hg, m):
            return x[:, 8 * m + 4 * hg:8 * m + 4 * hg + 4].unsqueeze(2).broadcast_to([128, 4, 128])

        def mm4(fn, *waits):
            bi, bk, fr = mbank.get()

            def go(e):
                for h in range(4):
                    r = fn(e, h, bk[:, 128 * h:128 * h + 128])
                return r
            return bi, bk, P(go, fr, *waits)

        o_tok = [None] * 8
        prev = x_free
        for hg in range(2):
            s_tok = V(lambda e: e.memset(SS, 0.0), prev)
            for mt in range(2):
                hs = [4 * hg + h for h in range(4)]
                tt = slice(128 * mt, 128 * mt + 128)
                qk = [qkv_tok[h] for h in hs] + [qkv_tok[8 + h] for h in hs]
                v = V(lambda e, hg=hg, mt=mt: e.tensor_tensor(h4(EG), mask4("tri"), colb(GG, hg, mt), mult), prev, sc_tok)
                bi, bk, fr = mbank.get()
                m = P(lambda e, bk=bk: e.matmul(bk[:, :], cn("ones"), EG, start=True, stop=True), v, fr)
                v2 = V(lambda e, hg=hg, mt=mt: e.tensor_tensor(h4(CT), mask4("ident"), colb(BETA, hg, mt), mult), v)
                b2, bk2, fr2 = mbank.get()
                m2 = P(lambda e, bk2=bk2: e.matmul(bk2[:, :], cn("ones"), CT, start=True, stop=True), v2, fr2)
                v = V(lambda e, bk=bk, hg=hg, mt=mt: e.tensor_tensor(h4(DD), h4(bk[:, :]), colb(GC, hg, mt), sub), m)
                v = V(lambda e: e.tensor_scalar(DD, DD, 0.0, None, ALU.min), v)
                a = A(lambda e, bk=bk: e.activation(EG, bk[:, :], ACT.Exp), m, v)
                eg_tok = a
                mbank.release(bi, a)
                a = A(lambda e: e.activation(DD, DD, ACT.Exp), v)
                dm = V(lambda e: e.tensor_tensor(h4(DD), h4(DD), mask4("tri"), mult), a)
                pump(1)
                b3, bk3, m3 = mm4(lambda e, h, o, hs=hs, tt=tt: e.matmul(o, B1[:, 8 + hs[h], tt], B1[:, hs[h], tt], start=True, stop=True), qk)
                at_tok = V(lambda e, bk3=bk3: e.tensor_tensor(AT, bk3[:, :], DD, mult), m3, dm)
                mbank.release(b3, at_tok)
                b3, bk3, m3 = mm4(lambda e, h, o, hs=hs, tt=tt: e.matmul(o, B1[:, 8 + hs[h], tt], B1[:, 8 + hs[h], tt], start=True, stop=True), qk)
                v = V(lambda e, bk3=bk3: e.tensor_tensor(LT, bk3[:, :], DD, mult), m3, dm)
                mbank.release(b3, v)
                lt_tok = V(lambda e, bk2=bk2: e.tensor_tensor(LT, bk2[:, :], LT, mult), v, m2)
                mbank.release(b2, lt_tok)
                b3, bk3, m3 = mm4(lambda e, h, o, hs=hs, tt=tt: e.transpose(o, B1[:, 8 + hs[h], tt], cn("ident")), qk)
                kbg_tok = V(lambda e, bk3=bk3, hg=hg, mt=mt: e.tensor_tensor(h4(KBG), h4(bk3[:, :]), colb(BG, hg, mt), mult), m3)
                kd_tok = V(lambda e, bk3=bk3, hg=hg, mt=mt: e.tensor_tensor(h4(KDEC), h4(bk3[:, :]), colb(DK, hg, mt), mult), m3)
                mbank.release(b3, kd_tok)
                b3, bk3, m3 = mm4(lambda e, h, o, hs=hs, tt=tt: e.transpose(o, B1[:, 16 + hs[h], tt], cn("ident")), [qkv_tok[16 + h] for h in hs])
                vb_tok = V(lambda e, bk3=bk3, hg=hg, mt=mt: e.tensor_tensor(h4(VB), h4(bk3[:, :]), colb(BETA, hg, mt), mult), m3)
                mbank.release(b3, vb_tok)
                qg_tok = V(lambda e, hg=hg, tt=tt: e.tensor_tensor(h4(QG), B1[:, 4 * hg:4 * hg + 4, tt], h4(EG), mult), eg_tok, qk)
                pump(1)
                v = V(lambda e: e.tensor_tensor(h4(CT), h4(LT), mask4("lm"), mult), lt_tok, m2)
                mt_tok = V(lambda e: e.tensor_tensor(h4(MT), mask4("ident"), h4(CT), sub), v)
                b3, bk3, m3 = mm4(lambda e, h, o: e.transpose(o, MT[:, 128 * h:128 * h + 128], cn("ident")), mt_tok)
                mm_tok = A(lambda e, bk3=bk3: e.activation(MM_, bk3[:, :], ACT.Copy), m3, prev)
                mbank.release(b3, mm_tok)
                for lv in range(1, 6):
                    ct = V(lambda e, lv=lv: e.tensor_tensor(h4(CT), h4(LT), mask4("lm", 128 * lv, 128 * lv + 128), mult), mt_tok, mm_tok)
                    b3, bk3, m3 = mm4(lambda e, h, o: e.matmul(o, CT[:, 128 * h:128 * h + 128], MM_[:, 128 * h:128 * h + 128], start=True, stop=True), ct, mm_tok)
                    u_tok = A(lambda e, bk3=bk3: e.activation(UU, bk3[:, :], ACT.Copy), m3, mt_tok)
                    mbank.release(b3, u_tok)
                    pump(1)
                    b4, bk4, m4 = mm4(lambda e, h, o: e.matmul(o, UU[:, 128 * h:128 * h + 128], MT[:, 128 * h:128 * h + 128], start=True, stop=True), u_tok, mt_tok)
                    if lv < 5:
                        b5, bk5, m5 = mm4(lambda e, h, o: e.matmul(o, MT[:, 128 * h:128 * h + 128], UU[:, 128 * h:128 * h + 128], start=True, stop=True), u_tok, mt_tok)
                        mm_tok = V(lambda e, bk5=bk5: e.tensor_tensor(MM_, MM_, bk5[:, :], sub), m5)
                        mbank.release(b5, mm_tok)
                        mt_tok = V(lambda e, bk4=bk4: e.tensor_tensor(MT, MT, bk4[:, :], sub), m4, m5)
                    else:
                        mt_tok = V(lambda e, bk4=bk4: e.tensor_tensor(MT, MT, bk4[:, :], sub), m4)
                    mbank.release(b4, mt_tok)
                b3, bk3, m3 = mm4(lambda e, h, o: e.matmul(o, MT[:, 128 * h:128 * h + 128], VB[:, 128 * h:128 * h + 128], start=True, stop=True), mt_tok, vb_tok)
                u_tok = A(lambda e, bk3=bk3: e.activation(UU, bk3[:, :], ACT.Copy), m3, m4)
                mbank.release(b3, u_tok)
                b3, bk3, m3 = mm4(lambda e, h, o: e.matmul(o, KBG[:, 128 * h:128 * h + 128], MT[:, 128 * h:128 * h + 128], start=True, stop=True), mt_tok, kbg_tok)
                w_tok = A(lambda e, bk3=bk3: e.activation(MM_, bk3[:, :], ACT.Copy), m3)
                mbank.release(b3, w_tok)
                pump(1)
                for cc in range(2):
                    r0 = 64 * cc
                    rr = slice(r0, r0 + 64)
                    b3, bk3, m3 = mm4(lambda e, h, o, rr=rr, hg=hg: e.matmul(o[rr, :], MM_[:, 128 * h + rr.start:128 * h + rr.stop], SS[:, 128 * h:128 * h + 128], start=True, stop=True),
                                      w_tok, s_tok)
                    vn = V(lambda e, bk3=bk3, rr=rr: e.tensor_tensor(UU[rr, :], UU[rr, :], bk3[rr, :], sub), m3, u_tok)
                    mbank.release(b3, vn)
                    pump(1)
                    bi, bk, fr = mbank.get()

                    def sup(e, bk=bk, rr=rr):
                        for h in range(4):
                            r = e.matmul(bk[:, 128 * h:128 * h + 128], KDEC[rr, 128 * h:128 * h + 128], UU[rr, 128 * h:128 * h + 128], start=True, stop=True)
                        return r
                    ms = P(sup, vn, kd_tok, fr)
                    b5, bk5, fr5 = mbank.get()

                    def om(e, bk5=bk5, rr=rr, hg=hg):
                        for h in range(4):
                            o = bk5[:, 64 * h:64 * h + 64]
                            e.matmul(o, SS[:, 128 * h:128 * h + 128], QG[:, 128 * h + rr.start:128 * h + rr.stop], start=True, stop=False)
                            r = e.matmul(o, UU[rr, 128 * h:128 * h + 128], AT[rr, 128 * h + rr.start:128 * h + rr.stop], start=False, stop=True)
                        return r
                    mo = P(om, vn, qg_tok, at_tok, s_tok, fr5)
                    ts = slice(128 * mt + r0, 128 * mt + r0 + 64)
                    oe = A(lambda e, bk5=bk5, ts=ts, hg=hg: e.activation(B1[:, 4 * hg:4 * hg + 4, ts], bk5[:, 0:256].rearrange("p (h n) -> p h n", h=4), ACT.Copy), mo, qg_tok)
                    mbank.release(b5, oe)
                    for h in range(4):
                        s_tok = V(lambda e, h=h, bk=bk, hg=hg, r0=r0: e.scalar_tensor_tensor(
                            SS[:, 128 * h:128 * h + 128], SS[:, 128 * h:128 * h + 128],
                            EG[:, 128 * h + r0 + 63:128 * h + r0 + 64], bk[:, 128 * h:128 * h + 128], mult, add), ms, mo)
                    mbank.release(bi, s_tok)
                    pump(1)
                for h in hs:
                    o_tok[h] = oe
                prev = now()
        x_free2 = now()
        for i in range(4):
            tk_x2 = D("x2", 16 * i + 16, lambda e, i=i: e.dma_start(X[:, 4 * i:4 * i + 4, :], xT[:, 4 * i:4 * i + 4, :]), x_free2)
        run(fill)
        rounds_done = x_free2
        run(filler_z())
        flush(True)
        gdn_tok = [None] * 8
        for h in range(8):
            i, t, fr = tv.get()
            o = B1[:, h, :]
            g = G(lambda e, o=o, t=t: e.tensor_tensor(t, o, o, mult), o_tok[h], fr)
            bi, bk, fb = mbank.get()
            m = P(lambda e, bk=bk, t=t: e.matmul(bk[:, 0:256], cn("ones"), t, start=True, stop=True), g, fb)
            j, y, fy = te.get()
            r = rsqrt(y, t, bk[:, 0:256], 1.0 / 128, 1e-6, m, fy)
            mbank.release(bi, r)
            v = V(lambda e, o=o, y=y: e.scalar_tensor_tensor(o, o, col("gdn_norm"), y, mult, mult), r)
            v = V(lambda e, o=o, h=h: e.tensor_tensor(o, o, Z[h], mult), v, z_tok[h])
            tv.release(i, r)
            te.release(j, v)
            gdn_tok[h] = split(H2, h, o, v, cq_done)

        mix_tok = [None] * 16

        def ev_gb(j):
            def f(bk, tok, bi):
                i, t, fr = tv.get()
                k = raw_sum(t, bk, tok, bi, fr)
                lin_tok[("gb", j)] = (i, t, A(lambda e: e.activation(t, t, ACT.Sigmoid), k))
            return f

        def ev_yb(j):
            def f(bk, tok, bi):
                i, t, fr = tv.get()
                k = raw_sum(t, bk, tok, bi, fr)
                gi, g, gk = lin_tok[("gb", j)]
                v = V(lambda e: e.tensor_tensor(t, t, g, mult), k, gk)
                tv.release(gi, v)
                v = V(lambda e: e.tensor_tensor(t, t, YA[j], add), v, ya_tok[j])
                lin_tok[("mix", j)] = (i, t, v)
                mixf(j)
            return f
        B1_free = None

        def mixf(j):
            i, t, v = lin_tok[("mix", j)]
            w = V(lambda e: e.tensor_copy(YA[j], t), v)
            tv.release(i, w)
            mix_tok[j] = w

        for j in range(16):
            run(block(H1, h_tok, 0, "w_in", 0, 58 + j, ev_gb(j)))
            run(block(H2, gdn_tok, 0, "w_o_gdn", 0, j, ev_yb(j)))
        flush(True)
        h1_free = now()
        m_tok = [split(H1, j, YA[j], mix_tok[j], h1_free) for j in range(16)]

        x_tok = [None] * 16
        S = Stats(Sp.done)

        def ev_res(gate, S, extra):
            def mk(j):
                def f(bk, tok, bi):
                    i, t, fr = tv.get()
                    k = raw_sum(t, bk, tok, bi, fr)
                    x_tok[j] = V(lambda e: e.scalar_tensor_tensor(X[:, j, :], t, MOD[:, 16 * gate + j:16 * gate + j + 1], X[:, j, :], mult, add),
                                 k, extra, mod_tok[2 * gate + j // 8], x_tok[j])
                    tv.release(i, x_tok[j])
                    if S is not None:
                        S.square(X[:, j, :], x_tok[j])
                return f
            return mk
        ev = ev_res(2, S, tk_x2)
        for j in range(16):
            run(block(H1, m_tok, 0, "w_o", 0, j, ev(j)))
        flush(True)
        rs_tok = S.finish(2048, 1e-6)
        Sp = S
        h_tok = adaln(3, 4, "norm_ffn", rs_tok, x_tok, now())

        def ffn(cuts, up, down_name, ev_down, KD):
            at = 0
            for ci, n in enumerate(cuts):
                f_tok = [None] * n
                for s in range(n):
                    run(up(at + s, s, f_tok))
                flush(True)
                for j in range(16):
                    run(block(H2, f_tok, 0, down_name, at, j, ev_down(ci, j)))
                at += n
            flush(True)

        G_ = {}

        def up1(i, s, f_tok):
            def e1(bk, tok, bi):
                q, t, fr = tv.get()
                k = raw_sum(t, bk, tok, bi, fr)
                G_[i] = (q, t, silu_to(t, t, k))

            def e2(bk, tok, bi):
                q, t, fr = tv.get()
                k = raw_sum(t, bk, tok, bi, fr)
                gq, g, gk = G_.pop(i)
                v = V(lambda e: e.tensor_tensor(t, t, g, mult), k, gk)
                tv.release(gq, v)
                f_tok[s] = split(H2, s, t, v, h2_free[0])
                tv.release(q, f_tok[s])
            yield from block(H1, h_tok, 0, "w_gate_up", 0, i, e1)
            yield from block(H1, h_tok, 0, "w_gate_up", 0, 44 + i, e2)

        h2_free = [now()]
        S = Stats(Sp.done)

        def evd(ci, j):
            if j == 0:
                h2_free[0] = now()
            f = ev_res(5, S if ci == 2 else None, None)(j)

            def go(bk, tok, bi):
                if ci < 2 and j == 15:
                    h2_free[0] = [tok]
                f(bk, tok, bi)
            return go
        ffn((15, 15, 14), up1, "w_down", evd, 44)
        rs_tok = S.finish(2048, 1e-6)
        Sp = S

        S = Stats(Sp.done)
        fin = now()
        for j in range(16):
            x_tok[j] = V(lambda e, j=j: e.scalar_tensor_tensor(X[:, j, :], X[:, j, :], col("final_norm", j), RS[:, 0, :], mult, mult), rs_tok, fin)
            S.square(X[:, j, :], x_tok[j])
        rs_tok = S.finish(2048, 1e-6, x_tok[15])
        Sp = S

        def norm_h1(name, rs_tok, *waits):
            out = []
            for j in range(16):
                i, t, fr = tv.get()
                k = V(lambda e, j=j, t=t: e.scalar_tensor_tensor(t, X[:, j, :], col(name, j), RS[:, 0, :], mult, mult), rs_tok, x_tok[j], fr)
                k = split(H1, j, t, k, *waits)
                tv.release(i, k)
                out.append(k)
            return out
        h_tok = norm_h1("pre_mix", rs_tok, now())

        b2_free = now()
        UP = B1[:, 0:9, :].rearrange("p a t -> p (a t)")[:, 0:8 * 286].rearrange("p (j n) -> p j n", j=8)
        pad_tok = V(lambda e: e.memset(UP, 0.0), b2_free)
        CA = [B1[:, 9 + j, :] for j in range(8)]
        Q2 = [B2[:, i, :] for i in range(8)]
        K2 = [B2[:, 8 + i, :] for i in range(8)]
        VT2 = B2[:, 16:24, :].rearrange("p a t -> p (a t)").rearrange("p (m n) -> p m n", m=2)
        BB = [B1[:, 17 + i, :] for i in range(4)]
        u_tok = [None] * 8

        def e_a(j):
            def f(bk, tok, bi):
                lin_tok[("a2", j)] = raw_sum(UP[:, j, 15:271], bk, tok, bi, pad_tok)
            return f

        def e_g(j):
            def f(bk, tok, bi):
                i, t, fr = tv.get()
                k = raw_sum(t, bk, tok, bi, fr)
                a = A(lambda e: e.activation(t, t, ACT.Sigmoid), k)
                u_tok[j] = V(lambda e: e.tensor_tensor(UP[:, j, 15:271], UP[:, j, 15:271], t, mult), a, lin_tok[("a2", j)])
                tv.release(i, u_tok[j])
            return f
        for j in range(8):
            run(block(H1, h_tok, 0, "w_in2", 0, j, e_a(j)))
            run(block(H1, h_tok, 0, "w_in2", 0, 8 + j, e_g(j)))

        conv_tok = [None] * 8

        def conv_gen():
            while u_tok[7] is None:
                yield
            for j in range(8):
                o = COLS["w_dw"][0] + 31 * j
                k = V(lambda e, j=j, o=o: e.tensor_scalar(CA[j], UP[:, j, 0:256], CO[:, o:o + 1], col("b_dw", j), mult, add), u_tok[j], b2_free)
                for i in range(1, 31):
                    k = V(lambda e, i=i, j=j, o=o: e.scalar_tensor_tensor(CA[j], UP[:, j, i:i + 256], CO[:, o + i:o + i + 1], CA[j], mult, add), k)
                    if i % 6 == 0:
                        yield
                conv_tok[j] = k
                yield

        cg = conv_gen()
        q2_tok, k2_tok, v2_tok = [None] * 8, [None] * 8, [None] * 8

        def e_p(lst, toks, j):
            def f(bk, tok, bi):
                toks[j] = raw_sum(lst[j], bk, tok, bi, b2_free)
            return f

        def e_v2(j):
            def f(bk, tok, bi):
                i, t, fr = tv.get()
                k = raw_sum(t, bk, tok, bi, fr)
                mi, mk, mf = mbank.get()

                def tr(e):
                    for m in range(2):
                        r = e.transpose(mk[:, 128 * m:128 * m + 128], t[:, 128 * m:128 * m + 128], cn("ident"))
                    return r
                m = P(tr, k, mf)
                tv.release(i, m)
                v2_tok[j] = A(lambda e: e.activation(VT2[:, :, 128 * j:128 * j + 128], mk[:, 0:256].rearrange("p (m n) -> p m n", m=2), ACT.Copy), m, b2_free)
                mbank.release(mi, v2_tok[j])
            return f
        for j in range(8):
            for _ in block(H1, h_tok, 0, "w_in2", 0, 16 + j, e_p(Q2, q2_tok, j)):
                next(cg, None)
        for j in range(8):
            for _ in block(H1, h_tok, 0, "w_in2", 0, 24 + j, e_p(K2, k2_tok, j)):
                next(cg, None)
        for j in range(8):
            for _ in block(H1, h_tok, 0, "w_in2", 0, 32 + j, e_v2(j)):
                next(cg, None)
        flush(True)
        for _ in cg:
            pass

        cat_tok = [None] * 16
        bi, bk, fr = mbank.get()
        S = Stats(Sp.done)
        for j in range(8):
            S.square(CA[j], conv_tok[j])

        def sums(e):
            for j in range(8):
                r = e.matmul(bk[:, 0:256], cn("ones"), CA[j], start=(j == 0), stop=(j == 7))
            return r
        m = P(sums, conv_tok[7], fr)
        k = V(lambda e: e.tensor_scalar(RS[:, 2, :], bk[:, 0:256], 1.0 / 1024, None, mult), m)
        mbank.release(bi, k)
        S = Stats(S.last[0])
        for j in range(8):
            conv_tok[j] = V(lambda e, j=j: e.tensor_tensor(CA[j], CA[j], RS[:, 2, :], sub), k, m, S.last)
        S = Stats(S.last[0])
        for j in range(8):
            S.square(CA[j], conv_tok[j])
        r = S.finish(1024, 1e-5)
        Sp = S

        def ln_gen():
            for j in range(8):
                i, t, fr = tv.get()
                v = V(lambda e, j=j, t=t: e.scalar_tensor_tensor(t, CA[j], col("ln_g", j), RS[:, 0, :], mult, mult), r, fr)
                v = V(lambda e, j=j, t=t: e.tensor_scalar(t, t, col("ln_b", j), None, add), v)
                q, y, fy = te.get()
                a = A(lambda e, y=y, t=t: e.activation(y, t, ACT.Sigmoid), v, fy)
                v = V(lambda e, y=y, t=t: e.tensor_tensor(t, t, y, mult), a)
                te.release(q, v)
                cat_tok[j] = split(H2, j, t, v, b2_free)
                tv.release(i, cat_tok[j])
                yield

        run(ln_gen())
        b_use = [b2_free] * 4
        bm_tok = {}

        def load_bias(i):
            s = i % 4
            d = D(f"b{s}", 16 * (i // 4 + 1), lambda e: e.dma_start(BB[s], bias_d[i]), b_use[s])
            bm_tok[i] = G(lambda e: e.tensor_tensor(BB[s], BB[s], cn("nm"), add), d)

        for i in range(3):
            load_bias(i)

        def na_scores(i, bk, fr):
            h, qb = divmod(i, 2)
            o = 64 * (h % 2)
            return P(lambda e: e.matmul(bk[:, 0:256], Q2[h // 2][o:o + 64, 128 * qb:128 * qb + 128], K2[h // 2][o:o + 64, :], start=True, stop=True),
                     q2_tok[h // 2], k2_tok[h // 2], fr)

        def na_mask(i, p, ps, m, pf):
            s = i % 4
            v = V(lambda e: e.scalar_tensor_tensor(p, ps, 0.125, BB[s], mult, add), m, pf, bm_tok[i])
            b_use[s] = [v]
            if i + 3 < 32:
                load_bias(i + 3)
            return v

        def na_pv(i, t, a):
            h, qb = divmod(i, 2)
            o = 64 * (h % 2)
            if i % 4 == 0:
                av["b"] = mbank.get()
            bi, bk, fr = av["b"]

            def mm(e):
                for q in range(2):
                    r = e.matmul(bk[o:o + 64, 128 * qb:128 * qb + 128], VT2[:, q, 64 * h:64 * h + 64], t[:, 128 * q:128 * q + 128],
                                 start=(q == 0), stop=(q == 1))
                return r
            m = P(mm, a, v2_tok[h // 2], fr if i % 4 == 0 else None)
            if i % 4 == 3:
                j = 8 + h // 2
                x = A(lambda e: e.activation(H2[:, j, 0:256], bk[:, 0:256], ACT.Copy), m, b2_free)
                cat_tok[j] = V(lambda e: e.tensor_tensor(H2[:, j, 256:512], bk[:, 0:256], H2[:, j, 0:256].bitcast(f32), sub), x)
                mbank.release(bi, cat_tok[j])
            return m

        mst.clear()
        pr.free = [b2_free for _ in pr.items]
        ptr.items = [B1[:, 21, :], B1[:, 22, :]]
        ptr.free = [b2_free for _ in ptr.items]
        pipeline(32, softmax_stages(32, na_scores, na_mask, 0.125, lambda i: 256, na_pv), lambda s: None)

        Y = [B2[:, i, :] for i in range(16)]
        y_free = now()
        y_tok = [None] * 16
        S = Stats(Sp.done)

        def ev_y(ci, j, last):
            def f(bk, tok, bi):
                if ci == 0:
                    y_tok[j] = raw_sum(Y[j], bk, tok, bi, y_free)
                else:
                    i, t, fr = tv.get()
                    k = raw_sum(t, bk, tok, bi, fr)
                    y_tok[j] = V(lambda e: e.tensor_tensor(Y[j], Y[j], t, add), k, y_tok[j])
                    tv.release(i, y_tok[j])
                if last:
                    S.square(Y[j], y_tok[j])
            return f
        for j in range(16):
            run(block(H2, cat_tok, 0, "w_out2", 0, j, ev_y(0, j, True)))
        flush(True)
        rs_tok = S.finish(2048, 1e-6, now())
        Sp = S

        def post(name, rs_tok):
            out = []
            for j in range(16):
                k = V(lambda e, j=j: e.scalar_tensor_tensor(Y[j], Y[j], col(name, j), RS[:, 0, :], mult, mult), rs_tok)
                x_tok[j] = V(lambda e, j=j: e.tensor_tensor(X[:, j, :], X[:, j, :], Y[j], add), k, x_tok[j])
                out.append(x_tok[j])
            return out
        post("post_mix", rs_tok)
        S = Stats(Sp.done)
        for j in range(16):
            S.square(X[:, j, :], x_tok[j])
        rs_tok = S.finish(2048, 1e-6, x_tok[15])
        Sp = S
        h_tok = norm_h1("pre_mlp", rs_tok, now())

        y_free = now()
        h2_free = [now()]
        S = Stats(Sp.done)

        def up2(i, s, f_tok):
            def e1(bk, tok, bi):
                q, t, fr = tv.get()
                k = raw_sum(t, bk, tok, bi, fr)
                v = V(lambda e: e.tensor_scalar(t, t, 0.0, None, ALU.max), k)
                v = V(lambda e: e.tensor_tensor(t, t, t, mult), v)
                f_tok[s] = split(H2, s, t, v, h2_free[0])
                tv.release(q, f_tok[s])
            yield from block(H1, h_tok, 0, "w_up2", 0, i, e1)

        def evd2(ci, j):
            f = ev_y(ci, j, ci == 3)

            def go(bk, tok, bi):
                if j == 15:
                    h2_free[0] = [tok]
                f(bk, tok, bi)
            return go

        def fix_flush():
            flush(True)
        ffn((16, 16, 16, 16), up2, "w_down2", evd2, 64)
        rs_tok = S.finish(2048, 1e-6, now())
        toks = post("post_mlp", rs_tok)
        for i in range(4):
            tk = D("out", 16 * i + 16, lambda e, i=i: e.dma_start(out[:, 4 * i:4 * i + 4, :], X[:, 4 * i:4 * i + 4, :]), toks[4 * i + 3])
        assert st["tile"] == N_TILES, st
        while st["proc"] < len(kinds):
            proc_next()

        block_ = ctx.enter_context(nc.Block())

        def play(name, e):
            seen = {}
            for fn, waits, inc in queue[name]:
                need = {}
                for s, v in waits:
                    need[s] = max(need.get(s, 0), v)
                for s, v in need.items():
                    if seen.get(s, 0) < v:
                        e.wait_ge(sems[s], v)
                        seen[s] = v
                r = fn(e)
                if inc is None:
                    r.then_inc(sems[name], 1)
                else:
                    r.then_inc(sems[inc], 16)

        @block_.sync
        def _(e):
            play("sp", e)
            e.wait_ge(sems["out"], 64)

        @block_.scalar
        def _(e):
            play("act", e)

        @block_.vector
        def _(e):
            play("dve", e)

        @block_.gpsimd
        def _(e):
            play("pool", e)

        @block_.tensor
        def _(e):
            play("pe", e)


def kernel(**inp):
    import concourse.bacc as _bacc
    from concourse import mybir as mb
    from concourse.bass_utils import run_bass_kernel_spmd as _run
    I = {k: np.asarray(v) for k, v in inp.items()}

    def feat(v):
        return v.reshape(-1, 128).T
    w_in = I["w_in"][0]
    kpe = w_in[:, 1024:1088]
    ba = w_in[:, 5184:5200]
    pad = np.zeros((2048, 112), np.float32)
    W = {"w_in": np.concatenate([w_in[:, 0:1024], kpe, kpe, w_in[:, 1088:5184], ba, pad, w_in[:, 5200:9296]], axis=1)}
    uq = I["w_uq"][0].reshape(512, 8, 192)
    W["w_uq"] = np.concatenate([uq[:, :, 0:128].reshape(512, 1024), uq[:, :, 128:192].reshape(512, 512)], axis=1)
    ukv = I["w_ukv"][0].reshape(512, 8, 256)
    W["w_ukv"] = np.concatenate([ukv[:, :, 0:128].reshape(512, 1024), ukv[:, :, 128:256].reshape(512, 1024)], axis=1)
    for a, b in (("w_o_mla", "w_o_mla"), ("w_o_gdn", "w_o_gdn"), ("w_o", "w_o"), ("w_gate_up", "w_gate_up"), ("w_down", "w_down"),
                 ("w_in2", "w_in_2"), ("w_out2", "w_out_2"), ("w_up2", "w_up_2"), ("w_down2", "w_down_2")):
        W[a] = I[b][0]
    cols = np.zeros((128, NCOLS), np.float32)

    def put(name, v):
        o, w = COLS[name]
        cols[:, o:o + w] = v
    put("c", feat(I["c"][0]))
    put("b_ada", feat(I["b_ada"][0]))
    put("norm_mix", feat(I["norm_mix"][0]))
    put("norm_ffn", feat(I["norm_ffn"][0]))
    put("q_a_norm", feat(I["q_a_norm"][0]))
    put("kv_a_norm", feat(I["kv_a_norm"][0]))
    put("conv_w", I["conv_w"][0].reshape(4, 24, 128).transpose(2, 1, 0).reshape(128, 96))
    put("gdn_norm", I["gdn_norm"][0][:, None])
    put("final_norm", feat(I["final_norm"]))
    put("pre_mix", feat(I["pre_mix_g_2"][0]))
    put("post_mix", feat(I["post_mix_g_2"][0]))
    put("pre_mlp", feat(I["pre_mlp_g_2"][0]))
    put("post_mlp", feat(I["post_mlp_g_2"][0]))
    put("w_dw", I["w_dw_2"][0].reshape(31, 8, 128).transpose(2, 1, 0).reshape(128, 248))
    put("b_dw", feat(I["b_dw_2"][0]))
    put("ln_g", feat(I["conv_ln_g_2"][0]))
    put("ln_b", feat(I["conv_ln_b_2"][0]))
    put("A_log", np.broadcast_to(I["A_log"][0][None, :], (128, 8)))
    put("dt_bias", np.broadcast_to(I["dt_bias"][0][None, :], (128, 8)))
    wada = np.ascontiguousarray(I["w_ada"][0].reshape(16, 128, 12, 1024).transpose(2, 0, 1, 3)).reshape(N_ADA, 128, 1024)
    r = np.arange(4)
    c = np.arange(64)
    dr = r[None, :] - r[:, None] + 7
    dc = np.clip(c[None, :] - c[:, None], -15, 15) + 15
    bias = I["rpb_2"][0][:, dr[:, None, :, None], dc[None, :, None, :]].reshape(32, 128, 256)

    arrays = {
        "xT": np.ascontiguousarray(I["x"][0].T.reshape(16, 128, 256).transpose(1, 0, 2)),
        "pos": I["positions"][0], "cols": cols, "consts": const_array(), "wada": wada, "bias": np.ascontiguousarray(bias),
    }
    nc = _bacc.Bacc("TRN2", target_bir_lowering=False, num_devices=1)
    aps = {n: nc.dram_tensor(n + "_dram", a.shape, mb.dt.from_np(a.dtype), kind="ExternalInput").ap() for n, a in arrays.items()}
    wst = nc.dram_tensor("wst_dram", (N_TILES // 8, 128, 1024), mb.dt.float32, kind="ExternalInput").ap()
    out = nc.dram_tensor("out_dram", (128, 16, 256), mb.dt.float32, kind="ExternalOutput").ap()
    log = []
    program(nc, aps["xT"], aps["pos"], aps["cols"], aps["consts"], aps["wada"], wst, aps["bias"], out, log)
    ws = np.empty((N_TILES // 8, 128, 1024), np.float32)
    for i, (name, k, n) in enumerate(log):
        ws[i // 8, :, 128 * (i % 8):128 * (i % 8) + 128] = W[name][128 * k:128 * k + 128, 128 * n:128 * n + 128]
    ins = {n + "_dram": a for n, a in arrays.items()}
    ins["wst_dram"] = ws
    res = _run(nc, [ins], core_ids=[0])
    o = res.results[0]["out_dram"]
    return np.ascontiguousarray(o.transpose(1, 0, 2).reshape(2048, 256).T).reshape(1, 256, 2048)
```

```python
import numpy as np
import concourse.bass as bass
from concourse import mybir
from contextlib import ExitStack

T = 256
NRAW, NHL = 5, 3
N_TILES = 6864
N_ADA = 192
ADA_FIRST = 64
ADA_EVERY = 2

COLS = {}
_n = 0
for _name, _w in (("c", 16), ("b_ada", 96), ("norm_mix", 16), ("norm_ffn", 16), ("q_a_norm", 4), ("kv_a_norm", 4),
                  ("conv_w", 96), ("gdn_norm", 1), ("final_norm", 16), ("pre_mix", 16), ("post_mix", 16),
                  ("pre_mlp", 16), ("post_mlp", 16), ("w_dw", 248), ("b_dw", 8), ("ln_g", 8), ("ln_b", 8),
                  ("A_log", 8), ("dt_bias", 8)):
    COLS[_name] = (_n, _w)
    _n += _w
NCOLS = _n

CONSTS = {}
_n = 0
for _name, _w in (("ident", 128), ("ones", 128), ("tri", 128), ("ch", 128), ("lm", 768), ("mm", 256), ("nm", 256),
                  ("rot", 128), ("invf", 1), ("slide", 15)):
    CONSTS[_name] = (_n, _w)
    _n += _w
NCONST = _n


def const_array():
    a = np.zeros((128, NCONST), np.float32)

    def put(name, v):
        o, w = CONSTS[name]
        a[:, o:o + w] = v
    s = np.arange(128)[:, None]
    c = np.arange(128)[None, :]
    put("ident", s == c)
    put("ones", 1.0)
    same = (s // 64) == (c // 64)
    put("tri", (s <= c) & same)
    put("ch", same)
    put("lm", np.concatenate([((c // k) % 2 == 1) & ((s // k) == (c // k) - 1) for k in (1, 2, 4, 8, 16, 32)], axis=1))
    k = np.arange(256)[None, :]
    put("mm", np.where(k <= 128 + s, 0.0, -1e30))
    start = np.clip(s % 64 - 8, 0, 48)
    put("nm", np.where((k % 64 >= start) & (k % 64 < start + 16), 0.0, -1e30))
    rot = np.zeros((128, 128), np.float32)
    for b in (0, 64):
        for j in range(32):
            rot[b + 32 + j, b + j] = -1.0
            rot[b + j, b + 32 + j] = 1.0
    put("rot", rot)
    put("slide", np.arange(15)[None, :] == 7)
    inv = (np.float32(1.0) / (np.float32(10000.0) ** (np.arange(0, 64, 2, dtype=np.float32) / np.float32(64)))).astype(np.float32)
    put("invf", inv[np.arange(128) % 32][:, None])
    return a


def program(nc, xT, pos, cols_d, consts_d, wada, wst, bias_d, out, log):
    f32 = mybir.dt.float32
    f32r = mybir.dt.float32r
    i32 = mybir.dt.int32
    ALU = mybir.AluOpType
    ACT = mybir.ActivationFunctionType
    AX = mybir.AxisListType.X
    add, sub, mult = ALU.add, ALU.subtract, ALU.mult
    ctx = ExitStack()
    with ctx:
        def sb(name, shape, dt=f32):
            return ctx.enter_context(nc.sbuf_tensor(name, shape, dt))

        RAW = sb("RAW", [128, NRAW, 1024])
        HI = sb("HI", [128, NHL, 1024], f32r)
        LO = sb("LO", [128, NHL, 1024], f32r)
        H1 = sb("H1", [128, 16, 512], f32r)
        H2 = sb("H2", [128, 16, 512], f32r)
        CO = sb("CO", [128, NCOLS])
        CN = sb("CN", [128, NCONST])
        MOD = sb("MOD", [128, 96])
        SC = sb("SC", [128, 256])
        TV = sb("TV", [128, 4, 256])
        TE = sb("TE", [128, 3, 256])
        RS = sb("RS", [128, 3, 256])
        SQ = sb("SQ", [128, 2, 256])
        ADA = sb("ADA", [128, 1024])
        X = sb("X", [128, 16, 256])
        B1 = sb("B1", [128, 24, 256])
        B2 = sb("B2", [128, 24, 256])
        B3 = sb("B3", [128, 8, 256])
        BANK = [ctx.enter_context(nc.psum_tensor(f"BK{i}", [128, 512], f32)) for i in range(8)]

        def sem(name):
            return ctx.enter_context(nc.semaphore(name))

        ENG = ("pe", "act", "dve", "pool", "sp")
        sems = {e: sem("s_" + e) for e in ENG}
        for i in range(NRAW):
            sems[f"r{i}"] = sem(f"s_raw{i}")
        for i in range(4):
            sems[f"b{i}"] = sem(f"s_bias{i}")
        for n in ("cols", "consts", "x", "pos", "x2", "out"):
            sems[n] = sem("s_" + n)
        queue = {e: [] for e in ENG}
        count = {e: 0 for e in ENG}

        def put(e, fn, waits):
            flat = []
            for w in waits:
                flat += w if isinstance(w, list) else [w] if w is not None else []
            queue[e].append((fn, flat, None))
            count[e] += 1
            return (e, count[e])

        def V(fn, *waits):
            return put("dve", fn, waits)

        def A(fn, *waits):
            return put("act", fn, waits)

        def G(fn, *waits):
            return put("pool", fn, waits)

        def P(fn, *waits):
            return put("pe", fn, waits)

        def D(name, value, fn, *waits):
            flat = []
            for w in waits:
                flat += w if isinstance(w, list) else [w] if w is not None else []
            queue["sp"].append((fn, flat, name))
            return (name, value)

        def now():
            return [(e, count[e]) for e in ("pe", "act", "dve", "pool")]

        def col(name, j=0, w=1):
            return CO[:, COLS[name][0] + j:COLS[name][0] + j + w]

        def cn(name, a=0, b=None):
            o, w = CONSTS[name]
            return CN[:, o + a:o + (w if b is None else b)]

        class Ring:
            def __init__(self, items):
                self.items = items
                self.free = [[] for _ in items]
                self.idle = list(range(len(items)))

            def get(self):
                i = self.idle.pop(0)
                return i, self.items[i], self.free[i]

            def release(self, i, *toks):
                self.free[i] = list(toks)
                assert i not in self.idle
                self.idle.append(i)

        tv = Ring([TV[:, i, :] for i in range(4)])
        te = Ring([TE[:, i, :] for i in range(3)])
        lbank = Ring(BANK[0:3])
        mbank = Ring(BANK[3:8])

        tk_cols = D("cols", 16, lambda e: e.dma_start(CO[:, :], cols_d))
        raw_free = [[] for _ in range(NRAW)]
        kinds = ["A"] * ADA_FIRST
        a = ADA_FIRST
        for i in range(N_TILES // 8):
            kinds.append("L")
            if i % ADA_EVERY == ADA_EVERY - 1 and a < N_ADA:
                kinds.append("A")
                a += 1
        lin_at = [i for i, k in enumerate(kinds) if k == "L"]
        st = {"load": 0, "proc": 0, "na": 0, "nl": 0, "la": 0, "ll": 0, "tile": 0}
        split_tok = {}
        unit_pe = {}
        mod_tok = [None] * 12
        ada_last = [None]
        ada_free = [[]]

        def load_next():
            s = st["load"]
            if s >= len(kinds):
                return
            slot = s % NRAW
            if kinds[s] == "A":
                src = wada[st["la"]]
                st["la"] += 1
            else:
                src = wst[st["ll"]]
                st["ll"] += 1
            D(f"r{slot}", 16 * (s // NRAW + 1), lambda e: e.dma_start(RAW[:, slot, :], src), *raw_free[slot])
            st["load"] += 1

        def proc_next():
            s = st["proc"]
            slot = s % NRAW
            got = (f"r{slot}", 16 * (s // NRAW + 1))
            if kinds[s] == "A":
                i = st["na"]
                st["na"] += 1
                j, t = divmod(i, 16)
                if t == 0:
                    k = V(lambda e: e.tensor_scalar(ADA[:, :], RAW[:, slot, :], SC[:, 0:1], None, mult), got, c_tok, ada_free[0])
                else:
                    k = V(lambda e: e.scalar_tensor_tensor(ADA[:, :], RAW[:, slot, :], SC[:, t:t + 1], ADA[:, :], mult, add),
                          got, ada_last[0])
                ada_last[0] = k
                raw_free[slot] = [k]
                if t == 15:
                    bi, bk, fr = mbank.get()

                    def mm(e):
                        for q in range(8):
                            r = e.matmul(bk[:, q:q + 1], ADA[:, q * 128:q * 128 + 128], cn("ones", 0, 1), start=True, stop=True)
                        return r
                    m = P(mm, k, fr, tk_consts)
                    ada_free[0] = [m]
                    ev = V(lambda e: e.tensor_tensor(MOD[:, 8 * j:8 * j + 8], bk[:, 0:8], col("b_ada", 8 * j, 8), add), m, tk_cols)
                    mbank.release(bi, ev)
                    mod_tok[j] = ev
            else:
                u = st["nl"]
                st["nl"] += 1
                h = u % NHL
                old = unit_pe.get(u - NHL)
                k1 = A(lambda e: e.activation(HI[:, h, :], RAW[:, slot, :], ACT.Copy), got, old)
                k2 = V(lambda e: e.tensor_tensor(LO[:, h, :], RAW[:, slot, :], HI[:, h, :].bitcast(f32), sub), k1, old)
                split_tok[u] = k2
                raw_free[slot] = [k2]
            st["proc"] += 1
            load_next()

        def feed(u):
            goal = lin_at[min(u, len(lin_at) - 1)]
            while st["proc"] <= goal:
                proc_next()

        pending = []

        def flush(force=False):
            while pending and (force or pending[0][0] <= st["tile"]):
                pending.pop(0)[1]()

        def block(H, toks, k0, wname, kbase, n, evac):
            while not lbank.idle:
                pending.pop(0)[1]()
            bi, bk, fr = lbank.get()
            K = len(toks)
            for k in range(K):
                t = st["tile"]
                st["tile"] += 1
                log.append((wname, kbase + k, n))
                u, q = divmod(t, 8)
                if q == 0:
                    feed(u)

                def mm(e, k=k, u=u, q=q):
                    hh = HI[:, u % NHL, q * 128:q * 128 + 128]
                    ll = LO[:, u % NHL, q * 128:q * 128 + 128]
                    e.matmul(bk[:, :], hh, H[:, k0 + k, :], start=(k == 0), stop=False, skip_group_check=True)
                    return e.matmul(bk[:, 256:512], ll, H[:, k0 + k, 0:256], start=False, stop=(k == K - 1), skip_group_check=True)
                while toks[k] is None:
                    pending.pop(0)[1]()
                tok = P(mm, split_tok[u], toks[k], fr if k == 0 else None)
                if q == 7:
                    unit_pe[u] = tok
                    feed(u + 2)
                    flush()
                    yield
            pending.append((st["tile"] + 8, lambda: evac(bk, tok, bi)))
            if q != 7:
                yield

        def raw_sum(dst, bk, tok, bi, *waits):
            i, t, fr = te.get()
            a = A(lambda e: e.activation(t, bk[:, 256:512], ACT.Copy), tok, fr)
            v = V(lambda e: e.tensor_tensor(dst, bk[:, 0:256], t, add), a, *waits)
            te.release(i, v)
            lbank.release(bi, v)
            return v

        def split(dst, j, src, tok, *waits, bias=None):
            if bias is None:
                a = A(lambda e: e.activation(dst[:, j, 0:256], src, ACT.Copy), tok, *waits)
                return V(lambda e: e.tensor_tensor(dst[:, j, 256:512], src, dst[:, j, 0:256].bitcast(f32), sub), a)
            a = A(lambda e: e.activation(dst[:, j, 0:256], src, ACT.Identity, bias=bias), tok, *waits)
            return V(lambda e: e.scalar_tensor_tensor(dst[:, j, 256:512], src, bias, dst[:, j, 0:256].bitcast(f32), add, sub), a)

        def run(gen):
            for _ in gen:
                pass

        def rsqrt(y, t, src, scale, eps, *waits):
            k = V(lambda e: e.tensor_scalar(t, src, scale, eps, mult, add), *waits)
            a = A(lambda e: e.activation(y, t, ACT.Ln), k)
            a = A(lambda e: e.activation(y, y, ACT.Exp, scale=-0.5), a)
            k = V(lambda e: e.tensor_tensor(t, t, y, mult), a)
            k = V(lambda e: e.tensor_tensor(t, t, y, mult), k)
            k = V(lambda e: e.tensor_scalar(t, t, -0.5, 1.5, mult, add), k)
            return V(lambda e: e.tensor_tensor(y, y, t, mult), k)

        class Stats:
            def __init__(self, *waits):
                self.last = list(waits)
                self.first = True

            def square(self, src, tok):
                if self.first:
                    k = G(lambda e: e.tensor_tensor(SQ[:, 0, :], src, src, mult), tok, self.last)
                    self.first = False
                else:
                    k = G(lambda e: e.tensor_tensor(SQ[:, 1, :], src, src, mult), tok, self.last)
                    k = G(lambda e: e.tensor_tensor(SQ[:, 0, :], SQ[:, 0, :], SQ[:, 1, :], add), k)
                self.last = [k]
                return k

            def finish(self, n, eps, *waits, y=None):
                bi, bk, fr = mbank.get()
                m = P(lambda e: e.matmul(bk[:, 0:256], cn("ones"), SQ[:, 0, :], start=True, stop=True), self.last, fr)
                self.done = m
                v = rsqrt(RS[:, 0, :] if y is None else y, RS[:, 1, :], bk[:, 0:256], 1.0 / n, eps, m, *waits)
                mbank.release(bi, v)
                return v

        tk_consts = D("consts", 16, lambda e: e.dma_start(CN[:, :], consts_d))
        for _ in range(NRAW):
            load_next()
        PI = B3[:, 1, :].bitcast(i32)
        k = A(lambda e: e.activation(SC[:, 16:32], col("c", 0, 16), ACT.Sigmoid), tk_cols)
        c_tok = V(lambda e: e.tensor_tensor(SC[:, 0:16], SC[:, 16:32], col("c", 0, 16), mult), k)
        cw_tok = V(lambda e: e.tensor_scalar(col("conv_w", 0, 96), col("conv_w", 0, 96), 0.5, None, mult), tk_cols)
        for s in range(16):
            proc_next()
        for i in range(4):
            tk_x = D("x", 16 * i + 16, lambda e, i=i: e.dma_start(X[:, 4 * i:4 * i + 4, :], xT[:, 4 * i:4 * i + 4, :]))
        tk_pos = D("pos", 16, lambda e: e.dma_start(PI, pos.rearrange("(a n) -> a n", a=1).broadcast_to([128, 256])))
        S1 = Stats(tk_x)
        for j in range(16):
            S1.square(X[:, j, :], None)
        for s in range(16, 40):
            proc_next()
        rs_tok = S1.finish(2048, 1e-6)

        COS, SIN = B3[:, 2, :], B3[:, 3, :]
        F = B3[:, 4, :]
        Q = B3[:, 5, :]
        k = V(lambda e: e.tensor_copy(F, PI), tk_pos, tk_consts)
        k = V(lambda e: e.tensor_scalar(F, F, cn("invf"), None, mult), k)
        k = V(lambda e: e.tensor_scalar(Q, F, float(1.0 / (2 * np.pi)), 12582912.0, mult, add), k)
        k = V(lambda e: e.tensor_scalar(Q, Q, 12582912.0, None, sub), k)
        rest = 2 * np.pi
        parts = []
        for bits in (8, 8, 8, 24):
            step = 2.0 ** (np.floor(np.log2(rest)) - bits + 1)
            p = float(np.floor(rest / step) * step)
            parts.append(p)
            rest = rest - p
        for p in parts:
            k = V(lambda e, p=p: e.scalar_tensor_tensor(F, Q, -p, F, mult, add), k)
        PIF = 3.1415925
        k = V(lambda e: e.tensor_scalar(F, F, PIF, -PIF, ALU.min, ALU.max), k)
        a1 = A(lambda e: e.activation(SIN, F, ACT.Sin), k)
        k = V(lambda e: e.scalar_tensor_tensor(Q, F, -1.0, F, mult, ALU.max), k)
        k = V(lambda e: e.tensor_scalar(Q, Q, -1.0, float(np.pi / 2), mult, add), k)
        tk_cos = A(lambda e: e.activation(COS, Q, ACT.Sin), k, a1)
        for s in range(40, ADA_FIRST):
            proc_next()

        def adaln(shift, scale, normname, S_tok, xtoks, *waits):
            m = [mod_tok[2 * shift], mod_tok[2 * shift + 1], mod_tok[2 * scale], mod_tok[2 * scale + 1]]
            assert None not in m
            g = V(lambda e: e.scalar_tensor_tensor(SC[:, 32:48], MOD[:, 16 * scale:16 * scale + 16], 1.0, col(normname, 0, 16), add, mult),
                  m, tk_cols, now())
            out = []
            for j in range(16):
                i, t, fr = tv.get()
                k = V(lambda e, j=j, t=t: e.scalar_tensor_tensor(t, X[:, j, :], SC[:, 32 + j:33 + j], RS[:, 0, :], mult, mult),
                      g, S_tok, xtoks[j], fr)
                k = split(H1, j, t, k, *waits, bias=MOD[:, 16 * shift + j:16 * shift + j + 1])
                tv.release(i, k)
                out.append(k)
            return out

        h_tok = adaln(0, 1, "norm_mix", rs_tok, [tk_x] * 16)

        x_read = now()
        CQ = [X[:, i, :] for i in range(8)]
        KPE = B3[:, 0, :]
        RN = {}

        def rope(dst, src, tok, *waits):
            bi, bk, fr = mbank.get()
            m = P(lambda e: e.matmul(bk[:, 0:256], cn("rot"), src, start=True, stop=True), tok, fr)
            i, t, fr2 = tv.get()
            v1 = V(lambda e: e.tensor_tensor(t, bk[:, 0:256], SIN, mult), m, tk_cos, fr2)
            v2 = V(lambda e: e.tensor_tensor(dst, src, COS, mult), m, *waits)
            v = V(lambda e: e.tensor_tensor(dst, dst, t, add), v1, v2)
            mbank.release(bi, v1)
            tv.release(i, v)
            return v

        cq_tok = [None] * 8
        SQS = [Stats(S1.done), None]

        def ev_c(j):
            def f(bk, tok, bi):
                cq_tok[j] = raw_sum(CQ[j], bk, tok, bi, x_read)
                if j == 4:
                    SQS[1] = Stats(*SQS[0].last, SQS[0].done)
                SQS[j // 4].square(CQ[j], cq_tok[j])
                if j == 3:
                    cnorm(0)
                if j == 7:
                    cnorm(1)
            return f

        H2_tok = [None] * 16

        def cnorm(half):
            k = SQS[half].finish(512, 1e-6, *([h_tok[-1]] if half == 0 else [H2_tok[3]]))
            name = "q_a_norm" if half == 0 else "kv_a_norm"
            for j in range(4):
                i, t, fr = tv.get()
                c = V(lambda e, j=j, t=t, half=half, name=name: e.scalar_tensor_tensor(t, CQ[4 * half + j], col(name, j), RS[:, 0, :], mult, mult), k, fr)
                H2_tok[4 * half + j] = split(H2, 4 * half + j, t, c)
                tv.release(i, H2_tok[4 * half + j])

        def ev_kpe(bk, tok, bi):
            k = raw_sum(KPE, bk, tok, bi)
            RN["kpe"] = rope(KPE, KPE, k)

        def need(lst, i):
            while lst[i] is None:
                pending.pop(0)[1]()
            return lst[i]

        qkv_tok = [None] * 24
        lin_tok = {"ba": None}

        def ev_qkv(j):
            def f(bk, tok, bi):
                dst = B1[:, j, :]
                i, t, fr = tv.get()
                k = raw_sum(t, bk, tok, bi, fr)
                o = COLS["conv_w"][0] + 4 * j
                v = V(lambda e: e.tensor_scalar(dst, t, CO[:, o + 3:o + 4], None, mult), k, cw_tok)
                for s in (1, 2, 3):
                    v = V(lambda e, s=s: e.scalar_tensor_tensor(dst[:, s:256], t[:, 0:256 - s], CO[:, o + 3 - s:o + 4 - s], dst[:, s:256], mult, add), v)
                s1 = A(lambda e: e.activation(t, dst, ACT.Tanh), v)
                v = V(lambda e: e.scalar_tensor_tensor(dst, t, 1.0, dst, add, mult), s1)
                tv.release(i, v)
                qkv_tok[j] = v
            return f

        BA = B3[:, 4, :]

        def ev_ba(bk, tok, bi):
            lin_tok["ba"] = raw_sum(BA, bk, tok, bi, tk_cos)

        for j in range(8):
            run(block(H1, h_tok, 0, "w_in", 0, j, ev_c(j)))
        run(block(H1, h_tok, 0, "w_in", 0, 8, ev_kpe))
        run(block(H1, h_tok, 0, "w_in", 0, 41, ev_ba))

        GS = B3[:, 5, :]

        def gs(o, w=16):
            return GS[:, o:o + w]
        BA_T, BETA, SPX, SPE, GG, GC, GL, BG, DK = (gs(0, 32), gs(32), gs(48), gs(64), gs(80), gs(96), gs(112), gs(128), gs(144))
        EA = GS[:, 160:168]

        def m28(x):
            return x.rearrange("p (m h) -> p m h", m=2)

        def scalars():
            bi, bk, fr = mbank.get()

            def trba(e):
                for m in range(2):
                    r = e.transpose(bk[:, 16 * m:16 * m + 16], BA[0:16, 128 * m:128 * m + 128], CN[0:16, 0:16])
                return r
            m = P(trba, need(lin_tok, "ba"), fr)
            k = V(lambda e: e.tensor_copy(BA_T, bk[:, 0:32]), m, tk_cos)
            mbank.release(bi, k)
            bat = BA_T.rearrange("p (m h) -> p m h", m=2)
            a1 = A(lambda e: e.activation(m28(BETA), bat[:, :, 0:8], ACT.Sigmoid), k)
            k = V(lambda e: e.tensor_tensor(m28(SPX), bat[:, :, 8:16], col("dt_bias", 0, 8).unsqueeze(1).broadcast_to([128, 2, 8]), add), k)
            k2 = V(lambda e: e.scalar_tensor_tensor(SPE, SPX, -1.0, SPX, mult, ALU.max), k)
            a = A(lambda e: e.activation(SPE, SPE, ACT.Exp, scale=-1.0), k2)
            a = A(lambda e: e.activation(SPE, SPE, ACT.Ln, bias=1.0), a)
            a2 = A(lambda e: e.activation(EA, col("A_log", 0, 8), ACT.Exp), a)
            k = V(lambda e: e.scalar_tensor_tensor(SPX, SPX, 0.0, SPE, ALU.max, add), a)
            g_tok = V(lambda e: e.scalar_tensor_tensor(m28(GG), m28(SPX), -1.0, EA.unsqueeze(1).broadcast_to([128, 2, 8]), mult, mult), k, a2)
            bi, bk2, fr = mbank.get()

            def cums(e):
                e.matmul(bk2[:, 0:16], cn("tri"), GG, start=True, stop=True)
                return e.matmul(bk2[:, 16:32], cn("ch"), GG, start=True, stop=True)
            m = P(cums, g_tok, fr)
            k = V(lambda e: e.tensor_copy(GC, bk2[:, 0:16]), m)
            k = V(lambda e: e.tensor_copy(GL, bk2[:, 16:32]), k)
            mbank.release(bi, k)
            v = V(lambda e: e.tensor_tensor(DK, GL, GC, sub), k)
            a = A(lambda e: e.activation(DK, DK, ACT.Exp), v)
            a = A(lambda e: e.activation(BG, GC, ACT.Exp), a)
            return V(lambda e: e.tensor_tensor(BG, BG, BETA, mult), a, a1)

        n = 0
        for h in range(4):
            for j in (8 + h, h, 16 + h):
                run(block(H1, h_tok, 0, "w_in", 0, 9 + j, ev_qkv(j)))
                n += 1
                if n == 2:
                    sc_tok = scalars()

        SCALE = 192.0 ** -0.5
        pr = Ring([B2[:, 11 + i, :] for i in range(4)])
        ptr = Ring([B2[:, 9, :], B2[:, 10, :]])
        qn_r = Ring([B2[:, 0, :], B2[:, 1, :]])
        kn_r = Ring([B2[:, 2, :], B2[:, 3, :]])
        qp_r = Ring([B2[:, 4, :], B2[:, 5, :]])
        vt_r = Ring([B2[:, 6 + i, :].rearrange("p (m n) -> p m n", m=2) for i in range(3)])
        mst = {}
        SM = SC[:, 64:256]
        av = {}
        mo_tok = [None] * 8
        HD = {}
        part = {}

        def softmax_stages(scores, biasmask, keys, pv):
            def s0(i):
                bi, bk, fr = mbank.get()
                m = scores(i, bk, fr)
                pi, p, pf = pr.get()
                v = biasmask(i, p[:, 0:keys(i)], bk[:, 0:keys(i)], m, pf)
                mbank.release(bi, v)
                mst[i] = [pi, p[:, 0:keys(i)], v]

            def s1(i):
                pi, p, v = mst[i]
                c = 3 * (i % 32)
                v = V(lambda e: e.tensor_reduce(SM[:, c:c + 1], p, AX, ALU.max, negate=True), v)
                a = A(lambda e: e.activation(p, p, ACT.Exp, bias=SM[:, c:c + 1], accum_out=SM[:, c + 1:c + 2]), v)
                mst[i].append(a)

            def s2(i):
                pi, p, _, a = mst[i]
                c = 3 * (i % 32)
                v = V(lambda e: e.reciprocal(SM[:, c + 2:c + 3], SM[:, c + 1:c + 2]), a)
                v = V(lambda e: e.tensor_scalar(p, p, SM[:, c + 2:c + 3], None, mult), v)
                bi, bk, fr = mbank.get()
                nk = keys(i) // 128

                def tr(e):
                    for q in range(nk):
                        r = e.transpose(bk[:, 128 * q:128 * q + 128], p[:, 128 * q:128 * q + 128], cn("ident"))
                    return r
                m = P(tr, v, fr)
                pr.release(pi, m)
                ti, t, tf = ptr.get()
                a = A(lambda e: e.activation(t[:, 0:keys(i)], bk[:, 0:keys(i)], ACT.Copy), m, tf)
                mbank.release(bi, a)
                mst[i] = [ti, t, a]

            def s3(i):
                ti, t, a = mst[i]
                ptr.release(ti, pv(i, t, a))
            return [s0, s1, s2, s3]

        def pipe_step(stages, step, n):
            for s in range(len(stages) - 1, -1, -1):
                i = step - s
                if 0 <= i < n:
                    stages[s](i)

        def token_major(dst, src, k, *waits):
            mi, mk, mf = mbank.get()

            def tr(e):
                for m in range(2):
                    r = e.transpose(mk[:, 128 * m:128 * m + 128], src[:, 128 * m:128 * m + 128], cn("ident"))
                return r
            m = P(tr, k, mf)
            a = A(lambda e: e.activation(dst, mk[:, 0:256].rearrange("p (m n) -> p m n", m=2), ACT.Copy), m, *waits)
            mbank.release(mi, a)
            return m, a

        def ev_ring(ring, key):
            HD[key] = None

            def f(bk, tok, bi):
                i, t, fr = ring.get()
                HD[key] = (i, t, raw_sum(t, bk, tok, bi, fr))
            return f

        def ev_qp(key):
            HD[key] = None

            def f(bk, tok, bi):
                i, t, fr = qp_r.get()
                k = raw_sum(t, bk, tok, bi, fr)
                need(RN, "kpe")
                HD[key] = (i, t, rope(t, t, k))
            return f

        def ev_vt(key):
            HD[key] = None

            def f(bk, tok, bi):
                i, t, fr = tv.get()
                k = raw_sum(t, bk, tok, bi, fr)
                vi, vt, vf = vt_r.get()
                m, a = token_major(vt, t, k, vf)
                tv.release(i, m)
                HD[key] = (vi, vt, a)
            return f

        RN.setdefault("kpe", None)

        def mla_scores(i, bk, fr):
            h, qb = divmod(i, 2)
            nk = 128 * (qb + 1)
            o = 64 * (h % 2)
            (qi, qn, qt), (ki, kn, kt), (pi, qp, pt) = need(HD, ("q", h)), need(HD, ("k", h)), need(HD, ("p", h // 2))

            def mm(e):
                e.matmul(bk[:, 0:nk], qn[:, 128 * qb:128 * qb + 128], kn[:, 0:nk], start=True, stop=False)
                return e.matmul(bk[:, 0:nk], qp[o:o + 64, 128 * qb:128 * qb + 128], KPE[o:o + 64, 0:nk], start=False, stop=True)
            m = P(mm, qt, kt, pt, RN["kpe"], fr)
            if qb == 1:
                qn_r.release(qi, m)
                kn_r.release(ki, m)
                if h % 2:
                    qp_r.release(pi, m)
            return m

        def mla_mask(i, p, ps, m, pf):
            qb = i % 2
            return V(lambda e: e.scalar_tensor_tensor(p, ps, SCALE, cn("mm", 128 - 128 * qb, 256), mult, add), m, pf)

        def mla_pv(i, t, a):
            h, qb = divmod(i, 2)
            if qb == 0:
                av["b"] = mbank.get()
            bi, bk, fr = av["b"]
            vi, vt, vtok = need(HD, ("v", h))

            def mm(e):
                for q in range(qb + 1):
                    r = e.matmul(bk[:, 128 * qb:128 * qb + 128], vt[:, q, :], t[:, 128 * q:128 * q + 128],
                                 start=(q == 0), stop=(q == qb))
                return r
            m = P(mm, a, vtok, fr if qb == 0 else None)
            if qb == 1:
                vt_r.release(vi, m)
                x = A(lambda e: e.activation(H2[:, 8 + h, 0:256], bk[:, 0:256], ACT.Copy), m)
                mo_tok[h] = V(lambda e: e.tensor_tensor(H2[:, 8 + h, 256:512], bk[:, 0:256], H2[:, 8 + h, 0:256].bitcast(f32), sub), x)
                mbank.release(bi, mo_tok[h])
            return m

        def mla_gen():
            stages = softmax_stages(mla_scores, mla_mask, lambda i: 128 * (i % 2 + 1), mla_pv)

            def make(h):
                if h % 2 == 0:
                    yield from block(H2, H2_tok[0:4], 0, "w_uq", 0, 8 + h // 2, ev_qp(("p", h // 2)))
                yield from block(H2, H2_tok[0:4], 0, "w_uq", 0, h, ev_ring(qn_r, ("q", h)))
                yield from block(H2, H2_tok[4:8], 4, "w_ukv", 0, h, ev_ring(kn_r, ("k", h)))
                yield from block(H2, H2_tok[4:8], 4, "w_ukv", 0, 8 + h, ev_vt(("v", h)))
            yield from make(0)
            for step in range(19):
                if step % 2 == 0 and step // 2 < 7:
                    yield from make(step // 2 + 1)
                pipe_step(stages, step, 16)
                yield

        def fill_a():
            for h in range(4, 8):
                for j in (8 + h, h, 16 + h):
                    yield from block(H1, h_tok, 0, "w_in", 0, 9 + j, ev_qkv(j))
            yield from mla_gen()

        fills = [fill_a()]

        def pump(n=1):
            for _ in range(n):
                while fills:
                    try:
                        next(fills[0])
                        break
                    except StopIteration:
                        fills.pop(0)

        def pair(t, i):
            return t[:, i:i + 2, :].rearrange("p a t -> p (a t)")
        KBG, KDEC, VB, AT, LT, CT, MM_, MT = (pair(X, 2 * i) for i in range(8))
        SS, DD, EG, QG, UU = pair(B2, 16), pair(B2, 18), pair(B2, 20), pair(B2, 22), pair(B3, 6)
        cq_read = [H2_tok[7], tk_cos]

        def h4(x):
            return x.rearrange("p (h n) -> p h n", h=4)

        def h2(x, s):
            return x[:, 256 * s:256 * s + 256]

        def mask4(name, a=0, b=128, n=4):
            return cn(name, a, b).unsqueeze(1).broadcast_to([128, n, 128])

        def colb(x, hg, m):
            return x[:, 8 * m + 4 * hg:8 * m + 4 * hg + 4].unsqueeze(2).broadcast_to([128, 4, 128])

        def mmn(heads, fn, *waits):
            bi, bk, fr = mbank.get()

            def go(e):
                for n, h in enumerate(heads):
                    r = fn(e, h, bk[:, 128 * n:128 * n + 128])
                return r
            return bi, bk, P(go, fr, *waits)

        def hx(t, h):
            return t[:, 128 * h:128 * h + 128]

        FULL = (0, 1, 2, 3)
        SUB = ((0, 1), (2, 3))
        o_tok = [None] * 8
        need(H2_tok, 7)
        cq_read = [H2_tok[7], tk_cos]
        last = {n: cq_read for n in ("KBG", "KDEC", "VB", "AT", "LT", "CT", "MM", "MT", "SS", "DD", "EG", "QG", "UU")}

        rs_read = [H2_tok[7]]
        for hg in range(2):
            hs = [4 * hg + h for h in range(4)]
            bi, bk, fr = mbank.get()
            for n in range(8):
                j = (hs[n] if n < 4 else 8 + hs[n - 4])
                i, t, ft = te.get()
                a = A(lambda e, j=j, t=t: e.activation(t, B1[:, j, :], ACT.Square), need(qkv_tok, j), ft)
                m = P(lambda e, n=n, t=t, bk=bk: e.matmul(bk[0:8, 0:256], cn("slide", 7 - n, 15 - n), t, start=(n == 0), stop=(n == 7)), a, fr)
                te.release(i, m)
            r = rsqrt(RS[0:8, 0, :], RS[0:8, 1, :], bk[0:8, 0:256], 1.0, 1e-6, m, rs_read)
            mbank.release(bi, r)
            for n in range(8):
                j = (hs[n] if n < 4 else 8 + hs[n - 4])
                if n % 2 == 0:
                    bi, bk, fr = mbank.get()
                    m = P(lambda e, n=n, bk=bk: [e.matmul(bk[:, 256 * q:256 * q + 256], CN[0:8, n + q:n + q + 1].broadcast_to([8, 128]), RS[0:8, 0, :],
                                                          start=True, stop=True) for q in range(2)][-1], r, fr)
                    rs_read = [m]
                qkv_tok[j] = V(lambda e, n=n, j=j, bk=bk: e.scalar_tensor_tensor(
                    B1[:, j, :], B1[:, j, :], 128.0 ** -0.5 if n < 4 else 1.0, bk[:, 256 * (n % 2):256 * (n % 2) + 256], mult, mult), m)
                if n % 2:
                    mbank.release(bi, qkv_tok[j])
                    pump(1)
            for h in hs:
                need(qkv_tok, 16 + h)
            s_tok = [V(lambda e, s=s: e.memset(h2(SS, s), 0.0), last["SS"]) for s in range(2)]
            for mt in range(2):
                tt = slice(128 * mt, 128 * mt + 128)
                qk = [qkv_tok[h] for h in hs] + [qkv_tok[8 + h] for h in hs]
                v = V(lambda e, hg=hg, mt=mt: e.tensor_tensor(h4(EG), mask4("tri"), colb(GG, hg, mt), mult), last["EG"], sc_tok)
                bi, bk, fr = mbank.get()
                m = P(lambda e, bk=bk: e.matmul(bk[:, :], cn("ones"), EG, start=True, stop=True), v, fr)
                b4, bk4, m4 = mmn(FULL, lambda e, h, o, hs=hs, tt=tt: e.matmul(o, B1[:, 8 + hs[h], tt], B1[:, 8 + hs[h], tt], start=True, stop=True), qk)
                v2 = V(lambda e, hg=hg, mt=mt: e.tensor_tensor(h4(CT), mask4("ident"), colb(BETA, hg, mt), mult), last["CT"], sc_tok)
                b2, bk2, fr2 = mbank.get()
                m2 = P(lambda e, bk2=bk2: e.matmul(bk2[:, :], cn("ones"), CT, start=True, stop=True), v2, fr2)
                v = V(lambda e, bk=bk, hg=hg, mt=mt: e.tensor_tensor(h4(DD), h4(bk[:, :]), colb(GC, hg, mt), sub), m, last["DD"])
                v = V(lambda e: e.tensor_scalar(DD, DD, 0.0, None, ALU.min), v)
                a = A(lambda e: e.activation(DD, DD, ACT.Exp), v)
                eg_tok = A(lambda e, bk=bk: e.activation(EG, bk[:, :], ACT.Exp), m)
                mbank.release(bi, v, eg_tok)
                dm = V(lambda e: e.tensor_tensor(h4(DD), h4(DD), mask4("tri"), mult), a)
                v = V(lambda e, bk4=bk4: e.tensor_tensor(LT, bk4[:, :], DD, mult), m4, dm, last["LT"])
                mbank.release(b4, v)
                lt_tok = V(lambda e, bk2=bk2: e.tensor_tensor(LT, bk2[:, :], LT, mult), v, m2)
                mbank.release(b2, lt_tok)
                mt_t, mm_t, ct_t, u_t = [None] * 2, [None] * 2, [None] * 2, [None] * 2

                def m2h(x):
                    return x.rearrange("p (h n) -> p h n", h=2)
                for s in range(2):
                    v = V(lambda e, s=s: e.tensor_tensor(m2h(h2(CT, s)), m2h(h2(LT, s)), mask4("lm", n=2), mult), lt_tok, m2)
                    mt_t[s] = V(lambda e, s=s: e.tensor_tensor(m2h(h2(MT, s)), mask4("ident", n=2), m2h(h2(CT, s)), sub), v, last["MT"])
                    b3, bk3, m3 = mmn(SUB[s], lambda e, h, o: e.transpose(o, hx(MT, h), cn("ident")), mt_t[s])
                    mm_t[s] = A(lambda e, bk3=bk3, s=s: e.activation(h2(MM_, s), bk3[:, 0:256], ACT.Copy), m3, last["MM"])
                    mbank.release(b3, mm_t[s])
                    ct_t[s] = V(lambda e, s=s: e.tensor_tensor(m2h(h2(CT, s)), m2h(h2(LT, s)), mask4("lm", 128, 256, n=2), mult), mt_t[s])
                rest_ops = []

                def side(n):
                    for _ in range(n):
                        if rest_ops:
                            rest_ops.pop(0)()
                R = {}

                def side_at(hs=hs, tt=tt, qk=qk):
                    b3, bk3, m3 = mmn(FULL, lambda e, h, o: e.matmul(o, B1[:, 8 + hs[h], tt], B1[:, hs[h], tt], start=True, stop=True), qk)
                    R["at"] = V(lambda e: e.tensor_tensor(AT, bk3[:, :], DD, mult), m3, dm, last["AT"])
                    mbank.release(b3, R["at"])

                def side_k(hs=hs, tt=tt, qk=qk, hg=hg, mt=mt):
                    b3, bk3, m3 = mmn(FULL, lambda e, h, o: e.transpose(o, B1[:, 8 + hs[h], tt], cn("ident")), qk)
                    R["kbg"] = V(lambda e: e.tensor_tensor(h4(KBG), h4(bk3[:, :]), colb(BG, hg, mt), mult), m3, last["KBG"])
                    R["kd"] = V(lambda e: e.tensor_tensor(h4(KDEC), h4(bk3[:, :]), colb(DK, hg, mt), mult), m3, last["KDEC"])
                    mbank.release(b3, R["kd"])

                def side_v(hs=hs, tt=tt, hg=hg, mt=mt):
                    b3, bk3, m3 = mmn(FULL, lambda e, h, o: e.transpose(o, B1[:, 16 + hs[h], tt], cn("ident")), [qkv_tok[16 + h] for h in hs])
                    R["vb"] = V(lambda e: e.tensor_tensor(h4(VB), h4(bk3[:, :]), colb(BETA, hg, mt), mult), m3, last["VB"])
                    mbank.release(b3, R["vb"])
                    R["v_read"] = m3

                def side_q(hg=hg, tt=tt, qk=qk):
                    R["qg"] = V(lambda e: e.tensor_tensor(h4(QG), B1[:, 4 * hg:4 * hg + 4, tt], h4(EG), mult), eg_tok, qk, last["QG"])
                rest_ops = [side_at, side_k, side_v, side_q]
                for lv in range(1, 6):
                    us = []
                    for s in range(2):
                        b3, bk3, m3 = mmn(SUB[s], lambda e, h, o: e.matmul(o, hx(CT, h), hx(MM_, h), start=True, stop=True), ct_t[s], mm_t[s])
                        us.append((b3, bk3, m3))
                    side(1)
                    for s in range(2):
                        b3, bk3, m3 = us[s]
                        u_t[s] = A(lambda e, bk3=bk3, s=s: e.activation(h2(UU, s), bk3[:, 0:256], ACT.Copy), m3, mt_t[s], last["UU"])
                        mbank.release(b3, u_t[s])
                    pump(1)
                    for s in range(2):
                        b4, bk4, m4 = mmn(SUB[s], lambda e, h, o: e.matmul(o, hx(UU, h), hx(MT, h), start=True, stop=True), u_t[s], mt_t[s])
                        if lv < 5:
                            ct_t[s] = V(lambda e, lv=lv, s=s: e.tensor_tensor(m2h(h2(CT, s)), m2h(h2(LT, s)), mask4("lm", 128 * lv + 128, 128 * lv + 256, n=2), mult), us[s][2])
                            b5, bk5, m5 = mmn(SUB[s], lambda e, h, o: e.matmul(o, hx(MT, h), hx(UU, h), start=True, stop=True), u_t[s], mt_t[s])
                            mm_t[s] = V(lambda e, bk5=bk5, s=s: e.tensor_tensor(h2(MM_, s), h2(MM_, s), bk5[:, 0:256], sub), m5)
                            mbank.release(b5, mm_t[s])
                            mt_t[s] = V(lambda e, bk4=bk4, s=s: e.tensor_tensor(h2(MT, s), h2(MT, s), bk4[:, 0:256], sub), m4, m5)
                        else:
                            mt_t[s] = V(lambda e, bk4=bk4, s=s: e.tensor_tensor(h2(MT, s), h2(MT, s), bk4[:, 0:256], sub), m4)
                        mbank.release(b4, mt_t[s])
                        u_t[s] = m4
                side(4)
                last["LT"] = last["CT"] = [us[0][2], us[1][2], ct_t[0], ct_t[1]]
                last["DD"] = [R["at"]]
                uu_t, w_t = [None] * 2, [None] * 2
                for s in range(2):
                    b3, bk3, m3 = mmn(SUB[s], lambda e, h, o: e.matmul(o, hx(KBG, h), hx(MT, h), start=True, stop=True), mt_t[s], R["kbg"])
                    w_t[s] = A(lambda e, bk3=bk3, s=s: e.activation(h2(MM_, s), bk3[:, 0:256], ACT.Copy), m3, us[s][2])
                    mbank.release(b3, w_t[s])
                    b3, bk3, m3 = mmn(SUB[s], lambda e, h, o: e.matmul(o, hx(MT, h), hx(VB, h), start=True, stop=True), mt_t[s], R["vb"])
                    uu_t[s] = A(lambda e, bk3=bk3, s=s: e.activation(h2(UU, s), bk3[:, 0:256], ACT.Copy), m3, u_t[s])
                    mbank.release(b3, uu_t[s])
                last["MT"] = last["VB"] = last["KBG"] = [m3]
                pump(1)
                for cc in range(2):
                    r0 = 64 * cc
                    rr = slice(r0, r0 + 64)
                    vns = []
                    for s in range(2):
                        b3, bk3, m3 = mmn(SUB[s], lambda e, h, o, rr=rr: e.matmul(o[rr, :], MM_[:, 128 * h + rr.start:128 * h + rr.stop], hx(SS, h), start=True, stop=True),
                                          w_t[s], s_tok[s])
                        vns.append(V(lambda e, bk3=bk3, rr=rr, s=s: e.tensor_tensor(UU[rr, 256 * s:256 * s + 256], UU[rr, 256 * s:256 * s + 256], bk3[rr, 0:256], sub), m3, uu_t[s]))
                        mbank.release(b3, vns[s])
                        w_read = m3
                    pump(1)
                    for s in range(2):
                        bi, bk, fr = mbank.get()

                        def sup(e, bk=bk, rr=rr, s=s):
                            for n, h in enumerate(SUB[s]):
                                r = e.matmul(bk[:, 128 * n:128 * n + 128], hx(KDEC, h)[rr, :], hx(UU, h)[rr, :], start=True, stop=True)
                            return r
                        ms = P(sup, vns[s], R["kd"], fr)
                        b5, bk5, fr5 = mbank.get()

                        def om(e, bk5=bk5, rr=rr, s=s):
                            for n, h in enumerate(SUB[s]):
                                o = bk5[:, 64 * n:64 * n + 64]
                                e.matmul(o, hx(SS, h), QG[:, 128 * h + rr.start:128 * h + rr.stop], start=True, stop=False)
                                r = e.matmul(o, hx(UU, h)[rr, :], AT[rr, 128 * h + rr.start:128 * h + rr.stop], start=False, stop=True)
                            return r
                        mo = P(om, vns[s], R["qg"], R["at"], s_tok[s], fr5)
                        ts = slice(128 * mt + r0, 128 * mt + r0 + 64)
                        oe = A(lambda e, bk5=bk5, ts=ts, hg=hg, s=s: e.activation(B1[:, 4 * hg + 2 * s:4 * hg + 2 * s + 2, ts], bk5[:, 0:128].rearrange("p (h n) -> p h n", h=2), ACT.Copy), mo, R["qg"])
                        mbank.release(b5, oe)
                        for n, h in enumerate(SUB[s]):
                            s_tok[s] = V(lambda e, n=n, h=h, bk=bk, r0=r0: e.scalar_tensor_tensor(
                                hx(SS, h), hx(SS, h), EG[:, 128 * h + r0 + 63:128 * h + r0 + 64], bk[:, 128 * n:128 * n + 128], mult, add), ms, mo)
                        mbank.release(bi, s_tok[s])
                    pump(1)
                for n in ("MM", "QG", "AT", "UU", "KDEC"):
                    last[n] = [mo, w_read]
                last["EG"] = last["SS"] = list(s_tok) + [mo, R["qg"]]
            for h in hs:
                o_tok[h] = oe
            if hg == 0:
                v_read0 = R["v_read"]
        x_free = now()
        v_read1 = R["v_read"]
        for i in range(4):
            tk_x2 = D("x2", 16 * i + 16, lambda e, i=i: e.dma_start(X[:, 4 * i:4 * i + 4, :], xT[:, 4 * i:4 * i + 4, :]), x_free)
        while fills:
            pump(1)
        Z = [B1[:, 16 + i, :] for i in range(8)]
        YA = [B1[:, 8 + i, :] for i in range(8)] + [B2[:, i, :] for i in range(8)]
        GB = [B2[:, 8 + i, :] for i in range(16)]
        z_tok, ya_tok, gb_tok = [None] * 8, [None] * 16, [None] * 16
        free2 = now()

        def half_sum(dst, bk, tok, bi, *waits):
            i, t, fr = te.get()
            a = A(lambda e: e.activation(t, bk[:, 256:512], ACT.Copy, scale=0.5), tok, fr)
            v = V(lambda e: e.scalar_tensor_tensor(dst, bk[:, 0:256], 0.5, t, mult, add), a, *waits)
            te.release(i, v)
            lbank.release(bi, v)
            return v

        def ev_z(j):
            def f(bk, tok, bi):
                k = half_sum(Z[j], bk, tok, bi, v_read1)
                i, t, fr = te.get()
                a = A(lambda e: e.activation(t, Z[j], ACT.Tanh), k, fr)
                z_tok[j] = V(lambda e: e.scalar_tensor_tensor(Z[j], t, 1.0, Z[j], add, mult), a)
                te.release(i, z_tok[j])
            return f

        def ev_gate(dst, toks, j):
            def f(bk, tok, bi):
                k = half_sum(dst[j], bk, tok, bi, free2)
                toks[j] = A(lambda e: e.activation(dst[j], dst[j], ACT.Tanh), k)
            return f

        def ev_ya(j):
            def f(bk, tok, bi):
                i, t, fr = tv.get()
                k = raw_sum(t, bk, tok, bi, fr)
                ya_tok[j] = V(lambda e: e.scalar_tensor_tensor(YA[j], YA[j], 1.0, t, add, mult), k, need(ga_tok, j))
                tv.release(i, ya_tok[j])
            return f
        ga_tok = [None] * 16

        def fill_b():
            for j in range(8):
                yield from block(H1, h_tok, 0, "w_in", 0, 33 + j, ev_z(j))
            for j in range(16):
                yield from block(H1, h_tok, 0, "w_in", 0, 42 + j, ev_gate(YA, ga_tok, j))
                yield from block(H2, mo_tok, 8, "w_o_mla", 0, j, ev_ya(j))
            for j in range(16):
                yield from block(H1, h_tok, 0, "w_in", 0, 58 + j, ev_gate(GB, gb_tok, j))
        fills.append(fill_b())
        bi, bk, fr = mbank.get()
        for h in range(8):
            i, t, ft = te.get()
            a = A(lambda e, h=h, t=t: e.activation(t, B1[:, h, :], ACT.Square), o_tok[h], ft)
            m = P(lambda e, h=h, t=t, bk=bk: e.matmul(bk[0:8, 0:256], cn("slide", 7 - h, 15 - h), t, start=(h == 0), stop=(h == 7)), a, fr)
            te.release(i, m)
        r = rsqrt(RS[0:8, 0, :], RS[0:8, 1, :], bk[0:8, 0:256], 1.0 / 128, 1e-6, m, now())
        mbank.release(bi, r)
        pump(8)
        gdn_tok = [None] * 8
        for h in range(8):
            if h % 2 == 0:
                bi, bk, fr = mbank.get()
                m = P(lambda e, h=h, bk=bk: [e.matmul(bk[:, 256 * q:256 * q + 256], CN[0:8, h + q:h + q + 1].broadcast_to([8, 128]), RS[0:8, 0, :],
                                                      start=True, stop=True) for q in range(2)][-1], r, fr)
            o = B1[:, h, :]
            v = V(lambda e, h=h, o=o, bk=bk: e.scalar_tensor_tensor(o, o, col("gdn_norm"), bk[:, 256 * (h % 2):256 * (h % 2) + 256], mult, mult), m)
            if h % 2:
                mbank.release(bi, v)
            v = V(lambda e, o=o, h=h: e.tensor_tensor(o, o, Z[h], mult), v, need(z_tok, h))
            gdn_tok[h] = split(H2, h, o, v, free2)
            pump(2)
        while fills:
            pump(1)
        h1_free = ("pe", count["pe"])
        m_tok = [None] * 16

        def ev_yb(j):
            def f(bk, tok, bi):
                i, t, fr = tv.get()
                k = raw_sum(t, bk, tok, bi, fr)
                v = V(lambda e: e.scalar_tensor_tensor(t, GB[j], 1.0, t, add, mult), k, need(gb_tok, j))
                v = V(lambda e: e.tensor_tensor(t, t, YA[j], add), v, need(ya_tok, j))
                a = A(lambda e: e.activation(H1[:, j, 0:256], t, ACT.Copy, scale=0.5), v, h1_free)
                m_tok[j] = V(lambda e: e.scalar_tensor_tensor(H1[:, j, 256:512], t, 0.5, H1[:, j, 0:256].bitcast(f32), mult, sub), a)
                tv.release(i, m_tok[j])
            return f
        for j in range(16):
            run(block(H2, gdn_tok, 0, "w_o_gdn", 0, j, ev_yb(j)))

        x_tok = [None] * 16
        S = Stats(SQS[1].done)

        def ev_res(gate, S, extra):
            def mk(j):
                def f(bk, tok, bi):
                    i, t, fr = tv.get()
                    k = raw_sum(t, bk, tok, bi, fr)
                    x_tok[j] = V(lambda e: e.scalar_tensor_tensor(X[:, j, :], t, MOD[:, 16 * gate + j:16 * gate + j + 1], X[:, j, :], mult, add),
                                 k, extra, mod_tok[2 * gate + j // 8], x_tok[j])
                    tv.release(i, x_tok[j])
                    if S is not None:
                        S.square(X[:, j, :], x_tok[j])
                return f
            return mk
        ev = ev_res(2, S, tk_x2)
        for j in range(16):
            run(block(H1, m_tok, 0, "w_o", 0, j, ev(j)))
        flush(True)
        rs_tok = S.finish(2048, 1e-6)
        Sp = S
        h_tok = adaln(3, 4, "norm_ffn", rs_tok, x_tok, now())

        def ffn(cuts, up, down_name, ev_down, KD):
            at = 0
            for ci, n in enumerate(cuts):
                f_tok = [None] * n
                for s in range(n):
                    run(up(at + s, s, f_tok))
                h1_last[0] = ("pe", count["pe"])
                for j in range(16):
                    run(block(H2, f_tok, 0, down_name, at, j, ev_down(ci, j)))
                h2_free[0] = [("pe", count["pe"])]
                at += n
            flush(True)

        h1_last = [None]
        def silu_to(dst, src, tok, *waits):
            i, t, fr = te.get()
            a = A(lambda e: e.activation(t, src, ACT.Sigmoid), tok, fr)
            v = V(lambda e: e.tensor_tensor(dst, src, t, mult), a, *waits)
            te.release(i, v)
            return v

        G_ = {}

        def up1(i, s, f_tok):
            def e1(bk, tok, bi):
                q, t, fr = tv.get()
                k = raw_sum(t, bk, tok, bi, fr)
                G_[i] = (q, t, silu_to(t, t, k))

            def e2(bk, tok, bi):
                q, t, fr = tv.get()
                k = raw_sum(t, bk, tok, bi, fr)
                gq, g, gk = G_.pop(i)
                v = V(lambda e: e.tensor_tensor(t, t, g, mult), k, gk)
                tv.release(gq, v)
                f_tok[s] = split(H2, s, t, v, h2_free[0])
                tv.release(q, f_tok[s])
            yield from block(H1, h_tok, 0, "w_gate_up", 0, i, e1)
            yield from block(H1, h_tok, 0, "w_gate_up", 0, 44 + i, e2)

        h2_free = [now()]
        S = Stats(Sp.done)
        R12, R1, ACC2 = B3[:, 0, :], B3[:, 1, :], B3[:, 2, :]
        FP = SC[:, 48:64]
        fp_tok = V(lambda e: e.tensor_tensor(FP, col("final_norm", 0, 16), col("pre_mix", 0, 16), mult), tk_cols)
        u_tok2 = [None] * 16
        acc2 = [None]

        def evd(ci, j):
            f = ev_res(5, S if ci == 2 else None, None)(j)

            def go(bk, tok, bi):
                f(bk, tok, bi)
                if ci < 2:
                    return
                sq = SQ[:, 1, :]
                k = G(lambda e: e.tensor_scalar(sq, X[:, j, :], col("final_norm", j), None, mult), x_tok[j], S.last)
                k = G(lambda e: e.tensor_tensor(ACC2 if j == 0 else sq, sq, sq, mult), k, acc2[0])
                if j:
                    k = G(lambda e: e.tensor_tensor(ACC2, ACC2, sq, add), k)
                acc2[0] = k
                S.last = S.last + [k]
                a = A(lambda e: e.activation(H1[:, j, 0:256], X[:, j, :], ACT.Copy, scale=FP[:, j:j + 1]), x_tok[j], fp_tok, h1_last[0])
                u_tok2[j] = V(lambda e: e.scalar_tensor_tensor(H1[:, j, 256:512], X[:, j, :], FP[:, j:j + 1], H1[:, j, 0:256].bitcast(f32), mult, sub), a)
            return go
        ffn((15, 15, 14), up1, "w_down", evd, 44)
        ffn_end = now()
        r1_tok = S.finish(2048, 1e-6, ffn_end, y=R1)
        Sp = S
        bi, bk, fr = mbank.get()
        m = P(lambda e, bk=bk: e.matmul(bk[:, 0:256], cn("ones"), ACC2, start=True, stop=True), acc2[0], fr)
        v = V(lambda e, bk=bk: e.tensor_tensor(RS[:, 2, :], bk[:, 0:256], R1, mult), m, r1_tok)
        mbank.release(bi, v)
        v = V(lambda e: e.tensor_tensor(RS[:, 2, :], RS[:, 2, :], R1, mult), v)
        v = rsqrt(RS[:, 0, :], RS[:, 1, :], RS[:, 2, :], 1.0 / 2048, 1e-6, v)
        r12_tok = V(lambda e: e.tensor_tensor(R12, R1, RS[:, 0, :], mult), v)
        b2_free = ffn_end
        UP = B1[:, 0:9, :].rearrange("p a t -> p (a t)")[:, 0:8 * 286].rearrange("p (j n) -> p j n", j=8)
        pad_tok = V(lambda e: e.memset(UP, 0.0), b2_free)
        CA = [B1[:, 9 + j, :] for j in range(8)]
        BB = [B2[:, 13 + i, :] for i in range(4)]
        MEAN = B2[:, 17, :]
        qn_r = Ring([B2[:, 0, :], B2[:, 1, :]])
        kn_r = Ring([B2[:, 2, :], B2[:, 3, :]])
        vt_r = Ring([B2[:, 4 + i, :].rearrange("p (m n) -> p m n", m=2) for i in range(3)])
        ptr = Ring([B2[:, 7, :], B2[:, 8, :]])
        pr = Ring([B2[:, 9 + i, :] for i in range(4)])
        for ring in (qn_r, kn_r, vt_r, ptr, pr):
            ring.free = [b2_free for _ in ring.items]
        mst.clear()
        HD.clear()
        u_tok, a2_tok = [None] * 8, [None] * 8

        def scaled_sum(dst, bk, tok, bi, *waits):
            k = raw_sum(dst, bk, tok, bi, *waits)
            return V(lambda e: e.tensor_tensor(dst, dst, R12, mult), k, r12_tok)

        def e_a(j):
            def f(bk, tok, bi):
                a2_tok[j] = scaled_sum(UP[:, j, 15:271], bk, tok, bi, pad_tok)
            return f

        def e_g(j):
            def f(bk, tok, bi):
                i, t, fr = tv.get()
                k = scaled_sum(t, bk, tok, bi, fr)
                a = A(lambda e: e.activation(t, t, ACT.Tanh, scale=0.5), k)
                v = V(lambda e: e.scalar_tensor_tensor(UP[:, j, 15:271], t, 1.0, UP[:, j, 15:271], add, mult), a, a2_tok[j])
                u_tok[j] = V(lambda e: e.tensor_scalar(UP[:, j, 15:271], UP[:, j, 15:271], 0.5, None, mult), v)
                tv.release(i, u_tok[j])
            return f

        conv_tok = [None] * 8
        cat_tok = [None] * 16

        def conv_gen():
            n = 0
            for j in range(8):
                while u_tok[j] is None:
                    yield
                o = COLS["w_dw"][0] + 31 * j
                k = V(lambda e, j=j, o=o: e.tensor_scalar(CA[j], UP[:, j, 0:256], CO[:, o:o + 1], col("b_dw", j), mult, add), u_tok[j], b2_free)
                for i in range(1, 31):
                    k = V(lambda e, i=i, j=j, o=o: e.scalar_tensor_tensor(CA[j], UP[:, j, i:i + 256], CO[:, o + i:o + i + 1], CA[j], mult, add), k)
                    n += 1
                    if n % CONV_STEP == 0:
                        yield
                conv_tok[j] = k
            bi, bk, fr = mbank.get()

            def sums(e):
                for j in range(8):
                    r = e.matmul(bk[:, 0:256], cn("ones"), CA[j], start=(j == 0), stop=(j == 7))
                return r
            m = P(sums, conv_tok[7], fr)
            k = V(lambda e: e.tensor_scalar(MEAN, bk[:, 0:256], 1.0 / 1024, None, mult), m, b2_free)
            mbank.release(bi, k)
            S = Stats(Sp.done)
            yield
            for j in range(8):
                conv_tok[j] = V(lambda e, j=j: e.tensor_tensor(CA[j], CA[j], MEAN, sub), k, m)
                S.square(CA[j], conv_tok[j])
                if j % 2:
                    yield
            yield
            r = S.finish(1024, 1e-5, r12_tok)
            ln["S"] = S
            yield
            for j in range(8):
                i, t, fr = tv.get()
                v = V(lambda e, j=j, t=t: e.scalar_tensor_tensor(t, CA[j], col("ln_g", j), RS[:, 0, :], mult, mult), r, fr)
                v = V(lambda e, j=j, t=t: e.tensor_scalar(t, t, col("ln_b", j), 0.5, add, mult), v)
                q, y, fy = te.get()
                a = A(lambda e, y=y, t=t: e.activation(y, t, ACT.Tanh), v, fy)
                v = V(lambda e, y=y, t=t: e.scalar_tensor_tensor(t, y, 1.0, t, add, mult), a)
                te.release(q, v)
                cat_tok[j] = split(H2, j, t, v, b2_free)
                tv.release(i, cat_tok[j])
                yield
        ln = {}
        CONV_STEP = 3
        cg = conv_gen()

        def xs_gen():
            for j in range(16):
                x_tok[j] = V(lambda e, j=j: e.scalar_tensor_tensor(X[:, j, :], X[:, j, :], col("final_norm", j), R1, mult, mult), r1_tok, u_tok2[j], acc2[0], x_tok[j])
                yield
        xg = xs_gen()
        for j in range(8):
            for _ in block(H1, u_tok2, 0, "w_in2", 0, j, e_a(j)):
                next(cg, None)
                next(xg, None)
            for _ in block(H1, u_tok2, 0, "w_in2", 0, 8 + j, e_g(j)):
                next(cg, None)
                next(xg, None)

        b_use = [b2_free] * 4
        bm_tok = {}

        def load_bias(i):
            s = i % 4
            d = D(f"b{s}", 16 * (i // 4 + 1), lambda e: e.dma_start(BB[s], bias_d[i]), b_use[s])
            bm_tok[i] = G(lambda e: e.tensor_tensor(BB[s], BB[s], cn("nm"), add), d)

        def e_r(ring, key):
            HD[key] = None

            def f(bk, tok, bi):
                i, t, fr = ring.get()
                HD[key] = (i, t, scaled_sum(t, bk, tok, bi, fr))
            return f

        def e_v(key):
            HD[key] = None

            def f(bk, tok, bi):
                i, t, fr = tv.get()
                k = scaled_sum(t, bk, tok, bi, fr)
                vi, vt, vf = vt_r.get()
                m, a = token_major(vt, t, k, vf)
                tv.release(i, m)
                HD[key] = (vi, vt, a)
            return f

        def na_scores(i, bk, fr):
            h, qb = divmod(i, 2)
            o = 64 * (h % 2)
            (qi, qn, qt), (ki, kn, kt) = need(HD, ("q", h // 2)), need(HD, ("k", h // 2))
            m = P(lambda e: e.matmul(bk[:, 0:256], qn[o:o + 64, 128 * qb:128 * qb + 128], kn[o:o + 64, :], start=True, stop=True), qt, kt, fr)
            if i % 4 == 3:
                qn_r.release(qi, m)
                kn_r.release(ki, m)
            return m

        def na_mask(i, p, ps, m, pf):
            s = i % 4
            v = V(lambda e: e.scalar_tensor_tensor(p, ps, 0.125, BB[s], mult, add), m, pf, bm_tok[i])
            b_use[s] = [v]
            if i + 3 < 32:
                load_bias(i + 3)
            return v

        def na_pv(i, t, a):
            h, qb = divmod(i, 2)
            o = 64 * (h % 2)
            if i % 4 == 0:
                av["b"] = mbank.get()
            bi, bk, fr = av["b"]
            vi, vt, vtok = need(HD, ("v", h // 2))

            def mm(e):
                for q in range(2):
                    r = e.matmul(bk[o:o + 64, 128 * qb:128 * qb + 128], vt[:, q, o:o + 64], t[:, 128 * q:128 * q + 128],
                                 start=(q == 0), stop=(q == 1))
                return r
            m = P(mm, a, vtok, fr if i % 4 == 0 else None)
            if i % 4 == 3:
                vt_r.release(vi, m)
                j = 8 + h // 2
                x = A(lambda e: e.activation(H2[:, j, 0:256], bk[:, 0:256], ACT.Copy), m, b2_free)
                cat_tok[j] = V(lambda e: e.tensor_tensor(H2[:, j, 256:512], bk[:, 0:256], H2[:, j, 0:256].bitcast(f32), sub), x)
                mbank.release(bi, cat_tok[j])
            return m

        def make2(j):
            for b, ev in ((16, e_r(qn_r, ("q", j))), (24, e_r(kn_r, ("k", j))), (32, e_v(("v", j)))):
                yield from block(H1, u_tok2, 0, "w_in2", 0, b + j, ev)

        for i in range(3):
            load_bias(i)
        stages = softmax_stages(na_scores, na_mask, lambda i: 256, na_pv)
        for _ in make2(0):
            next(cg, None)
        step = 0
        for j in range(1, 9):
            gen = make2(j) if j < 8 else iter(())
            for _ in range(6 if j < 8 else 4 + 3):
                next(gen, None)
                next(cg, None)
                if step < 4 * j or j == 8:
                    pipe_step(stages, step, 32)
                    step += 1
            run(gen)
        run(cg)

        Y = [B2[:, i, :] for i in range(16)]
        y_free = now()
        y_tok = [None] * 16
        S = Stats(ln["S"].done)

        def ev_y(ci, j, last):
            def f(bk, tok, bi):
                if ci == 0:
                    y_tok[j] = raw_sum(Y[j], bk, tok, bi, y_free)
                else:
                    i, t, fr = tv.get()
                    k = raw_sum(t, bk, tok, bi, fr)
                    y_tok[j] = V(lambda e: e.tensor_tensor(Y[j], Y[j], t, add), k, y_tok[j])
                    tv.release(i, y_tok[j])
                if last:
                    S.square(Y[j], y_tok[j])
            return f
        for j in range(16):
            run(block(H2, cat_tok, 0, "w_out2", 0, j, ev_y(0, j, True)))
        flush(True)
        rs_tok = S.finish(2048, 1e-6, now())
        Sp = S

        def post(name, rs_tok, then):
            out = []
            for j in range(16):
                k = V(lambda e, j=j: e.scalar_tensor_tensor(Y[j], Y[j], col(name, j), RS[:, 0, :], mult, mult), rs_tok)
                x_tok[j] = V(lambda e, j=j: e.tensor_tensor(X[:, j, :], X[:, j, :], Y[j], add), k, x_tok[j])
                out.append(x_tok[j])
                then(j)
            return out
        S = Stats(Sp.done)
        h1_free = ("pe", count["pe"])
        h_tok = [None] * 16

        def to_mlp(j):
            S.square(X[:, j, :], x_tok[j])
            g = col("pre_mlp", j)
            a = A(lambda e: e.activation(H1[:, j, 0:256], X[:, j, :], ACT.Copy, scale=g), x_tok[j], h1_free)
            h_tok[j] = V(lambda e: e.scalar_tensor_tensor(H1[:, j, 256:512], X[:, j, :], g, H1[:, j, 0:256].bitcast(f32), mult, sub), a)
        post("post_mix", rs_tok, to_mlp)
        rx_tok = S.finish(2048, 1e-6, x_tok[15])
        Sp = S

        y_free = now()
        h2_free = [now()]
        S = Stats(Sp.done)

        def up2(i, s, f_tok):
            def e1(bk, tok, bi):
                q, t, fr = tv.get()
                k = raw_sum(t, bk, tok, bi, fr)
                v = V(lambda e: e.scalar_tensor_tensor(t, t, 0.0, RS[:, 0, :], ALU.max, mult), k, rx_tok)
                v = V(lambda e: e.tensor_tensor(t, t, t, mult), v)
                f_tok[s] = split(H2, s, t, v, h2_free[0])
                tv.release(q, f_tok[s])
            yield from block(H1, h_tok, 0, "w_up2", 0, i, e1)

        def evd2(ci, j):
            return ev_y(ci, j, ci == 3)
        ffn((16, 16, 16, 16), up2, "w_down2", evd2, 64)
        rs_tok = S.finish(2048, 1e-6, now())
        toks = post("post_mlp", rs_tok, lambda j: None)
        for i in range(4):
            tk = D("out", 16 * i + 16, lambda e, i=i: e.dma_start(out[:, 4 * i:4 * i + 4, :], X[:, 4 * i:4 * i + 4, :]), toks[4 * i + 3])
        assert st["tile"] == N_TILES, st
        while st["proc"] < len(kinds):
            proc_next()

        block_ = ctx.enter_context(nc.Block())

        def play(name, e):
            seen = {}
            for fn, waits, inc in queue[name]:
                need = {}
                for s, v in waits:
                    need[s] = max(need.get(s, 0), v)
                for s, v in need.items():
                    if seen.get(s, 0) < v:
                        e.wait_ge(sems[s], v)
                        seen[s] = v
                r = fn(e)
                if inc is None:
                    r.then_inc(sems[name], 1)
                else:
                    r.then_inc(sems[inc], 16)

        @block_.sync
        def _(e):
            play("sp", e)
            e.wait_ge(sems["out"], 64)

        @block_.scalar
        def _(e):
            play("act", e)

        @block_.vector
        def _(e):
            play("dve", e)

        @block_.gpsimd
        def _(e):
            play("pool", e)

        @block_.tensor
        def _(e):
            play("pe", e)


def kernel(**inp):
    import concourse.bacc as _bacc
    from concourse import mybir as mb
    from concourse.bass_utils import run_bass_kernel_spmd as _run
    I = {k: np.asarray(v) for k, v in inp.items()}

    def feat(v):
        return v.reshape(-1, 128).T
    w_in = I["w_in"][0]
    kpe = w_in[:, 1024:1088]
    ba = w_in[:, 5184:5200]
    pad = np.zeros((2048, 112), np.float32)
    W = {"w_in": np.concatenate([w_in[:, 0:1024], kpe, kpe, w_in[:, 1088:5184], ba, pad, w_in[:, 5200:9296]], axis=1)}
    uq = I["w_uq"][0].reshape(512, 8, 192)
    W["w_uq"] = np.concatenate([uq[:, :, 0:128].reshape(512, 1024), uq[:, :, 128:192].reshape(512, 512)], axis=1)
    ukv = I["w_ukv"][0].reshape(512, 8, 256)
    W["w_ukv"] = np.concatenate([ukv[:, :, 0:128].reshape(512, 1024), ukv[:, :, 128:256].reshape(512, 1024)], axis=1)
    for a, b in (("w_o_mla", "w_o_mla"), ("w_o_gdn", "w_o_gdn"), ("w_o", "w_o"), ("w_gate_up", "w_gate_up"), ("w_down", "w_down"),
                 ("w_in2", "w_in_2"), ("w_out2", "w_out_2"), ("w_up2", "w_up_2"), ("w_down2", "w_down_2")):
        W[a] = I[b][0]
    cols = np.zeros((128, NCOLS), np.float32)

    def put(name, v):
        o, w = COLS[name]
        cols[:, o:o + w] = v
    put("c", feat(I["c"][0]))
    put("b_ada", feat(I["b_ada"][0]))
    put("norm_mix", feat(I["norm_mix"][0]))
    put("norm_ffn", feat(I["norm_ffn"][0]))
    put("q_a_norm", feat(I["q_a_norm"][0]))
    put("kv_a_norm", feat(I["kv_a_norm"][0]))
    put("conv_w", I["conv_w"][0].reshape(4, 24, 128).transpose(2, 1, 0).reshape(128, 96))
    put("gdn_norm", I["gdn_norm"][0][:, None])
    put("final_norm", feat(I["final_norm"]))
    put("pre_mix", feat(I["pre_mix_g_2"][0]))
    put("post_mix", feat(I["post_mix_g_2"][0]))
    put("pre_mlp", feat(I["pre_mlp_g_2"][0]))
    put("post_mlp", feat(I["post_mlp_g_2"][0]))
    put("w_dw", I["w_dw_2"][0].reshape(31, 8, 128).transpose(2, 1, 0).reshape(128, 248))
    put("b_dw", feat(I["b_dw_2"][0]))
    put("ln_g", feat(I["conv_ln_g_2"][0]))
    put("ln_b", feat(I["conv_ln_b_2"][0]))
    put("A_log", np.broadcast_to(I["A_log"][0][None, :], (128, 8)))
    put("dt_bias", np.broadcast_to(I["dt_bias"][0][None, :], (128, 8)))
    wada = np.ascontiguousarray(I["w_ada"][0].reshape(16, 128, 12, 1024).transpose(2, 0, 1, 3)).reshape(N_ADA, 128, 1024)
    r = np.arange(4)
    c = np.arange(64)
    dr = r[None, :] - r[:, None] + 7
    dc = np.clip(c[None, :] - c[:, None], -15, 15) + 15
    bias = I["rpb_2"][0][:, dr[:, None, :, None], dc[None, :, None, :]].reshape(32, 128, 256)

    arrays = {
        "xT": np.ascontiguousarray(I["x"][0].T.reshape(16, 128, 256).transpose(1, 0, 2)),
        "pos": I["positions"][0], "cols": cols, "consts": const_array(), "wada": wada, "bias": np.ascontiguousarray(bias),
    }
    nc = _bacc.Bacc("TRN2", target_bir_lowering=False, num_devices=1)
    aps = {n: nc.dram_tensor(n + "_dram", a.shape, mb.dt.from_np(a.dtype), kind="ExternalInput").ap() for n, a in arrays.items()}
    wst = nc.dram_tensor("wst_dram", (N_TILES // 8, 128, 1024), mb.dt.float32, kind="ExternalInput").ap()
    out = nc.dram_tensor("out_dram", (128, 16, 256), mb.dt.float32, kind="ExternalOutput").ap()
    log = []
    program(nc, aps["xT"], aps["pos"], aps["cols"], aps["consts"], aps["wada"], wst, aps["bias"], out, log)
    ws = np.empty((N_TILES // 8, 128, 1024), np.float32)
    for i, (name, k, n) in enumerate(log):
        ws[i // 8, :, 128 * (i % 8):128 * (i % 8) + 128] = W[name][128 * k:128 * k + 128, 128 * n:128 * n + 128]
    ins = {n + "_dram": a for n, a in arrays.items()}
    ins["wst_dram"] = ws
    res = _run(nc, [ins], core_ids=[0])
    o = res.results[0]["out_dram"]
    return np.ascontiguousarray(o.transpose(1, 0, 2).reshape(2048, 256).T).reshape(1, 256, 2048)
```

```python
import numpy as np
import concourse.bass as bass
from concourse import mybir
from contextlib import ExitStack

T = 256
NRAW, NHL = 5, 3
LAG, EVLAG = 3, 4
AHEAD0, EVLAG0 = 2, 4
N_TILES = 6864
N_ADA = 192
WOUT_ORDER = [8, 9, 10, 11, 12, 13, 14, 0, 1, 2, 3, 4, 5, 6, 7, 15]
ADA_START = 30
ADA_ORDER = (2, 0, 3, 1, 4, 5, 6, 7, 8, 9, 10, 11)
HALF_BLOCKS = 22
EARLY, PAIRS = 8, 0
X_AT, ADALN_AT = 2, 13

COLS = {}
_n = 0
for _name, _w in (("c", 16), ("b_ada", 96), ("norm_mix", 16), ("norm_ffn", 16), ("q_a_norm", 4), ("kv_a_norm", 4),
                  ("conv_w", 96), ("gdn_norm", 1), ("final_norm", 16), ("pre_mix", 16), ("post_mix", 16),
                  ("pre_mlp", 16), ("post_mlp", 16), ("w_dw", 248), ("b_dw", 8), ("ln_g", 8), ("ln_b", 8),
                  ("A_log", 8), ("dt_bias", 8)):
    COLS[_name] = (_n, _w)
    _n += _w
NCOLS = _n

CONSTS = {}
_n = 0
for _name, _w in (("ident", 128), ("ones", 128), ("tri", 128), ("ch", 128), ("lm", 768), ("mm", 256), ("nm", 256),
                  ("rot", 128), ("invf", 1), ("slide", 15)):
    CONSTS[_name] = (_n, _w)
    _n += _w
NCONST = _n


def const_array():
    a = np.zeros((128, NCONST), np.float32)

    def put(name, v):
        o, w = CONSTS[name]
        a[:, o:o + w] = v
    s = np.arange(128)[:, None]
    c = np.arange(128)[None, :]
    put("ident", s == c)
    put("ones", 1.0)
    same = (s // 64) == (c // 64)
    put("tri", (s <= c) & same)
    put("ch", same)
    put("lm", np.concatenate([((c // k) % 2 == 1) & ((s // k) == (c // k) - 1) for k in (1, 2, 4, 8, 16, 32)], axis=1))
    k = np.arange(256)[None, :]
    put("mm", np.where(k <= 128 + s, 0.0, -1e30))
    start = np.clip(s % 64 - 8, 0, 48)
    put("nm", np.where((k % 64 >= start) & (k % 64 < start + 16), 0.0, -1e30))
    rot = np.zeros((128, 128), np.float32)
    for b in (0, 64):
        for j in range(32):
            rot[b + 32 + j, b + j] = -1.0
            rot[b + j, b + 32 + j] = 1.0
    put("rot", rot)
    put("slide", np.arange(15)[None, :] == 7)
    inv = (np.float32(1.0) / (np.float32(10000.0) ** (np.arange(0, 64, 2, dtype=np.float32) / np.float32(64)))).astype(np.float32)
    put("invf", inv[np.arange(128) % 32][:, None])
    return a


def program(nc, xT, pos, cols_d, consts_d, wada, wst, bias_d, out, log):
    f32 = mybir.dt.float32
    f32r = mybir.dt.float32r
    i32 = mybir.dt.int32
    ALU = mybir.AluOpType
    ACT = mybir.ActivationFunctionType
    AX = mybir.AxisListType.X
    add, sub, mult = ALU.add, ALU.subtract, ALU.mult
    ctx = ExitStack()
    with ctx:
        def sb(name, shape, dt=f32):
            return ctx.enter_context(nc.sbuf_tensor(name, shape, dt))

        RAW = sb("RAW", [128, NRAW, 1024])
        HI = sb("HI", [128, NHL, 1024], f32r)
        LO = sb("LO", [128, NHL, 1024], f32r)
        H1 = sb("H1", [128, 16, 512], f32r)
        H2 = sb("H2", [128, 16, 512], f32r)
        CO = sb("CO", [128, NCOLS])
        CN = sb("CN", [128, NCONST])
        MOD = sb("MOD", [128, 96])
        SC = sb("SC", [128, 256])
        TV = sb("TV", [128, 4, 256])
        TE = sb("TE", [128, 3, 256])
        RS = sb("RS", [128, 3, 256])
        SQ = sb("SQ", [128, 2, 256])
        ADA = sb("ADA", [128, 1024])
        X = sb("X", [128, 16, 256])
        B1 = sb("B1", [128, 24, 256])
        B2 = sb("B2", [128, 24, 256])
        B3 = sb("B3", [128, 8, 256])
        BANK = [ctx.enter_context(nc.psum_tensor(f"BK{i}", [128, 512], f32)) for i in range(8)]

        def sem(name):
            return ctx.enter_context(nc.semaphore(name))

        ENG = ("pe", "act", "dve", "pool", "sp")
        sems = {e: sem("s_" + e) for e in ENG}
        for i in range(NRAW):
            sems[f"r{i}"] = sem(f"s_raw{i}")
        for i in range(4):
            sems[f"b{i}"] = sem(f"s_bias{i}")
        for n in ("cols", "consts", "x", "pos", "x2", "out"):
            sems[n] = sem("s_" + n)
        queue = {e: [] for e in ENG}
        count = {e: 0 for e in ENG}

        def put(e, fn, waits):
            flat = []
            for w in waits:
                flat += w if isinstance(w, list) else [w] if w is not None else []
            queue[e].append((fn, flat, None))
            count[e] += 1
            return (e, count[e])

        def V(fn, *waits):
            return put("dve", fn, waits)

        def A(fn, *waits):
            return put("act", fn, waits)

        def G(fn, *waits):
            return put("pool", fn, waits)

        def P(fn, *waits):
            return put("pe", fn, waits)

        def D(name, value, fn, *waits):
            flat = []
            for w in waits:
                flat += w if isinstance(w, list) else [w] if w is not None else []
            queue["sp"].append((fn, flat, name))
            return (name, value)

        def now():
            return [(e, count[e]) for e in ("pe", "act", "dve", "pool")]

        def col(name, j=0, w=1):
            return CO[:, COLS[name][0] + j:COLS[name][0] + j + w]

        def cn(name, a=0, b=None):
            o, w = CONSTS[name]
            return CN[:, o + a:o + (w if b is None else b)]

        class Ring:
            def __init__(self, items):
                self.items = items
                self.free = [[] for _ in items]
                self.idle = list(range(len(items)))

            def get(self):
                while not self.idle:
                    force()
                i = self.idle.pop(0)
                return i, self.items[i], self.free[i]

            def release(self, i, *toks):
                self.free[i] = list(toks)
                assert i not in self.idle
                self.idle.append(i)

        tv = Ring([TV[:, i, :] for i in range(4)])
        te = Ring([TE[:, i, :] for i in range(3)])
        lbank = Ring(BANK[0:3])
        mbank = Ring(BANK[3:8])

        tk_cols = D("cols", 16, lambda e: e.dma_start(CO[:, :], cols_d))
        raw_free = [[] for _ in range(NRAW)]
        kinds = ["A"] * (32 + EARLY)
        a = 32 + EARLY
        for i in range(N_TILES // 8):
            if i < PAIRS or a < 64:
                kinds += ["A", "A"][0:64 - a]
                a = min(a + 2, 64)
            elif i >= ADA_START and i % 2 == 0 and a < N_ADA:
                kinds.append("A")
                a += 1
            kinds.append("L")
        lin_at = [i for i, k in enumerate(kinds) if k == "L"]
        st = {"load": 0, "proc": 0, "na": 0, "nl": 0, "la": 0, "ll": 0, "tile": 0, "ahead": AHEAD0, "evlag": EVLAG0}
        split_tok = {}
        unit_pe = {}
        mod_tok = [None] * 12
        ada_last = [None]
        ada_pe = [None] * 12

        def load_next():
            s = st["load"]
            if s >= len(kinds):
                return
            slot = s % NRAW
            if kinds[s] == "A":
                src = wada[16 * ADA_ORDER[st["la"] // 16] + st["la"] % 16]
                st["la"] += 1
            else:
                src = wst[st["ll"]]
                st["ll"] += 1
            D(f"r{slot}", 16 * (s // NRAW + 1), lambda e: e.dma_start(RAW[:, slot, :], src), *raw_free[slot])
            st["load"] += 1

        def proc_next():
            s = st["proc"]
            slot = s % NRAW
            got = (f"r{slot}", 16 * (s // NRAW + 1))
            if kinds[s] == "A":
                i = st["na"]
                st["na"] += 1
                j, t = divmod(i, 16)
                acc = ADA[:, :] if j % 2 == 0 or j >= 4 else B2[:, 20:24, :].rearrange("p a t -> p (a t)")
                if t == 0:
                    before = j - 2 if j <= 4 else j - 1
                    free = need(ada_pe, before) if before >= 0 else None
                    k = V(lambda e: e.tensor_scalar(acc, RAW[:, slot, :], SC[:, 0:1], None, mult), got, c_tok, free)
                else:
                    k = V(lambda e: e.scalar_tensor_tensor(acc, RAW[:, slot, :], SC[:, t:t + 1], acc, mult, add),
                          got, ada_last[0])
                ada_last[0] = k
                raw_free[slot] = [k]
                if t == 15:
                    o = ADA_ORDER[j]

                    def ev():
                        bi, bk, fr = mbank.get()

                        def mm(e):
                            for q in range(8):
                                r = e.matmul(bk[:, q:q + 1], acc[:, q * 128:q * 128 + 128], cn("ones", 0, 1), start=True, stop=True)
                            return r
                        m = P(mm, k, fr, tk_consts)
                        ada_pe[j] = m
                        yield
                        mod_tok[o] = V(lambda e: e.tensor_tensor(MOD[:, 8 * o:8 * o + 8], bk[:, 0:8], col("b_ada", 8 * o, 8), add), m, tk_cols)
                        mbank.release(bi, mod_tok[o])
                    later(ev(), 3)
            else:
                u = st["nl"]
                st["nl"] += 1
                h = u % NHL
                k2 = V(lambda e: e.tensor_tensor(LO[:, h, :], RAW[:, slot, :], HI[:, h, :].bitcast(f32), sub), hi_tok[u], unit_pe.get(u - NHL))
                split_tok[u] = k2
                raw_free[slot] = [k2]
            st["proc"] += 1
            load_next()

        hi_tok = {}

        def hi_part(u):
            s = lin_at[u]
            slot = s % NRAW
            hi_tok[u] = A(lambda e: e.activation(HI[:, u % NHL, :], RAW[:, slot, :], ACT.Copy), (f"r{slot}", 16 * (s // NRAW + 1)), unit_pe.get(u - NHL))

        def feed(u):
            u = min(u, len(lin_at) - 1)
            for v in range(len(hi_tok), u + 1):
                hi_part(v)
            while st["proc"] <= lin_at[u]:
                proc_next()
            v = len(hi_tok)
            if v <= u + 1 and v < len(lin_at) and st["load"] > lin_at[v] and (v < NHL or v - NHL in unit_pe):
                hi_part(v)

        pending = []
        busy = []

        def later(gen, lag=0):
            pending.append([st["tile"] + lag, gen])

        def take(p):
            busy.append(p)
            try:
                next(p[1])
                p[0] = st["tile"] + LAG
            except StopIteration:
                pending.remove(p)
            busy.remove(p)

        def flush():
            for p in list(pending):
                if p[0] <= st["tile"] and p in pending and p not in busy:
                    take(p)

        def force():
            todo = [p for p in pending if p not in busy]
            assert todo
            for p in todo:
                if p in pending and p not in busy:
                    take(p)

        def need(lst, i):
            while lst[i] is None:
                force()
            return lst[i]

        def stagger(gens, width=3):
            active = []
            gens = list(gens)
            while gens or active:
                if gens and len(active) < width:
                    active.append(gens.pop(0))
                for g in list(active):
                    try:
                        next(g)
                    except StopIteration:
                        active.remove(g)
                yield

        def blocks(H, toks, k0, wname, kbase, outs, order=None):
            K = len(toks)
            banks = []
            for g in range(len(outs)):
                ring = lbank if g < 3 else mbank
                bi, bk, fr = ring.get()
                banks.append(((ring, bi), bk, fr))
            for c, k in enumerate(order or range(K)):
                for g, (n, evac) in enumerate(outs):
                    own, bk, fr = banks[g]
                    t = st["tile"]
                    st["tile"] += 1
                    log.append((wname, kbase + k, n))
                    u, q = divmod(t, 8)
                    if q == 0:
                        feed(u)

                    def mm(e, k=k, c=c, u=u, q=q, bk=bk):
                        hh = HI[:, u % NHL, q * 128:q * 128 + 128]
                        ll = LO[:, u % NHL, q * 128:q * 128 + 128]
                        e.matmul(bk[:, :], hh, H[:, k0 + k, :], start=(c == 0), stop=False, skip_group_check=True)
                        return e.matmul(bk[:, 256:512], ll, H[:, k0 + k, 0:256], start=False, stop=(c == K - 1), skip_group_check=True)
                    tok = P(mm, split_tok[u], need(toks, k), fr if c == 0 else None)
                    if c == K - 1:
                        later(evac(bk, tok, own), st["evlag"])
                    if q == 7:
                        unit_pe[u] = tok
                        feed(u + st["ahead"])
                        flush()
                        yield
                    elif q % 2 == 1:
                        flush()
            if q != 7:
                yield

        def block(H, toks, k0, wname, kbase, n, evac):
            return blocks(H, toks, k0, wname, kbase, [(n, evac)])

        def raw_sum(dst, bk, tok, own, *waits, scale=None, part=None):
            i, t, fr = te.get()
            a = A(lambda e: e.activation(t, bk[:, 256:512], ACT.Copy, scale=1.0 if scale is None else scale), tok, fr)
            yield
            if part is not None:
                a = G(lambda e: e.tensor_tensor(t, t, part[0], add), a, part[1])
                yield
            if scale is None:
                v = V(lambda e: e.tensor_tensor(dst, bk[:, 0:256], t, add), a, *waits)
            else:
                v = V(lambda e: e.scalar_tensor_tensor(dst, bk[:, 0:256], scale, t, mult, add), a, *waits)
            te.release(i, v)
            own[0].release(own[1], v)
            return v

        def split(dst, j, src, tok, *waits, bias=None, scale=None):
            hi, lo = dst[:, j, 0:256], dst[:, j, 256:512]
            if bias is not None:
                a = A(lambda e: e.activation(hi, src, ACT.Identity, bias=bias), tok, *waits)
            else:
                a = A(lambda e: e.activation(hi, src, ACT.Copy, scale=1.0 if scale is None else scale), tok, *waits)
            yield
            if bias is not None:
                return V(lambda e: e.scalar_tensor_tensor(lo, src, bias, hi.bitcast(f32), add, sub), a)
            if scale is not None:
                return V(lambda e: e.scalar_tensor_tensor(lo, src, scale, hi.bitcast(f32), mult, sub), a)
            return V(lambda e: e.tensor_tensor(lo, src, hi.bitcast(f32), sub), a)

        def run_pending():
            while pending:
                force()

        def run(gen):
            for _ in gen:
                pass

        def rsqrt_steps(y, t, src, scale, eps, *waits):
            k = V(lambda e: e.tensor_scalar(t, src, scale, eps, mult, add), *waits)
            yield
            a = A(lambda e: e.activation(y, t, ACT.Ln), k)
            a = A(lambda e: e.activation(y, y, ACT.Exp, scale=-0.5), a)
            yield
            k = V(lambda e: e.tensor_tensor(t, t, y, mult), a)
            k = V(lambda e: e.tensor_tensor(t, t, y, mult), k)
            k = V(lambda e: e.tensor_scalar(t, t, -0.5, 1.5, mult, add), k)
            return V(lambda e: e.tensor_tensor(y, y, t, mult), k)

        def whole(gen):
            while True:
                try:
                    next(gen)
                except StopIteration as end:
                    return end.value

        def rsqrt(*a):
            return whole(rsqrt_steps(*a))

        class Stats:
            def __init__(self, *waits):
                self.last = list(waits)
                self.first = True
                self.done = None
                self.tail = None
                self.n = 0

            def square(self, src, tok, final=False):
                if final:
                    self.tail = A(lambda e: e.activation(SQ[:, 1, :], src, ACT.Square), tok, self.last)
                    self.last = self.last + [self.tail]
                    return self.tail
                if self.first:
                    k = A(lambda e: e.activation(SQ[:, 0, :], src, ACT.Square), tok, self.last)
                    self.first = False
                    self.read = [self.last, self.last]
                else:
                    p = self.n % 2
                    self.n += 1
                    k = A(lambda e: e.activation(B3[:, 6 + p, :], src, ACT.Square), tok, self.read[p])
                    k = G(lambda e: e.tensor_tensor(SQ[:, 0, :], SQ[:, 0, :], B3[:, 6 + p, :], add), k, self.last)
                    self.read[p] = [k]
                self.last = [k]
                return k

            def finish_steps(self, n, eps, *waits, y=None):
                bi, bk, fr = mbank.get()

                def mm(e):
                    r = e.matmul(bk[:, 0:256], cn("ones"), SQ[:, 0, :], start=True, stop=self.tail is None)
                    if self.tail is not None:
                        r = e.matmul(bk[:, 0:256], cn("ones"), SQ[:, 1, :], start=False, stop=True)
                    return r
                m = P(mm, self.last, fr)
                self.done = m
                yield
                v = yield from rsqrt_steps(RS[:, 0, :] if y is None else y, RS[:, 1, :], bk[:, 0:256], 1.0 / n, eps, m, *waits)
                mbank.release(bi, v)
                return v

            def finish(self, *a, **k):
                return whole(self.finish_steps(*a, **k))

        for _ in range(NRAW):
            load_next()
        tk_consts = D("consts", 16, lambda e: e.dma_start(CN[:, :], consts_d))
        PI = B3[:, 1, :].bitcast(i32)
        k = A(lambda e: e.activation(SC[:, 16:32], col("c", 0, 16), ACT.Sigmoid), tk_cols)
        c_tok = V(lambda e: e.tensor_tensor(SC[:, 0:16], SC[:, 16:32], col("c", 0, 16), mult), k)
        dw_tok = V(lambda e: e.tensor_scalar(col("w_dw", 0, 248), col("w_dw", 0, 248), 0.5, None, mult), tk_cols)
        cw_tok = V(lambda e: e.tensor_scalar(col("conv_w", 0, 96), col("conv_w", 0, 96), 0.5, None, mult), tk_cols)
        for s in range(X_AT):
            proc_next()
        for i in range(4):
            tk_x = D("x", 16 * i + 16, lambda e, i=i: e.dma_start(X[:, 4 * i:4 * i + 4, :], xT[:, 4 * i:4 * i + 4, :]))
        tk_pos = D("pos", 16, lambda e: e.dma_start(PI, pos.rearrange("(a n) -> a n", a=1).broadcast_to([128, 256])))
        S1 = Stats(tk_x)
        for j in range(16):
            S1.square(X[:, j, :], None)
        for s in range(X_AT, 28):
            proc_next()
        fin = S1.finish_steps(2048, 1e-6)
        next(fin)
        proc_next()
        next(fin)
        proc_next()
        proc_next()
        rs_tok = whole(fin)
        proc_next()

        COS, SIN = B3[:, 2, :], B3[:, 3, :]
        F = B3[:, 4, :]
        Q = B3[:, 5, :]
        rot_tok = [None]

        def rotary():
            k = V(lambda e: e.tensor_copy(F, PI), tk_pos, tk_consts)
            k = V(lambda e: e.tensor_scalar(F, F, cn("invf"), None, mult), k)
            k = V(lambda e: e.tensor_scalar(Q, F, float(1.0 / (2 * np.pi)), 12582912.0, mult, add), k)
            k = V(lambda e: e.tensor_scalar(Q, Q, 12582912.0, None, sub), k)
            rest = 2 * np.pi
            parts = []
            for bits in (8, 8, 8, 24):
                step = 2.0 ** (np.floor(np.log2(rest)) - bits + 1)
                p = float(np.floor(rest / step) * step)
                parts.append(p)
                rest = rest - p
            for p in parts:
                yield
                k = V(lambda e, p=p: e.scalar_tensor_tensor(F, Q, -p, F, mult, add), k)
            PIF = 3.1415925
            k = V(lambda e: e.tensor_scalar(F, F, PIF, -PIF, ALU.min, ALU.max), k)
            yield
            a1 = A(lambda e: e.activation(SIN, F, ACT.Sin), k)
            yield
            k = V(lambda e: e.scalar_tensor_tensor(Q, F, -1.0, F, mult, ALU.max), k)
            k = V(lambda e: e.tensor_scalar(Q, Q, -1.0, float(np.pi / 2), mult, add), k)
            rot_tok[0] = A(lambda e: e.activation(COS, Q, ACT.Sin), k, a1)

        def adaln(shift, scale, normname, S_tok, xtoks, out, js, *waits):
            a, b = js[0], js[-1] + 1
            m = [need(mod_tok, 2 * c + j // 8) for c in (shift, scale) for j in (a, b - 1)]
            g = V(lambda e: e.scalar_tensor_tensor(SC[:, 32 + a:32 + b], MOD[:, 16 * scale + a:16 * scale + b], 1.0, col(normname, a, b - a), add, mult),
                  m, tk_cols, *waits)

            def one(j):
                i, t, fr = tv.get()
                k = V(lambda e: e.scalar_tensor_tensor(t, X[:, j, :], SC[:, 32 + j:33 + j], RS[:, 0, :], mult, mult),
                      g, S_tok, xtoks[j], fr)
                yield
                out[j] = yield from split(H1, j, t, k, *waits, bias=MOD[:, 16 * shift + j:16 * shift + j + 1])
                tv.release(i, out[j])
            yield from stagger(one(j) for j in js)

        h_tok = [None] * 16
        for n, _ in enumerate(adaln(0, 1, "norm_mix", rs_tok, [tk_x] * 16, h_tok, range(8))):
            if n < EARLY:
                proc_next()

        HALF = [(j, B2[:, j, :]) for j in range(8)] + [(8, B2[:, 8, :]), (41, B2[:, 9, :])]
        HALF += [(9 + j, B1[:, j, :]) for h in range(4) for j in (8 + h, h, 16 + h)]
        assert len(HALF) == HALF_BLOCKS
        half_tok = {n: None for n, _ in HALF}
        later(rotary())

        def ev_half(n, dst):
            def f(bk, tok, own):
                half_tok[n] = yield from raw_sum(dst, bk, tok, own)
            return f
        run(blocks(H1, h_tok[0:8], 0, "w_in", 0, [(n, ev_half(n, d)) for n, d in HALF[0:5]]))
        for i, (n, d) in enumerate(HALF[5:]):
            if i == ADALN_AT:
                second = adaln(0, 1, "norm_mix", rs_tok, [tk_x] * 16, h_tok, range(8, 16))
            run(block(H1, h_tok[0:8], 0, "w_in", 0, n, ev_half(n, d)))
            if i >= ADALN_AT:
                for _ in range(3):
                    next(second, None)
        run(second)

        st["ahead"], st["evlag"] = 2, EVLAG

        tk_cos = need(rot_tok, 0)

        def half_of(n):
            return dict(HALF)[n], need(half_tok, n)

        x_read = now()
        CQ = [X[:, i, :] for i in range(8)]
        KPE = B3[:, 0, :]
        RN = {"kpe": None}

        def rope(dst, src, tok, *waits):
            yield
            bi, bk, fr = mbank.get()
            m = P(lambda e: e.matmul(bk[:, 0:256], cn("rot"), src, start=True, stop=True), tok, fr)
            i, t, fr2 = tv.get()
            v2 = V(lambda e: e.tensor_tensor(dst, src, COS, mult), m, *waits)
            yield
            v1 = V(lambda e: e.tensor_tensor(t, bk[:, 0:256], SIN, mult), m, tk_cos, fr2)
            v = V(lambda e: e.tensor_tensor(dst, dst, t, add), v1, v2)
            mbank.release(bi, v1)
            tv.release(i, v)
            return v

        cq_tok = [None] * 8
        SQS = [Stats(S1.done), None]

        def ev_c(j):
            def f(bk, tok, bi):
                cq_tok[j] = yield from raw_sum(CQ[j], bk, tok, bi, x_read, part=half_of(j))
                if j == 4:
                    while SQS[0].done is None:
                        force()
                    SQS[1] = Stats(*SQS[0].last, SQS[0].done)
                SQS[j // 4].square(CQ[j], cq_tok[j])
                if j % 4 == 3:
                    yield
                    yield from cnorm(j // 4)
            return f

        H2_tok = [None] * 16

        def cnorm(half):
            k = yield from SQS[half].finish_steps(512, 1e-6, *([h_tok[-1]] if half == 0 else [need(H2_tok, 3)]))
            name = "q_a_norm" if half == 0 else "kv_a_norm"
            for j in range(4):
                i, t, fr = tv.get()
                c = V(lambda e, j=j, t=t: e.scalar_tensor_tensor(t, CQ[4 * half + j], col(name, j), RS[:, 0, :], mult, mult), k, fr)
                yield
                H2_tok[4 * half + j] = yield from split(H2, 4 * half + j, t, c)
                tv.release(i, H2_tok[4 * half + j])

        def ev_kpe(bk, tok, bi):
            k = yield from raw_sum(KPE, bk, tok, bi, part=half_of(8))
            RN["kpe"] = yield from rope(KPE, KPE, k)

        qkv_tok = [None] * 24
        lin_tok = {"ba": None}

        def ev_qkv(j):
            def f(bk, tok, bi):
                dst = B1[:, j, :]
                i, t, fr = tv.get()
                k = yield from raw_sum(t, bk, tok, bi, fr, part=half_of(9 + j) if j % 8 < 4 else None)
                yield
                o = COLS["conv_w"][0] + 4 * j
                v = V(lambda e: e.tensor_scalar(dst, t, CO[:, o + 3:o + 4], None, mult), k, cw_tok)
                for s in (1, 2, 3):
                    v = V(lambda e, s=s: e.scalar_tensor_tensor(dst[:, s:256], t[:, 0:256 - s], CO[:, o + 3 - s:o + 4 - s], dst[:, s:256], mult, add), v)
                s1 = A(lambda e: e.activation(t, dst, ACT.Tanh), v)
                yield
                v = V(lambda e: e.scalar_tensor_tensor(dst, t, 1.0, dst, add, mult), s1)
                tv.release(i, v)
                qkv_tok[j] = v
            return f

        BA = B3[:, 4, :]

        def ev_ba(bk, tok, bi):
            lin_tok["ba"] = yield from raw_sum(BA, bk, tok, bi, tk_cos, part=half_of(41))

        h_hi = h_tok[8:16]
        run(blocks(H1, h_hi, 8, "w_in", 8, [(j, ev_c(j)) for j in range(4)]))
        for j in range(4, 8):
            run(block(H1, h_hi, 8, "w_in", 8, j, ev_c(j)))
        run(block(H1, h_hi, 8, "w_in", 8, 8, ev_kpe))
        run(block(H1, h_hi, 8, "w_in", 8, 41, ev_ba))

        GS = B3[:, 5, :]

        def gs(o, w=16):
            return GS[:, o:o + w]
        BA_T, BETA, SPX, SPE, GG, GC, GL, BG, DK = (gs(0, 32), gs(32), gs(48), gs(64), gs(80), gs(96), gs(112), gs(128), gs(144))
        EA = GS[:, 160:168]

        def m28(x):
            return x.rearrange("p (m h) -> p m h", m=2)

        def scalars():
            bi, bk, fr = mbank.get()

            def trba(e):
                for m in range(2):
                    r = e.transpose(bk[:, 16 * m:16 * m + 16], BA[0:16, 128 * m:128 * m + 128], CN[0:16, 0:16])
                return r
            m = P(trba, need(lin_tok, "ba"), fr)
            yield
            k = V(lambda e: e.tensor_copy(BA_T, bk[:, 0:32]), m, tk_cos)
            mbank.release(bi, k)
            bat = BA_T.rearrange("p (m h) -> p m h", m=2)
            a1 = A(lambda e: e.activation(m28(BETA), bat[:, :, 0:8], ACT.Sigmoid), k)
            k = V(lambda e: e.tensor_tensor(m28(SPX), bat[:, :, 8:16], col("dt_bias", 0, 8).unsqueeze(1).broadcast_to([128, 2, 8]), add), k)
            k2 = V(lambda e: e.scalar_tensor_tensor(SPE, SPX, -1.0, SPX, mult, ALU.max), k)
            a = A(lambda e: e.activation(SPE, SPE, ACT.Exp, scale=-1.0), k2)
            a = A(lambda e: e.activation(SPE, SPE, ACT.Ln, bias=1.0), a)
            a2 = A(lambda e: e.activation(EA, col("A_log", 0, 8), ACT.Exp), a)
            yield
            k = V(lambda e: e.scalar_tensor_tensor(SPX, SPX, 0.0, SPE, ALU.max, add), a)
            g_tok = V(lambda e: e.scalar_tensor_tensor(m28(GG), m28(SPX), -1.0, EA.unsqueeze(1).broadcast_to([128, 2, 8]), mult, mult), k, a2)
            yield
            bi, bk2, fr = mbank.get()

            def cums(e):
                e.matmul(bk2[:, 0:16], cn("tri"), GG, start=True, stop=True)
                return e.matmul(bk2[:, 16:32], cn("ch"), GG, start=True, stop=True)
            m = P(cums, g_tok, fr)
            yield
            k = V(lambda e: e.tensor_copy(GC, bk2[:, 0:16]), m)
            k = V(lambda e: e.tensor_copy(GL, bk2[:, 16:32]), k)
            mbank.release(bi, k)
            v = V(lambda e: e.tensor_tensor(DK, GL, GC, sub), k)
            a = A(lambda e: e.activation(DK, DK, ACT.Exp), v)
            a = A(lambda e: e.activation(BG, GC, ACT.Exp), a)
            yield
            lin_tok["sc"] = V(lambda e: e.tensor_tensor(BG, BG, BETA, mult), a, a1)

        lin_tok["sc"] = None
        l2_tok = [None, None]
        rs_read = [None]

        def l2norm(hg):
            order = [(b + 4 * hg + i, n + i) for i in range(4) for b, n in ((8, 4), (0, 0))]
            while qkv_tok[order[0][0]] is None:
                yield
            bi, bk, fr = mbank.get()
            for c, (j, n) in enumerate(order):
                while qkv_tok[j] is None:
                    yield
                i, t, ft = te.get()
                a = A(lambda e, j=j, t=t: e.activation(t, B1[:, j, :], ACT.Square), qkv_tok[j], ft)
                yield
                m = P(lambda e, c=c, n=n, t=t, bk=bk: e.matmul(bk[0:8, 0:256], cn("slide", 7 - n, 15 - n), t, start=(c == 0), stop=(c == 7)), a, fr)
                te.release(i, m)
            yield
            need(H2_tok, 7)
            r = yield from rsqrt_steps(RS[0:8, 0, :], RS[0:8, 1, :], bk[0:8, 0:256], 1.0, 1e-6, m, H2_tok[7], rs_read[0])
            mbank.release(bi, r)
            for n in range(0, 8, 2):
                bi, bk, fr = mbank.get()
                m = P(lambda e, n=n, bk=bk: [e.matmul(bk[:, 256 * q:256 * q + 256], CN[0:8, n + q:n + q + 1].broadcast_to([8, 128]), RS[0:8, 0, :],
                                                      start=True, stop=True) for q in range(2)][-1], r, fr)
                rs_read[0] = m
                yield
                for q in range(2):
                    j = (0 if n < 4 else 8) + 4 * hg + n % 4 + q
                    qkv_tok[j] = V(lambda e, n=n, q=q, j=j, bk=bk: e.scalar_tensor_tensor(
                        B1[:, j, :], B1[:, j, :], 128.0 ** -0.5 if n < 4 else 1.0, bk[:, 256 * q:256 * q + 256], mult, mult), m)
                mbank.release(bi, qkv_tok[j])
            l2_tok[hg] = qkv_tok[j]
        n = 0
        for h in range(4):
            for j in (8 + h, h, 16 + h):
                run(block(H1, h_hi, 8, "w_in", 8, 9 + j, ev_qkv(j)))
                n += 1
                if n == 1:
                    later(scalars())
                    later(l2norm(0))
                    later(l2norm(1))

        SCALE = 192.0 ** -0.5
        pr = Ring([B2[:, 11 + i, :] for i in range(4)])
        ptr = Ring([B2[:, 9, :], B2[:, 10, :]])
        qn_r = Ring([B2[:, 0, :], B2[:, 1, :]])
        kn_r = Ring([B2[:, 2, :], B2[:, 3, :]])
        qp_r = Ring([B2[:, 4, :], B2[:, 5, :]])
        vt_r = Ring([B2[:, 6 + i, :].rearrange("p (m n) -> p m n", m=2) for i in range(3)])
        mst = {}
        SM = SC[:, 64:256]
        av = {}
        mo_tok = [None] * 8
        HD = {}
        part = {}

        def softmax_stages(scores, biasmask, keys, pv):
            def s0(i):
                bi, bk, fr = mbank.get()
                m = scores(i, bk, fr)
                pi, p, pf = pr.get()
                v = biasmask(i, p[:, 0:keys(i)], bk[:, 0:keys(i)], m, pf)
                mbank.release(bi, v)
                mst[i] = [pi, p[:, 0:keys(i)], v]

            def s1(i):
                pi, p, v = mst[i]
                c = 3 * (i % 32)
                v = V(lambda e: e.tensor_reduce(SM[:, c:c + 1], p, AX, ALU.max, negate=True), v)
                a = A(lambda e: e.activation(p, p, ACT.Exp, bias=SM[:, c:c + 1], accum_out=SM[:, c + 1:c + 2]), v)
                mst[i].append(a)

            def s2(i):
                pi, p, _, a = mst[i]
                c = 3 * (i % 32)
                v = V(lambda e: e.reciprocal(SM[:, c + 2:c + 3], SM[:, c + 1:c + 2]), a)
                v = V(lambda e: e.tensor_scalar(p, p, SM[:, c + 2:c + 3], None, mult), v)
                mst[i] = [pi, p, v]

            def s2b(i):
                pi, p, v = mst[i]
                bi, bk, fr = mbank.get()
                nk = keys(i) // 128

                def tr(e):
                    for q in range(nk):
                        r = e.transpose(bk[:, 128 * q:128 * q + 128], p[:, 128 * q:128 * q + 128], cn("ident"))
                    return r
                m = P(tr, v, fr)
                pr.release(pi, m)
                ti, t, tf = ptr.get()
                a = A(lambda e: e.activation(t[:, 0:keys(i)], bk[:, 0:keys(i)], ACT.Copy), m, tf)
                mbank.release(bi, a)
                mst[i] = [ti, t, a]

            def s3(i):
                ti, t, a = mst[i]
                ptr.release(ti, pv(i, t, a))
            return [s0, s1, s2, s2b, s3]

        def pipe_step(stages, step, n):
            for s in range(len(stages) - 1, -1, -1):
                i = step - s
                if 0 <= i < n:
                    stages[s](i)

        def token_major(dst, src, k, *waits):
            mi, mk, mf = mbank.get()

            def tr(e):
                for m in range(2):
                    r = e.transpose(mk[:, 128 * m:128 * m + 128], src[:, 128 * m:128 * m + 128], cn("ident"))
                return r
            m = P(tr, k, mf)
            yield
            a = A(lambda e: e.activation(dst, mk[:, 0:256].rearrange("p (m n) -> p m n", m=2), ACT.Copy), m, *waits)
            mbank.release(mi, a)
            return m, a

        def ev_ring(ring, key):
            HD[key] = None

            def f(bk, tok, bi):
                i, t, fr = ring.get()
                k = yield from raw_sum(t, bk, tok, bi, fr)
                HD[key] = (i, t, k)
            return f

        def ev_qp(key):
            HD[key] = None

            def f(bk, tok, bi):
                i, t, fr = qp_r.get()
                k = yield from raw_sum(t, bk, tok, bi, fr)
                need(RN, "kpe")
                k = yield from rope(t, t, k)
                HD[key] = (i, t, k)
            return f

        def ev_vt(key):
            HD[key] = None

            def f(bk, tok, bi):
                i, t, fr = tv.get()
                k = yield from raw_sum(t, bk, tok, bi, fr)
                yield
                vi, vt, vf = vt_r.get()
                m, a = yield from token_major(vt, t, k, vf)
                tv.release(i, m)
                HD[key] = (vi, vt, a)
            return f

        def mla_scores(i, bk, fr):
            h, qb = divmod(i, 2)
            nk = 128 * (qb + 1)
            o = 64 * (h % 2)
            (qi, qn, qt), (ki, kn, kt), (pi, qp, pt) = need(HD, ("q", h)), need(HD, ("k", h)), need(HD, ("p", h // 2))

            def mm(e):
                e.matmul(bk[:, 0:nk], qn[:, 128 * qb:128 * qb + 128], kn[:, 0:nk], start=True, stop=False)
                return e.matmul(bk[:, 0:nk], qp[o:o + 64, 128 * qb:128 * qb + 128], KPE[o:o + 64, 0:nk], start=False, stop=True)
            m = P(mm, qt, kt, pt, RN["kpe"], fr)
            if qb == 1:
                qn_r.release(qi, m)
                kn_r.release(ki, m)
                if h % 2:
                    qp_r.release(pi, m)
            return m

        def mla_mask(i, p, ps, m, pf):
            qb = i % 2
            return V(lambda e: e.scalar_tensor_tensor(p, ps, SCALE, cn("mm", 128 - 128 * qb, 256), mult, add), m, pf)

        def mla_pv(i, t, a):
            h, qb = divmod(i, 2)
            if qb == 0:
                av["b"] = mbank.get()
            bi, bk, fr = av["b"]
            vi, vt, vtok = need(HD, ("v", h))

            def mm(e):
                for q in range(qb + 1):
                    r = e.matmul(bk[:, 128 * qb:128 * qb + 128], vt[:, q, :], t[:, 128 * q:128 * q + 128],
                                 start=(q == 0), stop=(q == qb))
                return r
            m = P(mm, a, vtok, fr if qb == 0 else None)
            if qb == 1:
                vt_r.release(vi, m)

                def out():
                    mo_tok[h] = yield from split(H2, 8 + h, bk[:, 0:256], m)
                    mbank.release(bi, mo_tok[h])
                later(out())
            return m

        def mla_gen():
            stages = softmax_stages(mla_scores, mla_mask, lambda i: 128 * (i % 2 + 1), mla_pv)

            def make(h):
                if h % 2 == 0:
                    yield from block(H2, H2_tok[0:4], 0, "w_uq", 0, 8 + h // 2, ev_qp(("p", h // 2)))
                yield from block(H2, H2_tok[0:4], 0, "w_uq", 0, h, ev_ring(qn_r, ("q", h)))
                yield from block(H2, H2_tok[4:8], 4, "w_ukv", 0, h, ev_ring(kn_r, ("k", h)))
                yield from block(H2, H2_tok[4:8], 4, "w_ukv", 0, 8 + h, ev_vt(("v", h)))
            yield from make(0)
            for step in range(20):
                if step % 2 == 0 and step // 2 < 7:
                    yield from make(step // 2 + 1)
                pipe_step(stages, step, 16)
                yield

        fa_done = []

        def fill_a():
            for h in range(4, 8):
                for j in (8 + h, h, 16 + h):
                    yield from block(H1, h_tok, 0, "w_in", 0, 9 + j, ev_qkv(j))
            fa_done.append(True)
            yield from mla_gen()

        fills = [fill_a()]

        def pump(n=1):
            for _ in range(n):
                while fills:
                    try:
                        next(fills[0])
                        break
                    except StopIteration:
                        fills.pop(0)

        def pair(t, i):
            return t[:, i:i + 2, :].rearrange("p a t -> p (a t)")
        KBG, KDEC, VB, AT, LT, CT, MM_, MT = (pair(X, 2 * i) for i in range(8))
        SS, DD, EG, QG, UU = pair(B2, 16), pair(B2, 18), pair(B2, 20), pair(B2, 22), pair(B3, 6)
        cq_read = [H2_tok[7], tk_cos]

        def h4(x):
            return x.rearrange("p (h n) -> p h n", h=4)

        def h2(x, s):
            return x[:, 256 * s:256 * s + 256]

        def mask4(name, a=0, b=128, n=4):
            return cn(name, a, b).unsqueeze(1).broadcast_to([128, n, 128])

        def colb(x, hg, m):
            return x[:, 8 * m + 4 * hg:8 * m + 4 * hg + 4].unsqueeze(2).broadcast_to([128, 4, 128])

        def mmn(heads, fn, *waits):
            bi, bk, fr = mbank.get()

            def go(e):
                for n, h in enumerate(heads):
                    r = fn(e, h, bk[:, 128 * n:128 * n + 128])
                return r
            return bi, bk, P(go, fr, *waits)

        def hx(t, h):
            return t[:, 128 * h:128 * h + 128]

        FULL = (0, 1, 2, 3)
        SUB = ((0, 1), (2, 3))
        o_tok = [None] * 8
        need(H2_tok, 7)
        sc_tok = need(lin_tok, "sc")
        cq_read = [H2_tok[7], tk_cos]
        last = {n: cq_read for n in ("KBG", "KDEC", "VB", "AT", "LT", "CT", "MM", "MT", "SS", "DD", "EG", "QG", "UU")}

        for hg in range(2):
            hs = [4 * hg + h for h in range(4)]
            while hg == 1 and not fa_done:
                pump(1)
            need(l2_tok, hg)
            for h in hs:
                need(qkv_tok, 16 + h)
            s_tok = [V(lambda e, s=s: e.memset(h2(SS, s), 0.0), last["SS"]) for s in range(2)]
            for mt in range(2):
                tt = slice(128 * mt, 128 * mt + 128)
                qk = [qkv_tok[h] for h in hs] + [qkv_tok[8 + h] for h in hs]
                v = V(lambda e, hg=hg, mt=mt: e.tensor_tensor(h4(EG), mask4("tri"), colb(GG, hg, mt), mult), last["EG"], sc_tok)
                bi, bk, fr = mbank.get()
                m = P(lambda e, bk=bk: e.matmul(bk[:, :], cn("ones"), EG, start=True, stop=True), v, fr)
                b4, bk4, m4 = mmn(FULL, lambda e, h, o, hs=hs, tt=tt: e.matmul(o, B1[:, 8 + hs[h], tt], B1[:, 8 + hs[h], tt], start=True, stop=True), qk)
                v2 = V(lambda e, hg=hg, mt=mt: e.tensor_tensor(h4(CT), mask4("ident"), colb(BETA, hg, mt), mult), last["CT"], sc_tok)
                b2, bk2, fr2 = mbank.get()
                m2 = P(lambda e, bk2=bk2: e.matmul(bk2[:, :], cn("ones"), CT, start=True, stop=True), v2, fr2)
                v = V(lambda e, bk=bk, hg=hg, mt=mt: e.tensor_tensor(h4(DD), h4(bk[:, :]), colb(GC, hg, mt), sub), m, last["DD"])
                v = V(lambda e: e.tensor_scalar(DD, DD, 0.0, None, ALU.min), v)
                a = A(lambda e: e.activation(DD, DD, ACT.Exp), v)
                eg_tok = A(lambda e, bk=bk: e.activation(EG, bk[:, :], ACT.Exp), m)
                mbank.release(bi, v, eg_tok)
                dm = V(lambda e: e.tensor_tensor(h4(DD), h4(DD), mask4("tri"), mult), a)
                v = V(lambda e, bk4=bk4: e.tensor_tensor(LT, bk4[:, :], DD, mult), m4, dm, last["LT"])
                mbank.release(b4, v)
                lt_tok = V(lambda e, bk2=bk2: e.tensor_tensor(LT, bk2[:, :], LT, mult), v, m2)
                mbank.release(b2, lt_tok)
                mt_t, mm_t, ct_t, u_t = [None] * 2, [None] * 2, [None] * 2, [None] * 2

                def m2h(x):
                    return x.rearrange("p (h n) -> p h n", h=2)
                for s in range(2):
                    v = V(lambda e, s=s: e.tensor_tensor(m2h(h2(CT, s)), m2h(h2(LT, s)), mask4("lm", n=2), mult), lt_tok, m2)
                    mt_t[s] = V(lambda e, s=s: e.tensor_tensor(m2h(h2(MT, s)), mask4("ident", n=2), m2h(h2(CT, s)), sub), v, last["MT"])
                    b3, bk3, m3 = mmn(SUB[s], lambda e, h, o: e.transpose(o, hx(MT, h), cn("ident")), mt_t[s])
                    mm_t[s] = A(lambda e, bk3=bk3, s=s: e.activation(h2(MM_, s), bk3[:, 0:256], ACT.Copy), m3, last["MM"])
                    mbank.release(b3, mm_t[s])
                    ct_t[s] = V(lambda e, s=s: e.tensor_tensor(m2h(h2(CT, s)), m2h(h2(LT, s)), mask4("lm", 128, 256, n=2), mult), mt_t[s])
                rest_ops = []

                def side(n):
                    for _ in range(n):
                        if rest_ops:
                            rest_ops.pop(0)()
                R = {}

                def side_at(hs=hs, tt=tt, qk=qk):
                    b3, bk3, m3 = mmn(FULL, lambda e, h, o: e.matmul(o, B1[:, 8 + hs[h], tt], B1[:, hs[h], tt], start=True, stop=True), qk)
                    R["at"] = V(lambda e: e.tensor_tensor(AT, bk3[:, :], DD, mult), m3, dm, last["AT"])
                    mbank.release(b3, R["at"])

                def side_k(hs=hs, tt=tt, qk=qk, hg=hg, mt=mt):
                    b3, bk3, m3 = mmn(FULL, lambda e, h, o: e.transpose(o, B1[:, 8 + hs[h], tt], cn("ident")), qk)
                    R["kbg"] = V(lambda e: e.tensor_tensor(h4(KBG), h4(bk3[:, :]), colb(BG, hg, mt), mult), m3, last["KBG"])
                    R["kd"] = V(lambda e: e.tensor_tensor(h4(KDEC), h4(bk3[:, :]), colb(DK, hg, mt), mult), m3, last["KDEC"])
                    mbank.release(b3, R["kd"])

                def side_v(hs=hs, tt=tt, hg=hg, mt=mt):
                    b3, bk3, m3 = mmn(FULL, lambda e, h, o: e.transpose(o, B1[:, 16 + hs[h], tt], cn("ident")), [qkv_tok[16 + h] for h in hs])
                    R["vb"] = V(lambda e: e.tensor_tensor(h4(VB), h4(bk3[:, :]), colb(BETA, hg, mt), mult), m3, last["VB"])
                    mbank.release(b3, R["vb"])
                    R["v_read"] = m3

                def side_q(hg=hg, tt=tt, qk=qk):
                    R["qg"] = V(lambda e: e.tensor_tensor(h4(QG), B1[:, 4 * hg:4 * hg + 4, tt], h4(EG), mult), eg_tok, qk, last["QG"])
                rest_ops = [side_at, side_k, side_v, side_q]
                for lv in range(1, 6):
                    us = []
                    for s in range(2):
                        b3, bk3, m3 = mmn(SUB[s], lambda e, h, o: e.matmul(o, hx(CT, h), hx(MM_, h), start=True, stop=True), ct_t[s], mm_t[s])
                        us.append((b3, bk3, m3))
                    side(1)
                    for s in range(2):
                        b3, bk3, m3 = us[s]
                        u_t[s] = A(lambda e, bk3=bk3, s=s: e.activation(h2(UU, s), bk3[:, 0:256], ACT.Copy), m3, mt_t[s], last["UU"])
                        mbank.release(b3, u_t[s])
                    pump(1)
                    for s in range(2):
                        b4, bk4, m4 = mmn(SUB[s], lambda e, h, o: e.matmul(o, hx(UU, h), hx(MT, h), start=True, stop=True), u_t[s], mt_t[s])
                        if lv < 5:
                            ct_t[s] = V(lambda e, lv=lv, s=s: e.tensor_tensor(m2h(h2(CT, s)), m2h(h2(LT, s)), mask4("lm", 128 * lv + 128, 128 * lv + 256, n=2), mult), us[s][2])
                            b5, bk5, m5 = mmn(SUB[s], lambda e, h, o: e.matmul(o, hx(MT, h), hx(UU, h), start=True, stop=True), u_t[s], mt_t[s])
                            mm_t[s] = V(lambda e, bk5=bk5, s=s: e.tensor_tensor(h2(MM_, s), h2(MM_, s), bk5[:, 0:256], sub), m5)
                            mbank.release(b5, mm_t[s])
                            mt_t[s] = V(lambda e, bk4=bk4, s=s: e.tensor_tensor(h2(MT, s), h2(MT, s), bk4[:, 0:256], sub), m4, m5)
                        else:
                            mt_t[s] = V(lambda e, bk4=bk4, s=s: e.tensor_tensor(h2(MT, s), h2(MT, s), bk4[:, 0:256], sub), m4)
                        mbank.release(b4, mt_t[s])
                        u_t[s] = m4
                side(4)
                last["LT"] = last["CT"] = [us[0][2], us[1][2], ct_t[0], ct_t[1]]
                last["DD"] = [R["at"]]
                uu_t, w_t = [None] * 2, [None] * 2
                for s in range(2):
                    b3, bk3, m3 = mmn(SUB[s], lambda e, h, o: e.matmul(o, hx(KBG, h), hx(MT, h), start=True, stop=True), mt_t[s], R["kbg"])
                    w_t[s] = A(lambda e, bk3=bk3, s=s: e.activation(h2(MM_, s), bk3[:, 0:256], ACT.Copy), m3, us[s][2])
                    mbank.release(b3, w_t[s])
                    b3, bk3, m3 = mmn(SUB[s], lambda e, h, o: e.matmul(o, hx(MT, h), hx(VB, h), start=True, stop=True), mt_t[s], R["vb"])
                    uu_t[s] = A(lambda e, bk3=bk3, s=s: e.activation(h2(UU, s), bk3[:, 0:256], ACT.Copy), m3, u_t[s])
                    mbank.release(b3, uu_t[s])
                last["MT"] = last["VB"] = last["KBG"] = [m3]
                pump(1)
                for cc in range(2):
                    r0 = 64 * cc
                    rr = slice(r0, r0 + 64)
                    vns = []
                    for s in range(2):
                        b3, bk3, m3 = mmn(SUB[s], lambda e, h, o, rr=rr: e.matmul(o[rr, :], MM_[:, 128 * h + rr.start:128 * h + rr.stop], hx(SS, h), start=True, stop=True),
                                          w_t[s], s_tok[s])
                        vns.append(V(lambda e, bk3=bk3, rr=rr, s=s: e.tensor_tensor(UU[rr, 256 * s:256 * s + 256], UU[rr, 256 * s:256 * s + 256], bk3[rr, 0:256], sub), m3, uu_t[s]))
                        mbank.release(b3, vns[s])
                        w_read = m3
                    pump(1)
                    for s in range(2):
                        bi, bk, fr = mbank.get()

                        def sup(e, bk=bk, rr=rr, s=s):
                            for n, h in enumerate(SUB[s]):
                                r = e.matmul(bk[:, 128 * n:128 * n + 128], hx(KDEC, h)[rr, :], hx(UU, h)[rr, :], start=True, stop=True)
                            return r
                        ms = P(sup, vns[s], R["kd"], fr)
                        b5, bk5, fr5 = mbank.get()

                        def om(e, bk5=bk5, rr=rr, s=s):
                            for n, h in enumerate(SUB[s]):
                                o = bk5[:, 64 * n:64 * n + 64]
                                e.matmul(o, hx(SS, h), QG[:, 128 * h + rr.start:128 * h + rr.stop], start=True, stop=False)
                                r = e.matmul(o, hx(UU, h)[rr, :], AT[rr, 128 * h + rr.start:128 * h + rr.stop], start=False, stop=True)
                            return r
                        mo = P(om, vns[s], R["qg"], R["at"], s_tok[s], fr5)
                        ts = slice(128 * mt + r0, 128 * mt + r0 + 64)
                        oe = A(lambda e, bk5=bk5, ts=ts, hg=hg, s=s: e.activation(B1[:, 4 * hg + 2 * s:4 * hg + 2 * s + 2, ts], bk5[:, 0:128].rearrange("p (h n) -> p h n", h=2), ACT.Copy), mo, R["qg"])
                        mbank.release(b5, oe)
                        for n, h in enumerate(SUB[s]):
                            s_tok[s] = V(lambda e, n=n, h=h, bk=bk, r0=r0: e.scalar_tensor_tensor(
                                hx(SS, h), hx(SS, h), EG[:, 128 * h + r0 + 63:128 * h + r0 + 64], bk[:, 128 * n:128 * n + 128], mult, add), ms, mo)
                        mbank.release(bi, s_tok[s])
                    pump(1)
                for n in ("MM", "QG", "AT", "UU", "KDEC"):
                    last[n] = [mo, w_read]
                last["EG"] = last["SS"] = list(s_tok) + [mo, R["qg"]]
            for h in hs:
                o_tok[h] = oe
            if hg == 0:
                v_read0 = R["v_read"]
        x_free = now()
        v_read1 = R["v_read"]
        for i in range(4):
            tk_x2 = D("x2", 16 * i + 16, lambda e, i=i: e.dma_start(X[:, 4 * i:4 * i + 4, :], xT[:, 4 * i:4 * i + 4, :]), x_free)
        while fills:
            pump(1)
        Z = [B1[:, 16 + i, :] for i in range(8)]
        YA = [B1[:, 8 + i, :] for i in range(8)] + [B2[:, i, :] for i in range(8)]
        GB = [B2[:, 8 + i, :] for i in range(16)]
        z_tok, ya_tok, gb_tok = [None] * 8, [None] * 16, [None] * 16
        free2 = now()

        def ev_z(j):
            def f(bk, tok, bi):
                k = yield from raw_sum(Z[j], bk, tok, bi, v_read1, scale=0.5)
                yield
                i, t, fr = te.get()
                a = A(lambda e: e.activation(t, Z[j], ACT.Tanh), k, fr)
                yield
                z_tok[j] = V(lambda e: e.scalar_tensor_tensor(Z[j], t, 1.0, Z[j], add, mult), a)
                te.release(i, z_tok[j])
            return f

        def ev_gate(dst, toks, j):
            def f(bk, tok, bi):
                k = yield from raw_sum(dst[j], bk, tok, bi, free2, scale=0.5)
                yield
                toks[j] = A(lambda e: e.activation(dst[j], dst[j], ACT.Tanh), k)
            return f

        def ev_ya(j):
            def f(bk, tok, bi):
                i, t, fr = tv.get()
                k = yield from raw_sum(t, bk, tok, bi, fr)
                yield
                ya_tok[j] = V(lambda e: e.scalar_tensor_tensor(YA[j], YA[j], 1.0, t, add, mult), k, need(ga_tok, j))
                tv.release(i, ya_tok[j])
            return f
        ga_tok = [None] * 16

        def fill_b():
            for j in range(8):
                yield from block(H1, h_tok, 0, "w_in", 0, 33 + j, ev_z(j))
            for j in range(16):
                yield from block(H1, h_tok, 0, "w_in", 0, 42 + j, ev_gate(YA, ga_tok, j))
                yield from block(H2, mo_tok, 8, "w_o_mla", 0, j, ev_ya(j))
            for j in range(16):
                yield from block(H1, h_tok, 0, "w_in", 0, 58 + j, ev_gate(GB, gb_tok, j))
        fills.append(fill_b())
        bi, bk, fr = mbank.get()
        for h in range(8):
            i, t, ft = te.get()
            a = A(lambda e, h=h, t=t: e.activation(t, B1[:, h, :], ACT.Square), o_tok[h], ft)
            m = P(lambda e, h=h, t=t, bk=bk: e.matmul(bk[0:8, 0:256], cn("slide", 7 - h, 15 - h), t, start=(h == 0), stop=(h == 7)), a, fr)
            te.release(i, m)
        r = rsqrt(RS[0:8, 0, :], RS[0:8, 1, :], bk[0:8, 0:256], 1.0 / 128, 1e-6, m, now())
        mbank.release(bi, r)
        pump(8)
        gdn_tok = [None] * 8
        for h in range(8):
            if h % 2 == 0:
                bi, bk, fr = mbank.get()
                m = P(lambda e, h=h, bk=bk: [e.matmul(bk[:, 256 * q:256 * q + 256], CN[0:8, h + q:h + q + 1].broadcast_to([8, 128]), RS[0:8, 0, :],
                                                      start=True, stop=True) for q in range(2)][-1], r, fr)
            def one(h, bi, bk, m):
                o = B1[:, h, :]
                v = V(lambda e: e.scalar_tensor_tensor(o, o, col("gdn_norm"), bk[:, 256 * (h % 2):256 * (h % 2) + 256], mult, mult), m)
                if h % 2:
                    mbank.release(bi, v)
                yield
                v = V(lambda e: e.tensor_tensor(o, o, Z[h], mult), v, need(z_tok, h))
                yield
                gdn_tok[h] = yield from split(H2, h, o, v, free2)
            later(one(h, bi, bk, m))
            pump(2)
        while fills:
            pump(1)
        h1_free = ("pe", count["pe"])
        m_tok = [None] * 16

        def ev_yb(j):
            def f(bk, tok, bi):
                i, t, fr = tv.get()
                k = yield from raw_sum(t, bk, tok, bi, fr)
                yield
                v = V(lambda e: e.scalar_tensor_tensor(t, GB[j], 1.0, t, add, mult), k, need(gb_tok, j))
                v = V(lambda e: e.tensor_tensor(t, t, YA[j], add), v, need(ya_tok, j))
                yield
                m_tok[j] = yield from split(H1, j, t, v, h1_free, scale=0.5)
                tv.release(i, m_tok[j])
            return f
        for j in range(16):
            run(block(H2, gdn_tok, 0, "w_o_gdn", 0, j, ev_yb(j)))

        x_tok = [None] * 16
        S = Stats(SQS[1].done, *x_free)

        def ev_res(gate, S, extra):
            def mk(j):
                def f(bk, tok, bi):
                    i, t, fr = tv.get()
                    k = yield from raw_sum(t, bk, tok, bi, fr)
                    yield
                    x_tok[j] = V(lambda e: e.scalar_tensor_tensor(X[:, j, :], t, MOD[:, 16 * gate + j:16 * gate + j + 1], X[:, j, :], mult, add),
                                 k, extra, need(mod_tok, 2 * gate + j // 8), x_tok[j])
                    tv.release(i, x_tok[j])
                    if S is not None:
                        S.square(X[:, j, :], x_tok[j], final=(j == 15 and gate == 2))
                return f
            return mk
        ev = ev_res(2, S, tk_x2)
        for j in range(16):
            run(block(H1, m_tok, 0, "w_o", 0, j, ev(j)))
        run_pending()
        rs_tok = S.finish(2048, 1e-6)
        Sp = S
        h_tok = [None] * 16
        run(adaln(3, 4, "norm_ffn", rs_tok, x_tok, h_tok, range(16), now()))

        def ffn(cuts, up, first, down_name, ev_down):
            at = 0
            for ci, n in enumerate(cuts):
                f_tok = [None] * n
                s0 = 0
                if ci == 0:
                    s0 = first(f_tok)
                for s in range(s0, n):
                    run(up(at + s, s, f_tok))
                h1_last[0] = ("pe", count["pe"])
                for j in range(16):
                    run(block(H2, f_tok, 0, down_name, at, j, ev_down(ci, j)))
                h2_free[0] = [("pe", count["pe"])]
                at += n
            run_pending()

        h1_last = [None]
        def silu_to(dst, src, tok, *waits):
            i, t, fr = te.get()
            a = A(lambda e: e.activation(t, src, ACT.Sigmoid), tok, fr)
            yield
            v = V(lambda e: e.tensor_tensor(dst, src, t, mult), a, *waits)
            te.release(i, v)
            return v

        G_ = {}

        def up1_outs(i, s, f_tok):
            def e1(bk, tok, bi):
                q, t, fr = tv.get()
                k = yield from raw_sum(t, bk, tok, bi, fr)
                yield
                k = yield from silu_to(t, t, k)
                G_[i] = (q, t, k)

            def e2(bk, tok, bi):
                q, t, fr = tv.get()
                k = yield from raw_sum(t, bk, tok, bi, fr)
                yield
                gq, g, gk = need(G_, i)
                v = V(lambda e: e.tensor_tensor(t, t, g, mult), k, gk)
                tv.release(gq, v)
                yield
                f_tok[s] = yield from split(H2, s, t, v, h2_free[0])
                tv.release(q, f_tok[s])
            G_[i] = None
            return [(i, e1), (44 + i, e2)]

        def up1(i, s, f_tok):
            for o in up1_outs(i, s, f_tok):
                yield from blocks(H1, h_tok, 0, "w_gate_up", 0, [o])

        def first1(f_tok):
            run(blocks(H1, h_tok, 0, "w_gate_up", 0, up1_outs(0, 0, f_tok) + up1_outs(1, 1, f_tok)))
            return 2

        h2_free = [now()]
        S = Stats(Sp.done)
        R12, R1, ACC2 = B3[:, 0, :], B3[:, 1, :], B3[:, 2, :]
        FP = SC[:, 48:64]
        fp_tok = V(lambda e: e.tensor_tensor(FP, col("final_norm", 0, 16), col("pre_mix", 0, 16), mult), tk_cols)
        u_tok2 = [None] * 16
        acc2 = [None]

        def evd(ci, j):
            f = ev_res(5, S if ci == 2 else None, None)(j)

            def go(bk, tok, bi):
                yield from f(bk, tok, bi)
                if ci < 2:
                    return
                sq = SQ[:, 1, :]
                k = G(lambda e: e.tensor_scalar(sq, X[:, j, :], col("final_norm", j), None, mult), x_tok[j], S.last)
                k = G(lambda e: e.tensor_tensor(ACC2 if j == 0 else sq, sq, sq, mult), k, acc2[0])
                if j:
                    k = G(lambda e: e.tensor_tensor(ACC2, ACC2, sq, add), k)
                acc2[0] = k
                S.last = S.last + [k]
                yield
                u_tok2[j] = yield from split(H1, j, X[:, j, :], x_tok[j], fp_tok, h1_last[0], scale=FP[:, j:j + 1])
            return go
        ffn((15, 15, 14), up1, first1, "w_down", evd)
        ffn_end = now()
        Sp = S
        r_tok = {"r1": None, "r12": None}

        def norms2():
            r1_tok = yield from Sp.finish_steps(2048, 1e-6, ffn_end, y=R1)
            r_tok["r1"] = r1_tok
            bi, bk, fr = mbank.get()
            m = P(lambda e, bk=bk: e.matmul(bk[:, 0:256], cn("ones"), ACC2, start=True, stop=True), acc2[0], fr)
            yield
            v = V(lambda e, bk=bk: e.tensor_tensor(RS[:, 2, :], bk[:, 0:256], R1, mult), m, r1_tok)
            mbank.release(bi, v)
            v = V(lambda e: e.tensor_tensor(RS[:, 2, :], RS[:, 2, :], R1, mult), v)
            v = yield from rsqrt_steps(RS[:, 0, :], RS[:, 1, :], RS[:, 2, :], 1.0 / 2048, 1e-6, v)
            r_tok["r12"] = V(lambda e: e.tensor_tensor(R12, R1, RS[:, 0, :], mult), v)
        later(norms2(), 12)
        b2_free = ffn_end
        UP = B1[:, 0:9, :].rearrange("p a t -> p (a t)")[:, 0:8 * 286].rearrange("p (j n) -> p j n", j=8)
        pad_tok = V(lambda e: e.memset(UP, 0.0), b2_free)
        CA = [B1[:, 9 + j, :] for j in range(8)]
        BB = [B2[:, 13 + i, :] for i in range(4)]
        MEAN = B2[:, 17, :]
        qn_r = Ring([B2[:, 0, :], B2[:, 1, :]])
        kn_r = Ring([B2[:, 2, :], B2[:, 3, :]])
        vt_r = Ring([B2[:, 4 + i, :].rearrange("p (m n) -> p m n", m=2) for i in range(3)])
        ptr = Ring([B2[:, 7, :], B2[:, 8, :]])
        pr = Ring([B2[:, 9 + i, :] for i in range(4)])
        for ring in (qn_r, kn_r, vt_r, ptr, pr):
            ring.free = [b2_free for _ in ring.items]
        mst.clear()
        HD.clear()
        u_tok, a2_tok = [None] * 8, [None] * 8

        def scaled_sum(dst, bk, tok, bi, *waits):
            k = yield from raw_sum(dst, bk, tok, bi, *waits)
            yield
            return V(lambda e: e.tensor_tensor(dst, dst, R12, mult), k, need(r_tok, "r12"))

        def e_a(j):
            def f(bk, tok, bi):
                a2_tok[j] = yield from scaled_sum(UP[:, j, 15:271], bk, tok, bi, pad_tok)
            return f

        def e_g(j):
            def f(bk, tok, bi):
                i, t, fr = tv.get()
                k = yield from scaled_sum(t, bk, tok, bi, fr)
                yield
                a = A(lambda e: e.activation(t, t, ACT.Tanh, scale=0.5), k)
                yield
                u_tok[j] = V(lambda e: e.scalar_tensor_tensor(UP[:, j, 15:271], t, 1.0, UP[:, j, 15:271], add, mult), a, need(a2_tok, j))
                tv.release(i, u_tok[j])
            return f

        conv_tok = [None] * 8
        cat_tok = [None] * 16

        def conv_gen():
            n = 0
            for j in range(8):
                while u_tok[j] is None:
                    yield
                o = COLS["w_dw"][0] + 31 * j
                k = V(lambda e, j=j, o=o: e.tensor_scalar(CA[j], UP[:, j, 0:256], CO[:, o:o + 1], col("b_dw", j), mult, add), u_tok[j], b2_free, dw_tok)
                for i in range(1, 31):
                    k = V(lambda e, i=i, j=j, o=o: e.scalar_tensor_tensor(CA[j], UP[:, j, i:i + 256], CO[:, o + i:o + i + 1], CA[j], mult, add), k)
                    n += 1
                    if n % CONV_STEP == 0:
                        yield
                conv_tok[j] = k
            bi, bk, fr = mbank.get()

            def sums(e):
                for j in range(8):
                    r = e.matmul(bk[:, 0:256], cn("ones"), CA[j], start=(j == 0), stop=(j == 7))
                return r
            m = P(sums, conv_tok[7], fr)
            k = V(lambda e: e.tensor_scalar(MEAN, bk[:, 0:256], 1.0 / 1024, None, mult), m, b2_free)
            mbank.release(bi, k)
            yield
            for _ in xg:
                yield
            b2, sq_bk, fr = mbank.get()
            for j in range(8):
                conv_tok[j] = V(lambda e, j=j: e.tensor_tensor(CA[j], CA[j], MEAN, sub), k, m)
                yield
                i, t, ft = te.get()
                a = A(lambda e, j=j, t=t: e.activation(t, CA[j], ACT.Square), conv_tok[j], ft)
                yield
                m2 = P(lambda e, j=j, t=t: e.matmul(sq_bk[:, 0:256], cn("ones"), t, start=(j == 0), stop=(j == 7)), a, fr)
                te.release(i, m2)
            yield
            r = yield from rsqrt_steps(RS[:, 0, :], RS[:, 1, :], sq_bk[:, 0:256], 1.0 / 1024, 1e-5, m2, need(r_tok, "r12"))
            mbank.release(b2, r)
            SY.last = [Sp.done, r]
            yield

            def one(j):
                i, t, fr = tv.get()
                v = V(lambda e: e.scalar_tensor_tensor(t, CA[j], col("ln_g", j), RS[:, 0, :], mult, mult), r, fr)
                v = V(lambda e: e.tensor_scalar(t, t, col("ln_b", j), 0.5, add, mult), v)
                yield
                q, y, fy = te.get()
                a = A(lambda e: e.activation(y, t, ACT.Tanh), v, fy)
                yield
                v = V(lambda e: e.scalar_tensor_tensor(t, y, 1.0, t, add, mult), a)
                te.release(q, v)
                yield
                cat_tok[j] = yield from split(H2, j, t, v, b2_free)
                tv.release(i, cat_tok[j])
            for j in range(8):
                later(one(j))
                yield
        SY = Stats()
        CONV_STEP = 3
        cg = conv_gen()

        def xs_gen():
            for j in range(16):
                x_tok[j] = V(lambda e, j=j: e.scalar_tensor_tensor(X[:, j, :], X[:, j, :], col("final_norm", j), R1, mult, mult), need(r_tok, "r1"), u_tok2[j], acc2[0], x_tok[j])
                yield
        xg = xs_gen()
        for j in range(8):
            for _ in block(H1, u_tok2, 0, "w_in2", 0, j, e_a(j)):
                next(cg, None)
            for _ in block(H1, u_tok2, 0, "w_in2", 0, 8 + j, e_g(j)):
                next(cg, None)
                if j:
                    next(xg, None)

        b_use = [b2_free] * 4
        bm_tok = {}

        def load_bias(i):
            s = i % 4
            d = D(f"b{s}", 16 * (i // 4 + 1), lambda e: e.dma_start(BB[s], bias_d[i]), b_use[s])
            bm_tok[i] = G(lambda e: e.tensor_tensor(BB[s], BB[s], cn("nm"), add), d)

        def e_r(ring, key):
            HD[key] = None

            def f(bk, tok, bi):
                i, t, fr = ring.get()
                k = yield from scaled_sum(t, bk, tok, bi, fr)
                HD[key] = (i, t, k)
            return f

        def e_v(key):
            HD[key] = None

            def f(bk, tok, bi):
                i, t, fr = tv.get()
                k = yield from scaled_sum(t, bk, tok, bi, fr)
                yield
                yield
                vi, vt, vf = vt_r.get()
                m, a = yield from token_major(vt, t, k, vf)
                tv.release(i, m)
                HD[key] = (vi, vt, a)
            return f

        def na_scores(i, bk, fr):
            h, qb = divmod(i, 2)
            o = 64 * (h % 2)
            (qi, qn, qt), (ki, kn, kt) = need(HD, ("q", h // 2)), need(HD, ("k", h // 2))
            m = P(lambda e: e.matmul(bk[:, 0:256], qn[o:o + 64, 128 * qb:128 * qb + 128], kn[o:o + 64, :], start=True, stop=True), qt, kt, fr)
            if i % 4 == 3:
                qn_r.release(qi, m)
                kn_r.release(ki, m)
            return m

        def na_mask(i, p, ps, m, pf):
            s = i % 4
            v = V(lambda e: e.scalar_tensor_tensor(p, ps, 0.125, BB[s], mult, add), m, pf, bm_tok[i])
            b_use[s] = [v]
            if i + 3 < 32:
                load_bias(i + 3)
            return v

        def na_pv(i, t, a):
            h, qb = divmod(i, 2)
            o = 64 * (h % 2)
            if i % 4 == 0:
                av["b"] = mbank.get()
            bi, bk, fr = av["b"]
            vi, vt, vtok = need(HD, ("v", h // 2))

            def mm(e):
                for q in range(2):
                    r = e.matmul(bk[o:o + 64, 128 * qb:128 * qb + 128], vt[:, q, o:o + 64], t[:, 128 * q:128 * q + 128],
                                 start=(q == 0), stop=(q == 1))
                return r
            m = P(mm, a, vtok, fr if i % 4 == 0 else None)
            if i % 4 == 3:
                vt_r.release(vi, m)
                j = 8 + h // 2

                def out():
                    cat_tok[j] = yield from split(H2, j, bk[:, 0:256], m, b2_free)
                    mbank.release(bi, cat_tok[j])
                later(out())
            return m

        def make2(j):
            for b, ev in ((16, e_r(qn_r, ("q", j))), (24, e_r(kn_r, ("k", j))), (32, e_v(("v", j)))):
                yield from block(H1, u_tok2, 0, "w_in2", 0, b + j, ev)

        for i in range(3):
            load_bias(i)
        stages = softmax_stages(na_scores, na_mask, lambda i: 256, na_pv)
        for _ in make2(0):
            next(cg, None)
        step = 0
        for j in range(1, 8):
            gen = make2(j)
            for _ in range(6):
                next(gen, None)
                next(cg, None)
                if step < 4 * j:
                    pipe_step(stages, step, 32)
                    step += 1
            run(gen)

        def drain():
            for s in range(step, 36):
                pipe_step(stages, s, 32)
                yield
        later(drain())
        later(cg)

        Y = [B2[:, i, :] for i in range(16)]
        y_free = []
        y_tok = [None] * 16
        S = SY

        def ev_y(ci, j, last):
            def f(bk, tok, bi):
                if ci == 0:
                    if not y_free:
                        y_free.extend(now())
                    y_tok[j] = yield from raw_sum(Y[j], bk, tok, bi, y_free)
                else:
                    i, t, fr = tv.get()
                    k = yield from raw_sum(t, bk, tok, bi, fr)
                    yield
                    y_tok[j] = V(lambda e: e.tensor_tensor(Y[j], Y[j], t, add), k, y_tok[j])
                    tv.release(i, y_tok[j])
                if last:
                    S.square(Y[j], y_tok[j], final=(j == 15))
            return f
        run(blocks(H2, cat_tok, 0, "w_out2", 0, [(j, ev_y(0, j, True)) for j in range(5)], WOUT_ORDER))
        for j in range(5, 16):
            run(block(H2, cat_tok, 0, "w_out2", 0, j, ev_y(0, j, True)))
        run_pending()
        rs_tok = S.finish(2048, 1e-6, now())
        Sp = S

        def post(name, rs_tok, then):
            def one(j):
                k = V(lambda e: e.scalar_tensor_tensor(Y[j], Y[j], col(name, j), RS[:, 0, :], mult, mult), rs_tok)
                yield
                x_tok[j] = V(lambda e: e.tensor_tensor(X[:, j, :], X[:, j, :], Y[j], add), k, x_tok[j])
                yield from then(j)
            return stagger(one(j) for j in range(16))
        SX = Stats(Sp.done)
        h1_free = ("pe", count["pe"])
        h_tok = [None] * 16

        def to_mlp(j):
            SX.square(X[:, j, :], x_tok[j])
            yield
            h_tok[j] = yield from split(H1, j, X[:, j, :], x_tok[j], h1_free, scale=col("pre_mlp", j))
        run(post("post_mix", rs_tok, to_mlp))
        r_tok["rx"] = None

        def norm_x():
            need(h_tok, 15)
            r_tok["rx"] = yield from SX.finish_steps(2048, 1e-6, x_tok[15])
            S.last = [SX.done]
        later(norm_x(), 56)

        y_free = []
        h2_free = [now()]
        S = Stats()

        def up2_outs(i, s, f_tok):
            def e1(bk, tok, bi):
                q, t, fr = tv.get()
                k = yield from raw_sum(t, bk, tok, bi, fr)
                yield
                v = V(lambda e: e.scalar_tensor_tensor(t, t, 0.0, RS[:, 0, :], ALU.max, mult), k, need(r_tok, "rx"))
                v = V(lambda e: e.tensor_tensor(t, t, t, mult), v)
                yield
                f_tok[s] = yield from split(H2, s, t, v, h2_free[0])
                tv.release(q, f_tok[s])
            return [(i, e1)]

        def up2(i, s, f_tok):
            yield from blocks(H1, h_tok, 0, "w_up2", 0, up2_outs(i, s, f_tok))

        def first2(f_tok):
            run(blocks(H1, h_tok, 0, "w_up2", 0, [o for i in range(5) for o in up2_outs(i, i, f_tok)]))
            return 5

        def evd2(ci, j):
            return ev_y(ci, j, ci == 3)
        ffn((16, 16, 16, 16), up2, first2, "w_down2", evd2)
        rs_tok = S.finish(2048, 1e-6, now())
        run(post("post_mlp", rs_tok, lambda j: iter(())))
        toks = x_tok
        for i in range(4):
            tk = D("out", 16 * i + 16, lambda e, i=i: e.dma_start(out[:, 4 * i:4 * i + 4, :], X[:, 4 * i:4 * i + 4, :]), toks[4 * i + 3])
        assert st["tile"] == N_TILES, st
        assert st["proc"] == len(kinds) and not pending

        block_ = ctx.enter_context(nc.Block())

        def play(name, e):
            seen = {}
            for fn, waits, inc in queue[name]:
                need = {}
                for s, v in waits:
                    need[s] = max(need.get(s, 0), v)
                for s, v in need.items():
                    if seen.get(s, 0) < v:
                        e.wait_ge(sems[s], v)
                        seen[s] = v
                r = fn(e)
                if inc is None:
                    r.then_inc(sems[name], 1)
                else:
                    r.then_inc(sems[inc], 16)

        @block_.sync
        def _(e):
            play("sp", e)
            e.wait_ge(sems["out"], 64)

        @block_.scalar
        def _(e):
            play("act", e)

        @block_.vector
        def _(e):
            play("dve", e)

        @block_.gpsimd
        def _(e):
            play("pool", e)

        @block_.tensor
        def _(e):
            play("pe", e)


def kernel(**inp):
    import concourse.bacc as _bacc
    from concourse import mybir as mb
    from concourse.bass_utils import run_bass_kernel_spmd as _run
    I = {k: np.asarray(v) for k, v in inp.items()}

    def feat(v):
        return v.reshape(-1, 128).T
    w_in = I["w_in"][0]
    kpe = w_in[:, 1024:1088]
    ba = w_in[:, 5184:5200]
    pad = np.zeros((2048, 112), np.float32)
    W = {"w_in": np.concatenate([w_in[:, 0:1024], kpe, kpe, w_in[:, 1088:5184], ba, pad, w_in[:, 5200:9296]], axis=1)}
    uq = I["w_uq"][0].reshape(512, 8, 192)
    W["w_uq"] = np.concatenate([uq[:, :, 0:128].reshape(512, 1024), uq[:, :, 128:192].reshape(512, 512)], axis=1)
    ukv = I["w_ukv"][0].reshape(512, 8, 256)
    W["w_ukv"] = np.concatenate([ukv[:, :, 0:128].reshape(512, 1024), ukv[:, :, 128:256].reshape(512, 1024)], axis=1)
    for a, b in (("w_o_mla", "w_o_mla"), ("w_o_gdn", "w_o_gdn"), ("w_o", "w_o"), ("w_gate_up", "w_gate_up"), ("w_down", "w_down"),
                 ("w_in2", "w_in_2"), ("w_out2", "w_out_2"), ("w_up2", "w_up_2"), ("w_down2", "w_down_2")):
        W[a] = I[b][0]
    cols = np.zeros((128, NCOLS), np.float32)

    def put(name, v):
        o, w = COLS[name]
        cols[:, o:o + w] = v
    put("c", feat(I["c"][0]))
    put("b_ada", feat(I["b_ada"][0]))
    put("norm_mix", feat(I["norm_mix"][0]))
    put("norm_ffn", feat(I["norm_ffn"][0]))
    put("q_a_norm", feat(I["q_a_norm"][0]))
    put("kv_a_norm", feat(I["kv_a_norm"][0]))
    put("conv_w", I["conv_w"][0].reshape(4, 24, 128).transpose(2, 1, 0).reshape(128, 96))
    put("gdn_norm", I["gdn_norm"][0][:, None])
    put("final_norm", feat(I["final_norm"]))
    put("pre_mix", feat(I["pre_mix_g_2"][0]))
    put("post_mix", feat(I["post_mix_g_2"][0]))
    put("pre_mlp", feat(I["pre_mlp_g_2"][0]))
    put("post_mlp", feat(I["post_mlp_g_2"][0]))
    put("w_dw", I["w_dw_2"][0].reshape(31, 8, 128).transpose(2, 1, 0).reshape(128, 248))
    put("b_dw", feat(I["b_dw_2"][0]))
    put("ln_g", feat(I["conv_ln_g_2"][0]))
    put("ln_b", feat(I["conv_ln_b_2"][0]))
    put("A_log", np.broadcast_to(I["A_log"][0][None, :], (128, 8)))
    put("dt_bias", np.broadcast_to(I["dt_bias"][0][None, :], (128, 8)))
    wada = np.ascontiguousarray(I["w_ada"][0].reshape(16, 128, 12, 1024).transpose(2, 0, 1, 3)).reshape(N_ADA, 128, 1024)
    r = np.arange(4)
    c = np.arange(64)
    dr = r[None, :] - r[:, None] + 7
    dc = np.clip(c[None, :] - c[:, None], -15, 15) + 15
    bias = I["rpb_2"][0][:, dr[:, None, :, None], dc[None, :, None, :]].reshape(32, 128, 256)

    arrays = {
        "xT": np.ascontiguousarray(I["x"][0].T.reshape(16, 128, 256).transpose(1, 0, 2)),
        "pos": I["positions"][0], "cols": cols, "consts": const_array(), "wada": wada, "bias": np.ascontiguousarray(bias),
    }
    nc = _bacc.Bacc("TRN2", target_bir_lowering=False, num_devices=1)
    aps = {n: nc.dram_tensor(n + "_dram", a.shape, mb.dt.from_np(a.dtype), kind="ExternalInput").ap() for n, a in arrays.items()}
    wst = nc.dram_tensor("wst_dram", (N_TILES // 8, 128, 1024), mb.dt.float32, kind="ExternalInput").ap()
    out = nc.dram_tensor("out_dram", (128, 16, 256), mb.dt.float32, kind="ExternalOutput").ap()
    log = []
    program(nc, aps["xT"], aps["pos"], aps["cols"], aps["consts"], aps["wada"], wst, aps["bias"], out, log)
    ws = np.empty((N_TILES // 8, 128, 1024), np.float32)
    for i, (name, k, n) in enumerate(log):
        ws[i // 8, :, 128 * (i % 8):128 * (i % 8) + 128] = W[name][128 * k:128 * k + 128, 128 * n:128 * n + 128]
    ins = {n + "_dram": a for n, a in arrays.items()}
    ins["wst_dram"] = ws
    res = _run(nc, [ins], core_ids=[0])
    o = res.results[0]["out_dram"]
    return np.ascontiguousarray(o.transpose(1, 0, 2).reshape(2048, 256).T).reshape(1, 256, 2048)
```
